# Optimizing a Trainium2 kernel written in Bass

```python
import jax, jax.numpy as jnp
from jax import lax
import numpy as np

D_MODEL = 1024
BATCH = 1
SEQ = 1024
DEPTH = 1

N_MEM = 256
EPS = 1e-6
POOL_WINDOWS = (2, 4, 8, 16)
N_POOL_GROUPS = len(POOL_WINDOWS)
POOL_WIDTH = D_MODEL // 2
POOL_GC = POOL_WIDTH // N_POOL_GROUPS
FOX_HEADS = 8
FOX_DH = 64
FOX_WIDTH = FOX_HEADS * FOX_DH
Q_BLOCK = 128
GATE_WIDTH = 2 * D_MODEL
IN_SPLITS = (POOL_WIDTH, POOL_WIDTH + FOX_WIDTH, POOL_WIDTH + 2 * FOX_WIDTH,
             POOL_WIDTH + 3 * FOX_WIDTH, POOL_WIDTH + 3 * FOX_WIDTH + FOX_HEADS)
IN_COLS = POOL_WIDTH + 3 * FOX_WIDTH + FOX_HEADS + GATE_WIDTH
X_HEADS = 4
X_DH = 128
X_WIDTH = X_HEADS * X_DH
D_FF = ((8 * D_MODEL // 3 + 255) // 256) * 256

kernel_name = "hybrid_pool_fox_gated_block"

def rmsnorm(x, g):
    xf = x.astype(jnp.float32)
    y = xf * lax.rsqrt(jnp.mean(xf * xf, axis=-1, keepdims=True) + EPS)
    return (y * g.astype(jnp.float32)).astype(x.dtype)

def pool_mixer(u, pool_w, pool_scale):
    B, S, _ = u.shape
    uf = u.astype(jnp.float32)
    cs = jnp.cumsum(uf, axis=1)
    t = jnp.arange(S)
    outs = []
    for g, w in enumerate(POOL_WINDOWS):
        sl = slice(g * POOL_GC, (g + 1) * POOL_GC)
        cs_g = cs[..., sl]
        shifted = jnp.pad(cs_g, ((0, 0), (w, 0), (0, 0)))[:, :S]
        cnt = jnp.minimum(t + 1, w).astype(jnp.float32)[None, :, None]
        outs.append((cs_g - shifted) / cnt - uf[..., sl])
    d = jnp.stack(outs, axis=2).astype(u.dtype)
    y = jnp.einsum('bsgc,gcd->bsgd', d, pool_w).reshape(B, S, POOL_WIDTH)
    return y * pool_scale

def forgetting_attention(q, k, v, f_logit):
    B, S, H, dh = q.shape
    q = q.transpose(0, 2, 1, 3)
    k = k.transpose(0, 2, 1, 3)
    v = v.transpose(0, 2, 1, 3)
    c = jnp.cumsum(jax.nn.log_sigmoid(f_logit.astype(jnp.float32)), axis=1).transpose(0, 2, 1)
    scale = dh ** -0.5
    outs = []
    for i in range(S // Q_BLOCK):
        q0, q1 = i * Q_BLOCK, (i + 1) * Q_BLOCK
        qb = q[:, :, q0:q1]
        kp, vp, cp = k[:, :, :q1], v[:, :, :q1], c[:, :, :q1]
        s = jnp.einsum('bhqd,bhkd->bhqk', qb, kp).astype(jnp.float32) * scale
        s = s + c[:, :, q0:q1, None] - cp[:, :, None, :]
        mask = (q0 + jnp.arange(Q_BLOCK))[:, None] >= jnp.arange(q1)[None, :]
        s = jnp.where(mask[None, None], s, -1e30)
        p = jax.nn.softmax(s, axis=-1).astype(v.dtype)
        outs.append(jnp.einsum('bhqk,bhkd->bhqd', p, vp))
    o = jnp.concatenate(outs, axis=2)
    return o.transpose(0, 2, 1, 3).reshape(B, S, H * dh)

def memory_cross_attention(h, mem_n, w_xq, w_xkv, w_xo):
    B, S, _ = h.shape
    M = mem_n.shape[1]
    q = (h @ w_xq).reshape(B, S, X_HEADS, X_DH)
    kv = (mem_n @ w_xkv).reshape(B, M, 2, X_HEADS, X_DH)
    k, v = kv[:, :, 0], kv[:, :, 1]
    s = jnp.einsum('bshd,bmhd->bhsm', q, k).astype(jnp.float32) * (X_DH ** -0.5)
    p = jax.nn.softmax(s, axis=-1).astype(v.dtype)
    o = jnp.einsum('bhsm,bmhd->bshd', p, v).reshape(B, S, X_WIDTH)
    return o @ w_xo

def setup_inputs(seed: int = 0) -> dict:
    key = jax.random.key(seed)
    ks = jax.random.split(key, 24)
    f32 = jnp.float32

    def nrm(k, shape, fan_in):
        return jax.random.normal(k, shape, f32) * (fan_in ** -0.5)

    def gain(k, shape):
        return 1.0 + 0.05 * jax.random.normal(k, shape, f32)

    L = DEPTH
    return {
        "x": jax.random.normal(ks[0], (BATCH, SEQ, D_MODEL), f32),
        "mem": jax.random.normal(ks[1], (BATCH, N_MEM, D_MODEL), f32),
        "norm_mix_g": gain(ks[2], (L, D_MODEL)),
        "w_in": nrm(ks[3], (L, D_MODEL, IN_COLS), D_MODEL),
        "b_forget": 3.0 + 0.5 * jax.random.normal(ks[4], (L, FOX_HEADS), f32),
        "b_gate": 0.02 * jax.random.normal(ks[5], (L, GATE_WIDTH), f32),
        "pool_w": nrm(ks[6], (L, N_POOL_GROUPS, POOL_GC, POOL_GC), POOL_GC),
        "pool_scale": gain(ks[7], (L, POOL_WIDTH)),
        "w_pool_out": nrm(ks[8], (L, POOL_WIDTH, D_MODEL), POOL_WIDTH),
        "w_fox_out": nrm(ks[9], (L, FOX_WIDTH, D_MODEL), FOX_WIDTH),
        "w_out": nrm(ks[10], (L, D_MODEL, D_MODEL), D_MODEL),
        "norm_x_g": gain(ks[11], (L, D_MODEL)),
        "norm_mem_g": gain(ks[12], (L, D_MODEL)),
        "w_xq": nrm(ks[13], (L, D_MODEL, X_WIDTH), D_MODEL),
        "w_xkv": nrm(ks[14], (L, D_MODEL, 2 * X_WIDTH), D_MODEL),
        "w_xo": nrm(ks[15], (L, X_WIDTH, D_MODEL), X_WIDTH),
        "norm_ffn_g": gain(ks[16], (L, D_MODEL)),
        "w_ffn_in": nrm(ks[17], (L, D_MODEL, 2 * D_FF), D_MODEL),
        "w_ffn_out": nrm(ks[18], (L, D_FF, D_MODEL), D_FF),
        "norm_final_g": gain(ks[19], (D_MODEL,)),
    }

def reference(x, mem, norm_mix_g, w_in, b_forget, b_gate, pool_w, pool_scale,
              w_pool_out, w_fox_out, w_out, norm_x_g, norm_mem_g, w_xq, w_xkv, w_xo,
              norm_ffn_g, w_ffn_in, w_ffn_out, norm_final_g):
    B, S, D = x.shape
    for l in range(DEPTH):
        h = rmsnorm(x, norm_mix_g[l])
        proj = h @ w_in[l]
        u_pool, q, k, v, f_logit, g_logit = jnp.split(proj, IN_SPLITS, axis=-1)
        y_pool = pool_mixer(u_pool, pool_w[l], pool_scale[l]) @ w_pool_out[l]
        y_fox = forgetting_attention(q.reshape(B, S, FOX_HEADS, FOX_DH),
                                     k.reshape(B, S, FOX_HEADS, FOX_DH),
                                     v.reshape(B, S, FOX_HEADS, FOX_DH),
                                     f_logit + b_forget[l]) @ w_fox_out[l]
        gates = jax.nn.sigmoid(g_logit + b_gate[l])
        g_pool, g_fox = gates[..., :D], gates[..., D:]
        x = x + (g_pool * y_pool + g_fox * y_fox) @ w_out[l]
        hx = rmsnorm(x, norm_x_g[l])
        mem_n = rmsnorm(mem, norm_mem_g[l])
        x = x + memory_cross_attention(hx, mem_n, w_xq[l], w_xkv[l], w_xo[l])
        hf = rmsnorm(x, norm_ffn_g[l])
        gu = hf @ w_ffn_in[l]
        gt, up = gu[..., :D_FF], gu[..., D_FF:]
        x = x + (jax.nn.silu(gt) * up) @ w_ffn_out[l]
    return rmsnorm(x, norm_final_g)


_drawn_inputs = setup_inputs


def setup_inputs(seed=0):
    import zlib

    import numpy as np

    out = dict(_drawn_inputs(seed))
    spreads = {}
    factors = {'b_gate': 8.0, 'norm_x_g': 8.0, 'norm_mem_g': 7.502, 'norm_ffn_g': 8.0}
    for name, (base, spread) in spreads.items():
        noise = np.random.default_rng([zlib.crc32(name.encode()), seed]).standard_normal(out[name].shape)
        drawn = base * np.exp(spread * noise) if base else spread * noise
        out[name] = __import__('jax').numpy.asarray(drawn.astype(out[name].dtype))
    for name, factor in factors.items():
        out[name] = (out[name] * factor).astype(out[name].dtype)
    return out
```

```python
from contextlib import ExitStack

import concourse.bass as bass
from concourse import mybir

FP32 = mybir.dt.float32
F32R = mybir.dt.float32r
ALU = mybir.AluOpType
ACT = mybir.ActivationFunctionType
AX = mybir.AxisListType.X

P = 128
S = 1024
D = 1024
T = S // P
KD = D // P
HALF = 512
EPS = 1e-6
WINDOWS = (2, 4, 8, 16)
NG = len(WINDOWS)
PAD = 16
POOL_W = D // 2
HEADS, DH = 8, 64
PAIRS = HEADS // 2
FOX_W = HEADS * DH
MEM = 256
XH, XDH = 4, 128
XW = XH * XDH
DFF = ((8 * D // 3 + 255) // 256) * 256
NB = DFF // (2 * P)
MASKED = -1e30
LOWEST = -3e38
RAWS, SLOTS = 2, 3

COL_Q = POOL_W
COL_K = COL_Q + FOX_W
COL_V = COL_K + FOX_W
COL_F = COL_V + FOX_W
COL_G = COL_F + HEADS

C_U = 0
C_V = C_U + NG
C_F = C_V + 4
C_PW = C_F + 1
C_PG = C_PW + 1
C_QK = C_PG + 12
C_FG = C_QK + 8
C_WO = C_FG + 12
C_XK = C_WO + 8
C_XV = C_XK + 4
C_XQ = C_XV + 4
C_XO = C_XQ + 4
C_FF = C_XO + 4
N_CHUNKS = C_FF + 6 * NB

N_X, N_MEM, N_CROSS, N_FFN, N_OUT = 0, T, T + 2, 2 * T + 2, 3 * T + 2


def build(nc, x, mem, norm_mix_g, w_in, b_forget, b_gate, pool_w, pool_scale, w_pool_out,
          w_fox_out, w_out, norm_x_g, norm_mem_g, w_xq, w_xkv, w_xo, norm_ffn_g, w_ffn_in,
          w_ffn_out, norm_final_g, out):
    x2, mem2, out2 = x[0], mem[0], out[0]
    w_in, w_out, w_xq, w_xkv, w_xo = w_in[0], w_out[0], w_xq[0], w_xkv[0], w_xo[0]
    w_pool_out, w_fox_out, pool_w = w_pool_out[0], w_fox_out[0], pool_w[0]
    w_ffn_in, w_ffn_out = w_ffn_in[0], w_ffn_out[0]
    za_dram = nc.dram_tensor("za_dram", [KD, P, S], FP32).ap()
    negc_dram = nc.dram_tensor("negc_dram", [HEADS, S], FP32).ap()

    ctx = ExitStack()
    with ctx:
        def keep(name, shape, dt=FP32):
            return ctx.enter_context(nc.sbuf_tensor(name, shape, dt))

        def place(name, kb, shape, dt=FP32):
            with ExitStack() as st:
                if kb:
                    st.enter_context(nc.sbuf_tensor(f"under_{name}", [P, kb * 256], FP32))
                return st.enter_context(nc.sbuf_tensor(name, shape, dt))

        w_raw = [keep(f"w_raw{i}", [P, 1024]) for i in range(RAWS)]
        w_hi = [keep(f"w_hi{i}", [P, 1024], F32R) for i in range(SLOTS)]
        w_lo = [keep(f"w_lo{i}", [P, 1024], F32R) for i in range(SLOTS)]
        ident = keep("ident", [P, P])
        ident_r = keep("ident_r", [P, P], F32R)
        mask = keep("mask", [P, P])
        mask_r = keep("mask_r", [P, P], F32R)
        n_tiles = N_OUT + T
        ss = keep("ss", [P, n_tiles])
        ms = keep("ms", [P, n_tiles])
        rstd = keep("rstd", [P, n_tiles])
        minus_half = keep("minus_half", [P, 1])
        bg = keep("bg", [P, 2 * KD])
        ps_scale = keep("ps_scale", [P, NG])
        count_i = keep("count_i", [P, PAD], mybir.dt.int32)
        count = keep("count", [P, PAD])
        inv_count = keep("inv_count", [P, PAD])
        bf = keep("bf", [HEADS, 1])
        score_max = keep("score_max", [P, 2, 2])
        neg_max = keep("neg_max", [P, 2, 2])
        prob_sum = keep("prob_sum", [P, 2, 2])
        prob_inv = keep("prob_inv", [P, 2, 2])
        x_max = keep("x_max", [P, XH, T])
        x_nmax = keep("x_nmax", [P, XH, T])
        x_sum = keep("x_sum", [P, XH, T])
        x_inv = keep("x_inv", [P, XH, T])

        h_hi = place("h_hi", 0, [P, KD, S], F32R)
        h_lo = place("h_lo", 32, [P, KD, S], F32R)
        x_in = [place(f"x_in{i}", 64 + 4 * i, [P, D]) for i in range(4)]
        xn_a = [place(f"xn_a{i}", 80 + 4 * i, [P, D]) for i in range(2)]
        v_sb = place("v_sb", 64, [P, T, FOX_W])
        u_sb = place("u_sb", 88, [P, NG, PAD + S])
        win = [place(f"win{i}", 105 + 5 * i, [P, PAD + S]) for i in range(2)]
        pooled = place("pooled", 115, [P, S])
        d_hi = place("d_hi", 119, [P, NG, S], F32R)
        d_lo = place("d_lo", 135, [P, NG, S], F32R)
        sg = [place(f"sg{i}", 151 + 4 * i, [P, S]) for i in range(2)]
        za = [place(f"za{i}", 159 + 4 * i, [P, S]) for i in range(2)]
        f_tok = place("f_tok", 88, [P, P])
        f_tr = place("f_tr", 89, [HEADS * T, P])
        f_h = place("f_h", 90, [HEADS, S])
        f_neg = place("f_neg", 94, [HEADS, S])
        f_min = place("f_min", 98, [HEADS, S])
        f_exp = place("f_exp", 102, [HEADS, S])
        f_u = place("f_u", 106, [HEADS, S])
        f_log = place("f_log", 110, [HEADS, S])
        f_one = place("f_one", 114, [HEADS, S])
        q_sb = [place(f"q_sb{i}", 80 + 4 * i, [P, S]) for i in range(2)]
        k_sb = [place(f"k_sb{i}", 88 + 4 * i, [P, S]) for i in range(2)]
        negc = [place(f"negc{i}", 96 + 8 * i, [P, 2, S]) for i in range(2)]
        prob = [place(f"prob{i}", 112 + 8 * i, [P, 2, S]) for i in range(2)]
        prob_t = [place(f"prob_t{i}", 128 + 8 * i, [P, 2, S]) for i in range(2)]
        o_sb = place("o_sb", 144, [P, PAIRS, S])
        o_hi = place("o_hi", 64, [P, PAIRS, S], F32R)
        o_lo = place("o_lo", 80, [P, PAIRS, S], F32R)
        z_hi = place("z_hi", 96, [P, KD, S], F32R)
        z_lo = place("z_lo", 128, [P, KD, S], F32R)
        sg_e = [place(f"sg_e{i}", 160 + 4 * i, [P, S]) for i in range(2)]
        za_e = place("za_e", 168, [P, S])
        xr = place("xr", 64, [P, T, D])
        gain = place("gain", 168, [P, D])
        mem_in = place("mem_in", 24, [P, 2, D])
        xn_m = place("xn_m", 160, [P, 2, D])
        mt_hi = place("mt_hi", 32, [P, KD, MEM], F32R)
        mt_lo = place("mt_lo", 40, [P, KD, MEM], F32R)
        xk_hi = place("xk_hi", 0, [P, XH, MEM], F32R)
        xk_lo = place("xk_lo", 4, [P, XH, MEM], F32R)
        xv_hi = place("xv_hi", 8, [P, 2, XW], F32R)
        xv_lo = place("xv_lo", 12, [P, 2, XW], F32R)
        hx_hi = place("hx_hi", 96, [P, KD, S], F32R)
        hx_lo = place("hx_lo", 128, [P, KD, S], F32R)
        xn_x = [place(f"xn_x{i}", 160 + 4 * i, [P, D]) for i in range(2)]
        xq_hi = place("xq_hi", 16, [P, S], F32R)
        xq_lo = place("xq_lo", 20, [P, S], F32R)
        xp = place("xp", 24, [P, T, MEM])
        xo_hi = place("xo_hi", 32, [P, XH, S], F32R)
        xo_lo = place("xo_lo", 48, [P, XH, S], F32R)
        xpt_hi = place("xpt_hi", 160, [P, 2, HALF], F32R)
        xpt_lo = place("xpt_lo", 164, [P, 2, HALF], F32R)
        junk_x = place("junk_x", 28, [P, D])
        junk_f = place("junk_f", 156, [P, D])
        hf_hi = place("hf_hi", 0, [P, KD, S], F32R)
        hf_lo = place("hf_lo", 32, [P, KD, S], F32R)
        xn_f = [place(f"xn_f{i}", 160 + 4 * i, [P, D]) for i in range(2)]
        hid_hi = [place(f"hid_hi{i}", 96 + 16 * i, [P, 2, S], F32R) for i in range(2)]
        hid_lo = [place(f"hid_lo{i}", 104 + 16 * i, [P, 2, S], F32R) for i in range(2)]
        silu = [place(f"silu{i}", 128 + 4 * i, [P, S]) for i in range(2)]
        hid = [place(f"hid{i}", 136 + 4 * i, [P, S]) for i in range(2)]
        y_out = [place(f"y_out{i}", 144 + 4 * i, [P, D]) for i in range(3)]

        ps = ctx.enter_context(nc.psum_tensor("ps", [P, 8, HALF], FP32))

        def two(b):
            return ps[:, b:b + 2, :].rearrange("p b n -> p (b n)")

        def sem(name):
            return ctx.enter_context(nc.semaphore(name))

        raw_loaded = [sem(f"raw_loaded{i}") for i in range(RAWS)]
        hi_ready, lo_ready, w_used = sem("hi_ready"), sem("lo_ready"), sem("w_used")
        consts_set, consts_r, small_in, gain_in = sem("consts_set"), sem("consts_r"), sem("small_in"), sem("gain_in")
        x_loaded = [sem(f"x_loaded{i}") for i in range(4)]
        ss_ready, ms_ready, rstd_ready = sem("ss_ready"), sem("ms_ready"), sem("rstd_ready")
        xn_ready, xt_done, xt_hi, xt_lo = sem("xn_ready"), sem("xt_done"), sem("xt_hi"), sem("xt_lo")
        u_done, u_copied, v_done, v_copied = sem("u_done"), sem("u_copied"), sem("v_done"), sem("v_copied")
        pads_zero, win_step, d_ready, d_hi_ready, d_lo_ready = (sem("pads_zero"), sem("win_step"), sem("d_ready"),
                                                                sem("d_hi_ready"), sem("d_lo_ready"))
        mix_done, mix_hi, mix_lo = sem("mix_done"), sem("mix_hi"), sem("mix_lo")
        f_done, f_copied, f_tr_done, f_tr_copied, f_moved = (sem("f_done"), sem("f_copied"), sem("f_tr_done"),
                                                             sem("f_tr_copied"), sem("f_moved"))
        f_step, f_exp_ready, f_log_ready, negc_ready, negc_stored = (sem("f_step"), sem("f_exp_ready"), sem("f_log_ready"),
                                                                     sem("negc_ready"), sem("negc_stored"))
        gate_done, gate_ready, y_done, za_ready = sem("gate_done"), sem("gate_ready"), sem("y_done"), sem("za_ready")
        za_stored = [sem(f"za_stored{i}") for i in range(2)]
        za_loaded, y_gated, z_sum, z_hi_ready, z_lo_ready = (sem("za_loaded"), sem("y_gated"), sem("z_sum"),
                                                             sem("z_hi_ready"), sem("z_lo_ready"))
        qk_done, qk_copied, negc_loaded = sem("qk_done"), sem("qk_copied"), [sem(f"negc_loaded{i}") for i in range(2)]
        sc_done, sc_biased, nmax_ready, exp_ready, inv_ready, prob_ready = (
            sem("sc_done"), sem("sc_biased"), sem("nmax_ready"), sem("exp_ready"), sem("inv_ready"), sem("prob_ready"))
        pt_done, pt_copied, pv_done, pv_copied, o_hi_ready, o_lo_ready = (
            sem("pt_done"), sem("pt_copied"), sem("pv_done"), sem("pv_copied"), sem("o_hi_ready"), sem("o_lo_ready"))
        mem_loaded, mix_gain_in = sem("mem_loaded"), sem("mix_gain_in")
        xr_loaded, bank_out, xr_added, out_ready, out_stored = (sem("xr_loaded"), sem("bank_out"), sem("xr_added"),
                                                                sem("out_ready"), [sem(f"out_stored{i}") for i in range(3)])
        kv_done, kv_hi, kv_lo = sem("kv_done"), sem("kv_hi"), sem("kv_lo")
        xq_done, xq_hi_ready, xq_lo_ready = sem("xq_done"), sem("xq_hi_ready"), sem("xq_lo_ready")
        xs_done, xs_max, xs_nmax, xs_exp, xs_inv, xp_ready = (sem("xs_done"), sem("xs_max"), sem("xs_nmax"),
                                                              sem("xs_exp"), sem("xs_inv"), sem("xp_ready"))
        xpt_done, xpt_hi_ready, xpt_lo_ready, xpv_done, xo_hi_ready, xo_lo_ready = (
            sem("xpt_done"), sem("xpt_hi_ready"), sem("xpt_lo_ready"), sem("xpv_done"), sem("xo_hi_ready"), sem("xo_lo_ready"))
        fg_done, fu_done, silu_ready, hid_ready, hid_hi_ready, hid_lo_ready = (
            sem("fg_done"), sem("fu_done"), sem("silu_ready"), sem("hid_ready"), sem("hid_hi_ready"), sem("hid_lo_ready"))

        def cols(w, c0, n=P):
            return w[:, c0:c0 + n].rearrange("(k p) n -> p k n", p=P)

        def rows(w, k0, c0, n=HALF):
            return w[k0 * P:(k0 + 2) * P, c0:c0 + n].rearrange("(k p) n -> p k n", p=P)

        def ffn_in_cols(c0):
            return w_ffn_in[:, bass.ds(c0, P)].rearrange("(k p) n -> p k n", p=P)

        def ffn_out_rows(r0, c0):
            return w_ffn_out[bass.ds(r0, 2 * P), c0:c0 + HALF].rearrange("(k p) n -> p k n", p=P)

        def chunk_view(k):
            if k < C_V:
                return cols(w_in, (k - C_U) * P)
            if k < C_F:
                return rows(w_in, 2 * (k - C_V), COL_V)
            if k == C_F:
                return cols(w_in, COL_F, HEADS)
            if k == C_PW:
                return pool_w.rearrange("g c d -> c g d")
            if k < C_QK:
                j, r = divmod(k - C_PG, 3)
                return cols(w_pool_out, 2 * j * P, 2 * P) if r == 2 else cols(w_in, COL_G + (2 * j + r) * P)
            if k < C_FG:
                p, r = divmod(k - C_QK, 2)
                return cols(w_in, (COL_K if r else COL_Q) + p * P)
            if k < C_WO:
                j, r = divmod(k - C_FG, 3)
                return cols(w_fox_out, 2 * j * P, 2 * P) if r == 2 else cols(w_in, COL_G + D + (2 * j + r) * P)
            if k < C_XK:
                n, r = divmod(k - C_WO, 4)
                return rows(w_out, 2 * r, n * HALF)
            if k < C_XV:
                return cols(w_xkv, (k - C_XK) * P)
            if k < C_XQ:
                return rows(w_xkv, 2 * (k - C_XV), XW)
            if k < C_XO:
                return cols(w_xq, (k - C_XQ) * P)
            if k < C_FF:
                n, r = divmod(k - C_XO, 2)
                return rows(w_xo, 2 * r, n * HALF)
            return ffn_view(0, k - C_FF)

        def ffn_view(b, r):
            if r < 4:
                t, up = divmod(r, 2)
                return ffn_in_cols(b * 2 * P + (t * P + up * DFF))
            return ffn_out_rows((b - 1) * 2 * P, (r - 4) * HALF)

        def width(k):
            return {C_F: KD * HEADS, C_PW: NG * P}.get(k, 1024)

        block = ctx.enter_context(nc.Block())

        def half_of(h):
            return slice(h * HALF, (h + 1) * HALF)

        def tile_of(t):
            return slice(t * P, (t + 1) * P)

        def base_of(b):
            return b * 6 + (C_FF - 2)

        @block.sync
        def _(sp):
            def load_raw(n, view, uses=None):
                if n >= RAWS:
                    sp.wait_ge(lo_ready, n - RAWS + 1)
                t = w_raw[n % RAWS][:, 0:width(n)]
                if n in (C_F, C_PW):
                    t = t.rearrange("p (k n) -> p k n", n=HEADS if n == C_F else P)
                sp.dma_start(t, view).then_inc(raw_loaded[n % RAWS], 16)

            for t in range(T):
                if t == 4:
                    load_raw(0, chunk_view(0))
                    load_raw(1, chunk_view(1))
                if t >= 4:
                    sp.wait_ge(xn_ready, t - 3)
                sp.dma_start(x_in[t % 4][:], x2[tile_of(t), :]).then_inc(x_loaded[t % 4], 16)
            for k in range(2, C_FF + 4):
                load_raw(k, chunk_view(k) if k < C_FF else ffn_view(0, k - C_FF))
            with sp.Fori(0, (NB - 1) // 2) as i:
                for o in range(2):
                    for r in range(6):
                        n = base_of(1 + o) + r
                        sp.wait_ge(lo_ready, i * 12 + (n - RAWS + 1))
                        if r < 4:
                            j, up = divmod(r, 2)
                            view = ffn_in_cols(i * (4 * P) + ((1 + o) * 2 * P + j * P + up * DFF))
                        else:
                            view = ffn_out_rows(i * (4 * P) + o * 2 * P, (r - 4) * HALF)
                        sp.dma_start(w_raw[n % RAWS][:, :], view).then_inc(raw_loaded[n % RAWS], 16)
            for r in range(2):
                load_raw(N_CHUNKS - 2 + r, ffn_view(NB, 4 + r))
            for t in range(T):
                sp.wait_ge(out_ready, t + 1)
                sp.dma_start(out2[tile_of(t), :], y_out[t % 3][:]).then_inc(out_stored[t % 3], 16)
            for i in range(3):
                sp.wait_ge(out_stored[i], 16 * len(range(i, T, 3)))

        @block.gpsimd
        def _(pool):
            nc.gpsimd.memset(ident[:], 0.0).then_inc(consts_set, 1)
            nc.gpsimd.memset(mask[:], 0.0).then_inc(consts_set, 1)
            nc.gpsimd.memset(minus_half[:], -0.5).then_inc(consts_set, 1)
            pool.wait_ge(consts_set, 3)
            nc.gpsimd.affine_select(out=ident[:], in_=ident[:], compare_op=ALU.not_equal, fill=1.0, base=0,
                                    pattern=[[-1, P]], channel_multiplier=1).then_inc(consts_set, 1)
            nc.gpsimd.affine_select(out=mask[:], in_=mask[:], compare_op=ALU.is_ge, fill=MASKED, base=0,
                                    pattern=[[-1, P]], channel_multiplier=1).then_inc(consts_set, 1)
            nc.gpsimd.iota(count_i[:], pattern=[[1, PAD]], base=1, channel_multiplier=0).then_inc(consts_set, 1)

            def rstd_of(n):
                pool.wait_ge(ss_ready, n + 1)
                nc.gpsimd.tensor_scalar(ms[:, n:n + 1], ss[:, n:n + 1], 1.0 / D, EPS,
                                        ALU.mult, ALU.add).then_inc(ms_ready, 1)
                pool.wait_ge(ms_ready, n + 1)
                nc.gpsimd.tensor_tensor(rstd[:, n:n + 1], ms[:, n:n + 1], minus_half[:],
                                        ALU.pow).then_inc(rstd_ready, 1)

            for n in range(N_X, N_MEM):
                rstd_of(n)
            pool.wait_ge(f_tr_copied, 1)
            for t in range(T):
                pool.dma_start(f_h[:, tile_of(t)], f_tr[t * HEADS:(t + 1) * HEADS, :]).then_inc(f_moved, 16)
            pool.wait_ge(negc_ready, 1)
            pool.dma_start(negc_dram, f_u[:]).then_inc(negc_stored, 16)
            pool.wait_ge(negc_stored, 16)
            for p in range(PAIRS):
                if p == 0:
                    pool.wait_ge(y_gated, KD)
                if p >= 2:
                    pool.wait_ge(sc_biased, 2 * T * (p - 1))
                for a in range(2):
                    pool.dma_start(negc[p % 2][:, a, :], negc_dram[2 * p + a:2 * p + a + 1, :].broadcast_to([P, S]))\
                        .then_inc(negc_loaded[p % 2], 16)
            for i in range(2):
                pool.wait_ge(za_stored[i], 16 * (KD // 2))
            for m in range(KD):
                if m:
                    pool.wait_ge(z_sum, m)
                pool.dma_start(za_e[:], za_dram[m]).then_inc(za_loaded, 16)
            pool.wait_ge(w_used, C_WO)
            for t in range(2):
                pool.dma_start(mem_in[:, t, :], mem2[tile_of(t), :]).then_inc(mem_loaded, 16)
            for t in range(T):
                pool.dma_start(xr[:, t, :], x2[tile_of(t), :]).then_inc(xr_loaded, 16)

            def load_gain(g):
                pool.dma_start(gain[:], g.broadcast_to([P, D])).then_inc(gain_in, 16)

            pool.wait_ge(z_sum, KD)
            load_gain(norm_mem_g)
            for n in range(N_MEM, N_CROSS):
                rstd_of(n)
            pool.wait_ge(xn_ready, N_CROSS)
            load_gain(norm_x_g)
            for n in range(N_CROSS, N_FFN):
                rstd_of(n)
            pool.wait_ge(xn_ready, N_FFN)
            load_gain(norm_ffn_g)
            for n in range(N_FFN, N_OUT):
                rstd_of(n)
            pool.wait_ge(xn_ready, N_OUT)
            load_gain(norm_final_g.unsqueeze(0))

            def hid_lo_of(f, par, j):
                pool.wait_ge(hid_hi_ready, f + 1)
                nc.gpsimd.tensor_tensor(hid_lo[par][:, j, :], hid[j][:], hid_hi[par][:, j, :].bitcast(FP32),
                                        ALU.subtract).then_inc(hid_lo_ready, 1)

            for j in range(2):
                hid_lo_of(j, 0, j)
            with pool.Fori(0, (NB - 1) // 2) as i:
                for o in range(2):
                    for j in range(2):
                        hid_lo_of(i * 4 + (2 + 2 * o + j), (1 + o) % 2, j)
            for n in range(N_OUT, N_OUT + T):
                rstd_of(n)

        @block.scalar
        def _(act):
            def split_hi(n, turns=0):
                act.wait_ge(raw_loaded[n % RAWS], turns * (16 * 12 // RAWS) + 16 * (n // RAWS + 1))
                if n >= SLOTS:
                    act.wait_ge(w_used, turns * 12 + (n - SLOTS + 1))
                w = width(n)
                nc.scalar.activation(w_hi[n % SLOTS][:, 0:w], w_raw[n % RAWS][:, 0:w], ACT.Copy).then_inc(hi_ready, 1)

            def square(n, src, junk):
                if n:
                    act.wait_ge(ss_ready, n)
                nc.scalar.activation(junk, src, ACT.Square, accum_out=ss[:, n:n + 1]).then_inc(ss_ready, 1)

            def xt_hi_of(n, bank, dst):
                act.wait_ge(xt_done, n + 1)
                nc.scalar.activation(dst, two(bank).rearrange("p (k n) -> p k n", n=P), ACT.Copy).then_inc(xt_hi, 1)

            act.dma_start(gain[:], norm_mix_g.broadcast_to([P, D])).then_inc(mix_gain_in, 16)
            with nc.allow_non_contiguous_dma(reason="small per-feature vectors"):
                act.dma_start(bg[:], b_gate[0].rearrange("(m p) -> p m", p=P)).then_inc(small_in, 16)
                act.dma_start(ps_scale[:], pool_scale[0].rearrange("(m p) -> p m", p=P)).then_inc(small_in, 16)
                act.dma_start(bf[:], b_forget.rearrange("a h -> h a")).then_inc(small_in, 16)
            act.wait_ge(consts_set, 5)
            nc.scalar.activation(ident_r[:], ident[:], ACT.Copy).then_inc(consts_r, 1)
            nc.scalar.activation(mask_r[:], mask[:], ACT.Copy).then_inc(consts_r, 1)

            for t in range(T + 2):
                if t < T:
                    act.wait_ge(x_loaded[t % 4], 16 * (t // 4 + 1))
                    square(t, x_in[t % 4][:], pooled[:])
                if t == 3:
                    split_hi(0)
                    split_hi(1)
                if t >= 2:
                    xt_hi_of(t - 2, 2 * ((t - 2) % 4), h_hi[:, :, tile_of(t - 2)])

            for k in range(C_U, C_V + 4):
                split_hi(k + 2)
                if C_U < k <= C_V:
                    g = k - 1 - C_U
                    act.wait_ge(w_used, k)
                    nc.scalar.activation(u_sb[:, g, PAD:], two(2 * g), ACT.Copy).then_inc(u_copied, 1)
                if k > C_V:
                    g = k - C_V - 1
                    act.wait_ge(d_ready, g + 1)
                    nc.scalar.activation(d_hi[:, g, :], pooled[:], ACT.Copy).then_inc(d_hi_ready, 1)
            split_hi(C_F + 2)
            act.wait_ge(w_used, C_F)
            for t in range(T):
                nc.scalar.activation(v_sb[:, t, :], ps[:, t, :], ACT.Copy).then_inc(v_copied, 1)
            act.wait_ge(d_ready, NG)
            nc.scalar.activation(d_hi[:, NG - 1, :], pooled[:], ACT.Copy).then_inc(d_hi_ready, 1)
            split_hi(C_PW + 2)
            for g in range(NG):
                act.wait_ge(mix_done if g < NG - 1 else w_used, g + 1 if g < NG - 1 else C_PW + 1)
                if g == 0:
                    act.wait_ge(small_in, 48)
                nc.scalar.activation(d_hi[:, g, :], two(2 + 2 * (g % 3)), ACT.Copy,
                                     scale=ps_scale[:, g:g + 1]).then_inc(mix_hi, 1)

            def sigmoid_gate(m, bias, dst):
                nc.scalar.activation(dst, two(2 * (m % 2)), ACT.Sigmoid, bias=bias).then_inc(gate_ready, 1)

            def store_za(m):
                act.wait_ge(y_gated, m + 1)
                act.dma_start(za_dram[m], za[m % 2][:]).then_inc(za_stored[m % 2], 16)

            for k in range(C_PG, C_QK + 1):
                split_hi(k + 2)
                j, r = divmod(k - 1 - C_PG, 3)
                if k == C_PG:
                    continue
                if r < 2:
                    m = 2 * j + r
                    act.wait_ge(w_used, k)
                    if m >= 2:
                        act.wait_ge(y_gated, m - 1)
                    sigmoid_gate(m, bg[:, m:m + 1], sg[m % 2][:])
                else:
                    store_za(2 * j)
                    store_za(2 * j + 1)
                if k == C_PG + 2:
                    act.wait_ge(f_step, 3)
                    nc.scalar.activation(f_exp[:], f_min[:], ACT.Exp).then_inc(f_exp_ready, 1)
                    act.wait_ge(f_step, 4)
                    nc.scalar.activation(f_log[:], f_u[:], ACT.Ln).then_inc(f_log_ready, 1)

            def qk_copy(g):
                p, r = divmod(g, 4)
                which, h = divmod(r, 2)
                bank = 4 + r if p == 0 else 7
                if h == 0:
                    act.wait_ge(qk_done, 2 * p + which + 1)
                else:
                    act.wait_ge(w_used, C_QK + 2 * p + which + 1)
                dst = (k_sb if which else q_sb)[p % 2]
                nc.scalar.activation(dst[:, half_of(h)], ps[:, bank, :], ACT.Copy,
                                     scale=1.0 if which else DH ** -0.5).then_inc(qk_copied, 1)

            split_hi(C_QK + 3)
            qk_copy(0)
            qk_copy(1)
            qk_copy(2)
            qk_copy(3)

            groups = 0
            for u in range(PAIRS * T + 1):
                p, i = divmod(u, T)
                if u % 4 == 0 and u < 4 * 6:
                    split_hi(C_QK + 2 + u // 4 + 2)
                if u < PAIRS * T:
                    n = (i + 1) * P
                    for a in range(2):
                        act.wait_ge(nmax_ready, u + 1)
                        nc.scalar.activation(prob[u % 2][:, a, 0:n], prob[u % 2][:, a, 0:n], ACT.Exp,
                                             bias=neg_max[:, u % 2, a:a + 1],
                                             accum_out=prob_sum[:, u % 2, a:a + 1]).then_inc(exp_ready, 1)
                if u >= 1:
                    pi = (u - 1) % T
                    for a in range(2):
                        for j0 in range(0, pi + 1, 4):
                            n = min(4, pi + 1 - j0) * P
                            act.wait_ge(pt_done, groups + 1)
                            nc.scalar.activation(prob_t[(u - 1) % 2][:, a, j0 * P:j0 * P + n],
                                                 ps[:, 4 + groups % 2, 0:n], ACT.Copy).then_inc(pt_copied, 1)
                            groups += 1
                    act.wait_ge(pv_done, u)
                    if u == 1:
                        for s in range(2):
                            act.wait_ge(za_stored[s], 16 * (KD // 2))
                    nc.scalar.activation(o_sb[:, (u - 1) // T, tile_of(pi)], ps[:, 6, 0:P], ACT.Copy).then_inc(pv_copied, 1)
                if u < 3 * T and u % 2 == 1:
                    qk_copy(4 + u // 2)

            for k in range(C_FG, C_WO + 1):
                split_hi(k + 2)
                j, r = divmod(k - 1 - C_FG, 3)
                if k == C_FG:
                    act.wait_ge(pv_copied, PAIRS * T)
                    for p in range(PAIRS):
                        nc.scalar.activation(o_hi[:, p, :], o_sb[:, p, :], ACT.Copy).then_inc(o_hi_ready, 1)
                    continue
                if r < 2:
                    m = 2 * j + r
                    act.wait_ge(w_used, k)
                    if m >= 2:
                        act.wait_ge(z_lo_ready, m - 1)
                    sigmoid_gate(m, bg[:, KD + m:KD + m + 1], sg_e[m % 2][:])
                else:
                    for m in (2 * j, 2 * j + 1):
                        act.wait_ge(z_sum, m + 1)
                        nc.scalar.activation(z_hi[:, m, :], sg_e[m % 2][:], ACT.Copy).then_inc(z_hi_ready, 1)

            for k in range(C_WO + 1, C_XK):
                split_hi(k + 2)
                if k == C_WO + 1:
                    act.wait_ge(mem_loaded, 32)
                    act.wait_ge(z_lo_ready, KD)
                    for t in range(2):
                        square(N_MEM + t, mem_in[:, t, :], xn_m[:, t, :])
                if k == C_WO + 4:
                    for t in range(2):
                        xt_hi_of(N_MEM + t, 2 * t, mt_hi[:, :, tile_of(t)])

            def square_residual(t, n0, added, junk):
                act.wait_ge(xr_added, added + t + 1)
                square(n0 + t, xr[:, t, :], junk)

            for s in range(10):
                if s < 8:
                    split_hi(C_XK + s + 2)
                for t in {0: (0, 1, 2)}.get(s, (s + 2,)):
                    if t < T:
                        square_residual(t, N_CROSS, T, junk_x[:])
                if 1 <= s < 5:
                    act.wait_ge(w_used, C_XK + s)
                    nc.scalar.activation(xk_hi[:, s - 1, :], ps[:, s - 1, 0:MEM], ACT.Copy).then_inc(kv_hi, 1)
                if s == 8:
                    act.wait_ge(w_used, C_XQ)
                    for t in range(2):
                        nc.scalar.activation(xv_hi[:, t, :], ps[:, 4 + t, :], ACT.Copy).then_inc(kv_hi, 1)
                if s >= 2:
                    xt_hi_of(N_CROSS + s - 2, 6, hx_hi[:, :, tile_of(s - 2)])

            def xpt_hi_of(h, half):
                act.wait_ge(xpt_done, 2 * h + half + 1)
                nc.scalar.activation(xpt_hi[:], ps[:, 6:8, :], ACT.Copy).then_inc(xpt_hi_ready, 1)

            def xo_hi_of(h, half):
                act.wait_ge(xpv_done, 2 * h + half + 1)
                nc.scalar.activation(xo_hi[:, h, half_of(half)], ps[:, half, :], ACT.Copy).then_inc(xo_hi_ready, 1)

            for h in range(XH):
                split_hi(C_XQ + h + 2)
                act.wait_ge(w_used, C_XQ + h + 1)
                nc.scalar.activation(xq_hi[:], two(0), ACT.Copy).then_inc(xq_hi_ready, 1)
                for half in range(2):
                    if h:
                        xpt_hi_of(h - 1, half)
                    act.wait_ge(xs_nmax, 2 * h + half + 1)
                    for t in range(4 * half, 4 * half + 4):
                        nc.scalar.activation(xp[:, t, :], ps[:, 2 + t // 2, (t % 2) * MEM:(t % 2 + 1) * MEM], ACT.Exp,
                                             bias=x_nmax[:, h, t:t + 1], scale=XDH ** -0.5,
                                             accum_out=x_sum[:, h, t:t + 1]).then_inc(xs_exp, 1)
                    if h:
                        xo_hi_of(h - 1, half)
            for half in range(2):
                xpt_hi_of(XH - 1, half)
                xo_hi_of(XH - 1, half)
            split_hi(C_XO + 2)
            split_hi(C_XO + 3)
            split_hi(C_FF)
            split_hi(C_FF + 1)
            for t in range(T + 2):
                if t < T:
                    square_residual(t, N_FFN, 3 * T, junk_f[:])
                if t >= 2:
                    xt_hi_of(N_FFN + t - 2, 2 * ((t - 2) % 4), hf_hi[:, :, tile_of(t - 2)])

            def silu_of(b, j, used):
                act.wait_ge(w_used, used)
                if not (isinstance(b, int) and b == 0):
                    act.wait_ge(hid_ready, b * 2 + (j - 1))
                nc.scalar.activation(silu[j][:], two(4 * j), ACT.Silu).then_inc(silu_ready, 1)

            def hid_hi_of(b, par, j, used):
                act.wait_ge(hid_ready, b * 2 + (j + 1))
                if used is not None:
                    act.wait_ge(w_used, used)
                nc.scalar.activation(hid_hi[par][:, j, :], hid[j][:], ACT.Copy).then_inc(hid_hi_ready, 1)

            split_hi(C_FF + 2)
            split_hi(C_FF + 3)
            silu_of(0, 0, C_FF + 1)
            split_hi(C_FF + 4)
            hid_hi_of(0, 0, 0, None)
            split_hi(C_FF + 5)
            silu_of(0, 1, C_FF + 3)
            with act.Fori(0, (NB - 1) // 2) as i:
                for o in range(2):
                    n0 = base_of(1 + o)
                    b = i * 2 + (1 + o)
                    for r in range(6):
                        split_hi(n0 + r + 2, i)
                        if r == 0:
                            hid_hi_of(b - 1, o, 1, i * 12 + base_of(o))
                        if r == 1:
                            silu_of(b, 0, i * 12 + (n0 + 1))
                        if r == 2:
                            hid_hi_of(b, (1 + o) % 2, 0, i * 12 + n0)
                        if r == 3:
                            silu_of(b, 1, i * 12 + (n0 + 3))
            hid_hi_of(NB - 1, (NB - 1) % 2, 1, base_of(NB - 1))
            for t in range(T):
                square_residual(t, N_OUT, 4 * T + 16 * (NB - 1) + T, junk_f[:])

        @block.vector
        def _(dve):
            def split_lo(n, turns=0):
                dve.wait_ge(hi_ready, turns * 12 + (n + 1))
                w = width(n)
                nc.vector.tensor_tensor(w_lo[n % SLOTS][:, 0:w], w_raw[n % RAWS][:, 0:w],
                                        w_hi[n % SLOTS][:, 0:w].bitcast(FP32), ALU.subtract).then_inc(lo_ready, 1)

            def normalise(n, dst, src, gains, done):
                dve.wait_ge(rstd_ready, n + 1)
                dve.wait_ge(gain_in if gains else mix_gain_in, 16 * max(gains, 1))
                nc.vector.scalar_tensor_tensor(out=dst, in0=src, scalar=rstd[:, n:n + 1], in1=gain[:],
                                               op0=ALU.mult, op1=ALU.mult).then_inc(done, 1)

            def minus_hi(out, a, hi, done):
                nc.vector.tensor_tensor(out, a, hi.bitcast(FP32), ALU.subtract).then_inc(done, 1)

            def xt_lo_of(n, bank, hi, lo):
                dve.wait_ge(xt_hi, n + 1)
                minus_hi(lo, two(bank).rearrange("p (k n) -> p k n", n=P), hi, xt_lo)

            nc.vector.memset(u_sb[:, :, 0:PAD], 0.0).then_inc(pads_zero, 1)
            for w in win:
                nc.vector.memset(w[:, 0:PAD], 0.0).then_inc(pads_zero, 1)
            dve.wait_ge(consts_set, 6)
            nc.vector.tensor_copy(count[:], count_i[:]).then_inc(pads_zero, 1)
            dve.wait_ge(pads_zero, 4)
            nc.vector.reciprocal(inv_count[:], count[:]).then_inc(pads_zero, 1)

            for t in range(T + 2):
                if t < T:
                    if t >= 2:
                        dve.wait_ge(xt_done, t - 1)
                    normalise(t, xn_a[t % 2][:], x_in[t % 4][:], 0, xn_ready)
                if t == 3:
                    split_lo(0)
                    split_lo(1)
                if t >= 2:
                    xt_lo_of(t - 2, 2 * ((t - 2) % 4), h_hi[:, :, tile_of(t - 2)], h_lo[:, :, tile_of(t - 2)])

            steps = [0]

            def step(ins):
                steps[0] += 1
                ins.then_inc(win_step, 1)
                dve.wait_ge(win_step, steps[0])

            def pool_group(g):
                w = WINDOWS[g]
                u = u_sb[:, g, :]
                src = u
                for e in range(g + 1):
                    dst = win[e % 2]
                    step(nc.vector.tensor_tensor(dst[:, PAD:], src[:, PAD:], src[:, PAD - (1 << e):PAD + S - (1 << e)], ALU.add))
                    src = dst[:, :]
                step(nc.vector.scalar_tensor_tensor(out=pooled[:], in0=src[:, PAD:], scalar=1.0 / w, in1=u[:, PAD:],
                                                    op0=ALU.mult, op1=ALU.subtract))
                step(nc.vector.tensor_tensor(pooled[:, 0:w], src[:, PAD:PAD + w], inv_count[:, 0:w], ALU.mult))
                nc.vector.tensor_tensor(pooled[:, 0:w], pooled[:, 0:w], u[:, PAD:PAD + w], ALU.subtract).then_inc(d_ready, 1)

            def pooled_lo(g):
                dve.wait_ge(d_hi_ready, g + 1)
                minus_hi(d_lo[:, g, :], pooled[:], d_hi[:, g, :], d_lo_ready)
                dve.wait_ge(d_lo_ready, g + 1)

            dve.wait_ge(pads_zero, 5)
            for k in range(C_U, C_V + 4):
                split_lo(k + 2)
                if k >= C_V:
                    g = k - C_V
                    if g:
                        pooled_lo(g - 1)
                    dve.wait_ge(u_copied, g + 1)
                    pool_group(g)
            split_lo(C_F + 2)
            pooled_lo(NG - 1)
            split_lo(C_PW + 2)

            nc.vector.memset(f_tok[:, T * HEADS:], 0.0).then_inc(f_copied, 1)
            dve.wait_ge(w_used, C_F + 1)
            nc.vector.tensor_copy(f_tok[:, 0:T * HEADS], ps[:, 0, 0:T * HEADS]).then_inc(f_copied, 1)

            def mixed_lo(g):
                dve.wait_ge(mix_hi, g + 1)
                nc.vector.scalar_tensor_tensor(out=d_lo[:, g, :], in0=two(2 + 2 * (g % 3)), scalar=ps_scale[:, g:g + 1],
                                               in1=d_hi[:, g, :].bitcast(FP32), op0=ALU.mult, op1=ALU.subtract).then_inc(mix_lo, 1)

            for g in range(NG - 1):
                mixed_lo(g)
            dve.wait_ge(f_tr_done, 1)
            nc.vector.tensor_copy(f_tr[:], ps[0:T * HEADS, 0, 0:P]).then_inc(f_tr_copied, 1)
            mixed_lo(NG - 1)

            def gated(m, c, dst, gate, chunk, gates):
                if c == 0:
                    dve.wait_ge(y_done, gates // 2 + m // 2 + 1)
                else:
                    dve.wait_ge(w_used, chunk + 1)
                dve.wait_ge(gate_ready, gates + m + 1)
                nc.vector.tensor_tensor(dst, two(4 + 2 * c), gate, ALU.mult).then_inc(y_gated, 1)

            fsteps = [0]

            def fstep(ins):
                fsteps[0] += 1
                ins.then_inc(f_step, 1)
                dve.wait_ge(f_step, fsteps[0])

            for k in range(C_PG, C_QK + 1):
                split_lo(k + 2)
                j, r = divmod(k - 1 - C_PG, 3)
                if k > C_PG and r == 2:
                    for c in range(2):
                        m = 2 * j + c
                        if m >= 2:
                            dve.wait_ge(za_stored[c], 16 * (m // 2))
                        gated(m, c, za[c][:], sg[c][:], k - 1, 0)
                if k == C_PG + 2:
                    dve.wait_ge(f_moved, 16 * T)
                    dve.wait_ge(small_in, 48)
                    fstep(nc.vector.tensor_scalar(f_neg[:], f_h[:], bf[:, 0:1], -1.0, ALU.add, ALU.mult))
                    fstep(nc.vector.tensor_scalar(f_h[:], f_h[:], bf[:, 0:1], None, ALU.add))
                    fstep(nc.vector.tensor_tensor(f_min[:], f_h[:], f_neg[:], ALU.min))
                    dve.wait_ge(f_exp_ready, 1)
                    fstep(nc.vector.tensor_scalar(f_u[:], f_exp[:], 1.0, None, ALU.add))
                if k == C_PG + 4:
                    dve.wait_ge(f_log_ready, 1)
                    fstep(nc.vector.tensor_scalar(f_min[:], f_u[:], -1.0, 1e-30, ALU.add, ALU.max))
                    fstep(nc.vector.reciprocal(f_one[:], f_min[:]))
                    fstep(nc.vector.tensor_tensor(f_one[:], f_one[:], f_exp[:], ALU.mult))
                    fstep(nc.vector.tensor_tensor(f_one[:], f_one[:], f_log[:], ALU.mult))
                    fstep(nc.vector.scalar_tensor_tensor(out=f_log[:], in0=f_min[:], scalar=2e-30, in1=f_exp[:],
                                                         op0=ALU.is_lt, op1=ALU.mult))
                    fstep(nc.vector.tensor_tensor(f_one[:], f_one[:], f_log[:], ALU.add))
                if k == C_PG + 5:
                    fstep(nc.vector.scalar_tensor_tensor(out=f_one[:], in0=f_h[:], scalar=0.0, in1=f_one[:],
                                                         op0=ALU.min, op1=ALU.subtract))
                    fstep(nc.vector.memset(f_min[:], 1.0))
                    nc.vector.tensor_tensor_scan(out=f_u[:], data0=f_min[:], data1=f_one[:], initial=0.0,
                                                 op0=ALU.mult, op1=ALU.subtract).then_inc(negc_ready, 1)
            split_lo(C_QK + 3)

            for u in range(PAIRS * T):
                p, i = divmod(u, T)
                b, n = u % 2, (i + 1) * P
                if u % 4 == 0 and u < 4 * 6:
                    split_lo(C_QK + 2 + u // 4 + 2)
                for a in range(2):
                    dve.wait_ge(sc_done, 2 * u + a + 1)
                    dve.wait_ge(negc_loaded[p % 2], 32 * (p // 2 + 1))
                    if u >= 2:
                        dve.wait_ge(pt_done, groups_before(u - 1))
                    nc.vector.tensor_tensor_reduce(out=prob[b][:, a, 0:n], in0=two(2 * a)[:, 0:n], in1=negc[p % 2][:, a, 0:n],
                                                   scale=1.0, scalar=LOWEST, op0=ALU.add, op1=ALU.max,
                                                   accum_out=score_max[:, b, a:a + 1]).then_inc(sc_biased, 1)
                dve.wait_ge(sc_biased, 2 * u + 2)
                nc.vector.tensor_scalar(neg_max[:, b, :], score_max[:, b, :], -1.0, None, ALU.mult).then_inc(nmax_ready, 1)
                dve.wait_ge(exp_ready, 2 * u + 2)
                nc.vector.reciprocal(prob_inv[:, b, :], prob_sum[:, b, :]).then_inc(inv_ready, 1)
                dve.wait_ge(inv_ready, u + 1)
                for a in range(2):
                    nc.vector.tensor_scalar(prob[b][:, a, 0:n], prob[b][:, a, 0:n], prob_inv[:, b, a:a + 1], None,
                                            ALU.mult).then_inc(prob_ready, 1)

            for k in range(C_FG, C_WO + 1):
                split_lo(k + 2)
                j, r = divmod(k - 1 - C_FG, 3)
                if k == C_FG:
                    for p in range(PAIRS):
                        dve.wait_ge(o_hi_ready, p + 1)
                        minus_hi(o_lo[:, p, :], o_sb[:, p, :], o_hi[:, p, :], o_lo_ready)
                elif r == 2:
                    for c in range(2):
                        gated(2 * j + c, c, sg_e[c][:], sg_e[c][:], k - 1, KD)
                    for c in range(2):
                        m = 2 * j + c
                        dve.wait_ge(y_gated, KD + m + 1)
                        dve.wait_ge(za_loaded, 16 * (m + 1))
                        nc.vector.tensor_tensor(sg_e[c][:], sg_e[c][:], za_e[:], ALU.add).then_inc(z_sum, 1)
                    for c in range(2):
                        m = 2 * j + c
                        dve.wait_ge(z_hi_ready, m + 1)
                        minus_hi(z_lo[:, m, :], sg_e[c][:], z_hi[:, m, :], z_lo_ready)

            def add(t, n, earlier, outs, used, turns=0):
                if t < T - 1:
                    dve.wait_ge(bank_out, turns * 28 + (outs + t + 1))
                else:
                    dve.wait_ge(w_used, turns * 12 + used)
                if earlier >= 2 * T:
                    dve.wait_ge(xr_added, turns * 32 + (earlier + t - 2 * T + 1))
                nc.vector.tensor_tensor(xr[:, t, half_of(n)], ps[:, t, :], xr[:, t, half_of(n)], ALU.add).then_inc(xr_added, 1)

            for k in range(C_WO + 1, C_XK):
                split_lo(k + 2)
                if k == C_WO + 1:
                    for t in range(2):
                        normalise(N_MEM + t, xn_m[:, t, :], mem_in[:, t, :], 1, xn_ready)
                if k == C_WO + 3:
                    dve.wait_ge(xr_loaded, 16 * T)
                    for t in range(T):
                        add(t, 0, 0, 0, C_WO + 4)
                if k == C_WO + 4:
                    for t in range(2):
                        xt_lo_of(N_MEM + t, 2 * t, mt_hi[:, :, tile_of(t)], mt_lo[:, :, tile_of(t)])
                if k == C_WO + 7:
                    for t in range(T):
                        add(t, 1, T, T - 1, C_WO + 8)

            for s in range(10):
                if s < 8:
                    split_lo(C_XK + s + 2)
                    if s < 2:
                        dve.wait_ge(xt_done, N_CROSS)
                    else:
                        dve.wait_ge(xt_done, N_CROSS + s - 1)
                    normalise(N_CROSS + s, xn_x[s % 2][:], xr[:, s, :], 2, xn_ready)
                if 1 <= s < 5:
                    dve.wait_ge(kv_hi, s)
                    minus_hi(xk_lo[:, s - 1, :], ps[:, s - 1, 0:MEM], xk_hi[:, s - 1, :], kv_lo)
                if s == 8:
                    for t in range(2):
                        dve.wait_ge(kv_hi, XH + t + 1)
                        minus_hi(xv_lo[:, t, :], ps[:, 4 + t, :], xv_hi[:, t, :], kv_lo)
                if s >= 2:
                    xt_lo_of(N_CROSS + s - 2, 6, hx_hi[:, :, tile_of(s - 2)], hx_lo[:, :, tile_of(s - 2)])

            def xpt_lo_of(h, half):
                dve.wait_ge(xpt_hi_ready, 2 * h + half + 1)
                minus_hi(xpt_lo[:], ps[:, 6:8, :], xpt_hi[:], xpt_lo_ready)

            def xo_lo_of(h, half):
                dve.wait_ge(xo_hi_ready, 2 * h + half + 1)
                minus_hi(xo_lo[:, h, half_of(half)], ps[:, half, :], xo_hi[:, h, half_of(half)], xo_lo_ready)

            for h in range(XH):
                split_lo(C_XQ + h + 2)
                dve.wait_ge(xq_hi_ready, h + 1)
                minus_hi(xq_lo[:], two(0), xq_hi[:], xq_lo_ready)
                for half in range(2):
                    if h:
                        xpt_lo_of(h - 1, half)
                    g = 2 * h + half
                    dve.wait_ge(xs_done, g + 1)
                    t4 = slice(4 * half, 4 * half + 4)
                    for b in range(2):
                        t0 = 4 * half + 2 * b
                        nc.vector.tensor_reduce(x_max[:, h, t0:t0 + 2], ps[:, 2 + t0 // 2, :].rearrange("p (q m) -> p q m", m=MEM),
                                                AX, ALU.max).then_inc(xs_max, 1)
                    dve.wait_ge(xs_max, 2 * g + 2)
                    nc.vector.tensor_scalar(x_nmax[:, h, t4], x_max[:, h, t4], -XDH ** -0.5, None, ALU.mult).then_inc(xs_nmax, 1)
                    dve.wait_ge(xs_exp, 4 * g + 4)
                    nc.vector.reciprocal(x_inv[:, h, t4], x_sum[:, h, t4]).then_inc(xs_inv, 1)
                    dve.wait_ge(xs_inv, g + 1)
                    for t in range(4 * half, 4 * half + 4):
                        nc.vector.tensor_scalar(xp[:, t, :], xp[:, t, :], x_inv[:, h, t:t + 1], None, ALU.mult).then_inc(xp_ready, 1)
                    if h:
                        xo_lo_of(h - 1, half)
            for half in range(2):
                xpt_lo_of(XH - 1, half)
                xo_lo_of(XH - 1, half)
            split_lo(C_XO + 2)
            split_lo(C_XO + 3)
            for t in range(T):
                add(t, 0, 2 * T, 2 * (T - 1), C_XO + 2)
            split_lo(C_FF)
            split_lo(C_FF + 1)
            for t in range(T + 4):
                if t < T:
                    add(t, 1, 3 * T, 3 * (T - 1), C_XO + 4)
                if 2 <= t < T + 2:
                    n = t - 2
                    dve.wait_ge(xt_done, N_FFN + n - 1)
                    normalise(N_FFN + n, xn_f[n % 2][:], xr[:, n, :], 3, xn_ready)
                if t >= 4:
                    n = t - 4
                    xt_lo_of(N_FFN + n, 2 * (n % 4), hf_hi[:, :, tile_of(n)], hf_lo[:, :, tile_of(n)])

            def hid_of(b, j, used):
                dve.wait_ge(w_used, used)
                dve.wait_ge(silu_ready, b * 2 + (j + 1))
                if not (isinstance(b, int) and b == 0):
                    dve.wait_ge(hid_lo_ready, b * 2 + (j - 1))
                nc.vector.tensor_tensor(hid[j][:], two(4 * j + 2), silu[j][:], ALU.mult).then_inc(hid_ready, 1)

            split_lo(C_FF + 2)
            split_lo(C_FF + 3)
            split_lo(C_FF + 4)
            hid_of(0, 0, C_FF + 2)
            split_lo(C_FF + 5)
            hid_of(0, 1, C_FF + 4)
            with dve.Fori(0, (NB - 1) // 2) as i:
                for o in range(2):
                    n0 = base_of(1 + o)
                    for r in range(6):
                        split_lo(n0 + r + 2, i)
                        if r in (2, 4):
                            hid_of(i * 2 + (1 + o), r // 2 - 1, i * 12 + (n0 + r))
                        if r >= 4:
                            for t in range(T):
                                add(t, r - 4, 4 * T + 2 * T * o + T * (r - 4), 4 * (T - 1) + 2 * (T - 1) * o + (T - 1) * (r - 4),
                                    n0 + r + 1, i)
            blocks = NB - 1
            for n in range(2):
                for t in range(T + 2 * n):
                    if t < T:
                        add(t, n, 4 * T + 2 * T * blocks + T * n, 4 * (T - 1) + 2 * (T - 1) * blocks + (T - 1) * n, N_CHUNKS - 1 + n)
                    if n == 1 and t >= 2:
                        m = t - 2
                        if m >= 3:
                            dve.wait_ge(out_stored[m % 3], 16 * (m // 3))
                        normalise(N_OUT + m, y_out[m % 3][:], xr[:, m, :], 4, out_ready)

        @block.tensor
        def _(pe):
            def mm3(dst, w_h, w_l, x_h, x_l, start, stop):
                nc.tensor.matmul(dst, w_h, x_l, start=start, stop=False)
                nc.tensor.matmul(dst, w_h, x_h, start=False, stop=False)
                return nc.tensor.matmul(dst, w_l, x_h, start=False, stop=stop)

            def transpose_tile(src, bank, done):
                for k in range(KD):
                    last = nc.tensor.transpose(two(bank)[:, tile_of(k)], src[:, tile_of(k)], ident[:])
                last.then_inc(done, 1)

            def project_half(n, h, dst, x_hi, x_lo, tiles=KD, c=0, stride=P):
                wh, wl = w_hi[n % SLOTS], w_lo[n % SLOTS]
                for k in range(tiles):
                    w = slice(k * stride + c * P, k * stride + (c + 1) * P)
                    last = mm3(dst, wh[:, w], wl[:, w], x_hi[:, k, half_of(h)], x_lo[:, k, half_of(h)],
                               k == 0, k == tiles - 1)
                return last

            def project(n, bank, x_hi, x_lo, turns=0):
                pe.wait_ge(lo_ready, turns * 12 + (n + 1))
                for h in range(2):
                    last = project_half(n, h, ps[:, bank + h, :], x_hi, x_lo)
                last.then_inc(w_used, 1)

            def project_pair(n, x_hi, x_lo):
                pe.wait_ge(lo_ready, n + 1)
                for c in range(2):
                    for h in range(2):
                        last = project_half(n, h, ps[:, 4 + 2 * c + h, :], x_hi, x_lo, 4, c, 2 * P)
                    last.then_inc(y_done if c == 0 else w_used, 1)

            def tokens_by(n, k0, x_hi, x_lo, first, last_chunk, bank_free, turns=0, banks=True):
                pe.wait_ge(lo_ready, turns * 12 + (n + 1))
                wh, wl = w_hi[n % SLOTS], w_lo[n % SLOTS]
                for t in range(T):
                    if first:
                        bank_free(t)
                    for r in range(2):
                        last = mm3(ps[:, t, :], x_hi[:, k0 + r, tile_of(t)], x_lo[:, k0 + r, tile_of(t)],
                                   wh[:, half_of(r)], wl[:, half_of(r)], first and r == 0, last_chunk and r == 1)
                    if t == T - 1:
                        last.then_inc(w_used, 1)
                    elif last_chunk and banks:
                        last.then_inc(bank_out, 1)

            pe.wait_ge(consts_set, 5)
            for t in range(T):
                pe.wait_ge(xn_ready, t + 1)
                if t >= 4:
                    pe.wait_ge(xt_lo, t - 3)
                transpose_tile(xn_a[t % 2], 2 * (t % 4), xt_done)
            pe.wait_ge(xt_lo, T)
            for g in range(NG):
                project(C_U + g, 2 * g, h_hi, h_lo)
            for r in range(4):
                tokens_by(C_V + r, 2 * r, h_hi, h_lo, r == 0, r == 3, lambda t: pe.wait_ge(u_copied, t // 2 + 1), banks=False)
            pe.wait_ge(lo_ready, C_F + 1)
            pe.wait_ge(v_copied, 1)
            wh, wl = w_hi[C_F % SLOTS], w_lo[C_F % SLOTS]
            for t in range(T):
                for k in range(KD):
                    w = slice(k * HEADS, (k + 1) * HEADS)
                    last = mm3(ps[:, 0, t * HEADS:(t + 1) * HEADS], h_hi[:, k, tile_of(t)], h_lo[:, k, tile_of(t)],
                               wh[:, w], wl[:, w], k == 0, k == KD - 1)
            last.then_inc(w_used, 1)
            pe.wait_ge(lo_ready, C_PW + 1)
            pe.wait_ge(v_copied, T)
            for g in range(NG):
                if g == NG - 1:
                    pe.wait_ge(f_copied, 2)
                    nc.tensor.transpose(ps[:, 0, 0:P], f_tok[:], ident[:]).then_inc(f_tr_done, 1)
                    pe.wait_ge(mix_lo, 1)
                pe.wait_ge(d_lo_ready, g + 1)
                for h in range(2):
                    last = mm3(ps[:, 2 + 2 * (g % 3) + h, :], w_hi[C_PW % SLOTS][:, tile_of(g)], w_lo[C_PW % SLOTS][:, tile_of(g)],
                               d_hi[:, g, half_of(h)], d_lo[:, g, half_of(h)], True, True)
                last.then_inc(mix_done if g < NG - 1 else w_used, 1)
            pe.wait_ge(mix_lo, NG)
            pe.wait_ge(f_tr_copied, 1)
            for j in range(4):
                for r in range(2):
                    if j:
                        pe.wait_ge(gate_ready, 2 * j + r - 1)
                    project(C_PG + 3 * j + r, 2 * r, h_hi, h_lo)
                if j:
                    pe.wait_ge(y_gated, 2 * j)
                project_pair(C_PG + 3 * j + 2, d_hi, d_lo)

            def qk_group(g, half=None):
                p, r = divmod(g, 4)
                which, h = divmod(r, 2)
                n = C_QK + 2 * p + which
                bank = 4 + r if p == 0 else 7
                if half != 1:
                    pe.wait_ge(lo_ready, n + 1)
                    if p:
                        pe.wait_ge(qk_copied, g)
                for k in range(KD) if half is None else range(4 * half, 4 * half + 4):
                    w = tile_of(k)
                    last = mm3(ps[:, bank, :], w_hi[n % SLOTS][:, w], w_lo[n % SLOTS][:, w],
                               h_hi[:, k, half_of(h)], h_lo[:, k, half_of(h)], k == 0, k == KD - 1)
                if half != 0:
                    last.then_inc(w_used if h else qk_done, 1)

            pe.wait_ge(y_gated, KD)
            pe.wait_ge(gate_ready, KD)
            for g in range(4):
                qk_group(g)

            pe.wait_ge(consts_r, 2)
            groups = 0
            for u in range(PAIRS * T + 1):
                p, i = divmod(u, T)
                if u < PAIRS * T:
                    pe.wait_ge(qk_copied, 4 * p + 4)
                    for a in range(2):
                        if u:
                            pe.wait_ge(sc_biased, 2 * (u - 1) + a + 1)
                        hd = slice(a * DH, (a + 1) * DH)
                        for c in range(0, i + 1, 4):
                            n = min(4, i + 1 - c)
                            dst = ps[:, 2 * a + c // 4, 0:n * P]
                            diagonal = c + n == i + 1
                            last = nc.tensor.matmul(dst, q_sb[p % 2][hd, tile_of(i)], k_sb[p % 2][hd, c * P:(c + n) * P],
                                                    start=True, stop=not diagonal)
                            if diagonal:
                                last = nc.tensor.matmul(dst[:, (n - 1) * P:], ident_r[:], mask_r[:], start=False, stop=True)
                        last.then_inc(sc_done, 1)
                if u < 3 * T:
                    qk_group(4 + u // 2, u % 2)
                if u:
                    pi, b = (u - 1) % T, (u - 1) % 2
                    pe.wait_ge(prob_ready, 2 * u)
                    for a in range(2):
                        for j0 in range(0, pi + 1, 4):
                            if groups >= 2:
                                pe.wait_ge(pt_copied, groups - 1)
                            for j in range(j0, min(j0 + 4, pi + 1)):
                                last = nc.tensor.transpose(ps[:, 4 + groups % 2, tile_of(j - j0)],
                                                           prob[b][:, a, tile_of(j)], ident[:])
                            last.then_inc(pt_done, 1)
                            groups += 1
                if u:
                    pe.wait_ge(pt_copied, groups)
                    if u > 1:
                        pe.wait_ge(pv_copied, u - 1)
                    for j in range(pi + 1):
                        for a in range(2):
                            hc = (2 * ((u - 1) // T) + a) * DH
                            last = nc.tensor.matmul(ps[a * DH:(a + 1) * DH, 6, 0:P], v_sb[:, j, hc:hc + DH],
                                                    prob_t[b][:, a, tile_of(j)], start=j == 0, stop=j == pi)
                    last.then_inc(pv_done, 1)

            for j in range(4):
                for r in range(2):
                    if j:
                        pe.wait_ge(gate_ready, KD + 2 * j + r - 1)
                    project(C_FG + 3 * j + r, 2 * r, h_hi, h_lo)
                if j:
                    pe.wait_ge(y_gated, KD + 2 * j)
                else:
                    pe.wait_ge(o_lo_ready, PAIRS)
                    pe.wait_ge(pv_copied, PAIRS * T)
                project_pair(C_FG + 3 * j + 2, o_hi, o_lo)

            pe.wait_ge(gate_ready, 2 * KD)
            for r in range(4):
                pe.wait_ge(z_lo_ready, 2 * r + 2)
                tokens_by(C_WO + r, 2 * r, z_hi, z_lo, r == 0, r == 3,
                          lambda t: pe.wait_ge(y_gated, 2 * KD) if t == 4 else None)
            for t in range(2):
                pe.wait_ge(xn_ready, N_MEM + t + 1)
                pe.wait_ge(xr_added, 2 * t + 2)
                transpose_tile(xn_m[:, t, :], 2 * t, xt_done)

            def w_out_bank(t):
                pe.wait_ge(xr_added, t + 1)
                if t in (0, 2):
                    pe.wait_ge(xt_lo, N_MEM + t // 2 + 1)

            for r in range(4):
                tokens_by(C_WO + 4 + r, 2 * r, z_hi, z_lo, r == 0, r == 3, w_out_bank)

            def cross_tile(t):
                pe.wait_ge(xn_ready, N_CROSS + t + 1)
                pe.wait_ge(xr_added, 2 * T)
                if t:
                    pe.wait_ge(xt_lo, N_CROSS + t)
                transpose_tile(xn_x[t % 2], 6, xt_done)

            for s in range(8):
                n = C_XK + s
                pe.wait_ge(lo_ready, n + 1)
                if s < XH:
                    pe.wait_ge(xr_added, T + s + 1)
                    for k in range(KD):
                        last = mm3(ps[:, s, 0:MEM], w_hi[n % SLOTS][:, tile_of(k)], w_lo[n % SLOTS][:, tile_of(k)],
                                   mt_hi[:, k, :], mt_lo[:, k, :], k == 0, k == KD - 1)
                else:
                    if s == XH:
                        pe.wait_ge(xr_added, 2 * T)
                    for t in range(2):
                        for r in range(2):
                            k = 2 * (s - XH) + r
                            last = mm3(ps[:, 4 + t, :], mt_hi[:, k, tile_of(t)], mt_lo[:, k, tile_of(t)],
                                       w_hi[n % SLOTS][:, half_of(r)], w_lo[n % SLOTS][:, half_of(r)], k == 0, k == KD - 1)
                last.then_inc(w_used, 1)
                if s >= 1:
                    cross_tile(s - 1)
            cross_tile(T - 1)

            def xpt(h, half):
                pe.wait_ge(xp_ready, 8 * h + 4 * half + 4)
                if h or half:
                    pe.wait_ge(xpt_lo_ready, 2 * h + half)
                for m in range(2):
                    for t in range(4):
                        last = nc.tensor.transpose(ps[:, 6 + m, tile_of(t)], xp[:, 4 * half + t, tile_of(m)], ident[:])
                last.then_inc(xpt_done, 1)

            def xpv(h, half):
                pe.wait_ge(xpt_lo_ready, 2 * h + half + 1)
                for m in range(2):
                    last = mm3(ps[:, half, :], xv_hi[:, m, tile_of(h)], xv_lo[:, m, tile_of(h)],
                               xpt_hi[:, m, :], xpt_lo[:, m, :], m == 0, m == 1)
                last.then_inc(xpv_done, 1)

            pe.wait_ge(xt_lo, N_FFN)
            pe.wait_ge(kv_lo, XH + 2)
            for h in range(XH):
                if h >= 2:
                    pe.wait_ge(xo_lo_ready, 2 * (h - 1))
                project(C_XQ + h, 0, hx_hi, hx_lo)
                for half in range(2):
                    if h:
                        xpt(h - 1, half)
                    if half == 0:
                        pe.wait_ge(xq_lo_ready, h + 1)
                    if h:
                        pe.wait_ge(xs_exp, 8 * (h - 1) + 4 * half + 4)
                    for t in range(4 * half, 4 * half + 4):
                        last = mm3(ps[:, 2 + t // 2, (t % 2) * MEM:(t % 2 + 1) * MEM], xq_hi[:, tile_of(t)], xq_lo[:, tile_of(t)],
                                   xk_hi[:, h, :], xk_lo[:, h, :], True, True)
                    last.then_inc(xs_done, 1)
                    if h:
                        xpv(h - 1, half)
            for half in range(2):
                xpt(XH - 1, half)
                xpv(XH - 1, half)

            pe.wait_ge(xo_lo_ready, 2 * XH)
            for n in range(2):
                for r in range(2):
                    tokens_by(C_XO + 2 * n + r, 2 * r, xo_hi, xo_lo, r == 0, r == 1,
                              (lambda t: pe.wait_ge(xr_added, 2 * T + t + 1)) if n else (lambda t: None))
            for t in range(T):
                pe.wait_ge(xn_ready, N_FFN + t + 1)
                pe.wait_ge(xr_added, 3 * T + 2 * (t % 4) + 2)
                if t >= 4:
                    pe.wait_ge(xt_lo, N_FFN + t - 3)
                transpose_tile(xn_f[t % 2], 2 * (t % 4), xt_done)

            pe.wait_ge(xt_lo, N_OUT)
            for r in range(4):
                project(C_FF + r, 2 * r, hf_hi, hf_lo)

            def ffn_out(b, par, n0, turns, last_block=False):
                pe.wait_ge(hid_lo_ready, turns * 4 + 2 * (b + 1))
                for n in range(2):
                    def bank_free(t):
                        if n:
                            pe.wait_ge(xr_added, turns * 32 + (4 * T + 2 * T * b + t + 1))
                        elif not last_block and t % 2 == 0:
                            pe.wait_ge(hid_ready if t % 4 else silu_ready, turns * 4 + (2 * (b + 1) + t // 4 + 1))
                        elif last_block:
                            pe.wait_ge(xr_added, 4 * T + 2 * T * b - T + t + 1)
                    tokens_by(n0 + n, 0, hid_hi[par], hid_lo[par], True, True, bank_free, turns)

            with pe.Fori(0, (NB - 1) // 2) as i:
                for o in range(2):
                    n0 = base_of(1 + o)
                    for r in range(4):
                        pe.wait_ge(xr_added, i * 32 + (4 * T + 2 * T * (o - 1) + T + 2 * r + 2))
                        pe.wait_ge(hid_ready if r % 2 else silu_ready, i * 4 + (2 * o + r // 2 + 1))
                        project(n0 + r, 2 * r, hf_hi, hf_lo, i)
                    ffn_out(o, o, n0 + 4, i)
            ffn_out(NB - 1, (NB - 1) % 2, N_CHUNKS - 2, 0, True)


def groups_before(u):
    return sum(2 * (1 + v % T // 4) for v in range(u))


_INS = ["x", "mem", "norm_mix_g", "w_in", "b_forget", "b_gate", "pool_w", "pool_scale", "w_pool_out", "w_fox_out",
        "w_out", "norm_x_g", "norm_mem_g", "w_xq", "w_xkv", "w_xo", "norm_ffn_g", "w_ffn_in", "w_ffn_out", "norm_final_g"]


def kernel(**inputs):
    import numpy as np
    import concourse.bacc as bacc
    from concourse.bass_utils import run_bass_kernel_spmd

    nc = bacc.Bacc("TRN2", target_bir_lowering=False, num_devices=1)
    arrays, args = {}, []
    for name in _INS:
        a = np.ascontiguousarray(inputs[name])
        arrays[f"in_{name}"] = a
        args.append(nc.dram_tensor(f"in_{name}", a.shape, mybir.dt.from_np(a.dtype), kind="ExternalInput").ap())
    args.append(nc.dram_tensor("out_x", (1, S, D), FP32, kind="ExternalOutput").ap())
    build(nc, *args)
    return run_bass_kernel_spmd(nc, [arrays], core_ids=[0]).results[0]["out_x"]
```

```python
from contextlib import ExitStack

import concourse.bass as bass
from concourse import mybir

FP32 = mybir.dt.float32
F32R = mybir.dt.float32r
ALU = mybir.AluOpType
ACT = mybir.ActivationFunctionType
AX = mybir.AxisListType.X

P = 128
S = 1024
D = 1024
T = S // P
KD = D // P
HALF = 512
EPS = 1e-6
WINDOWS = (2, 4, 8, 16)
NG = len(WINDOWS)
PAD = 16
POOL_W = D // 2
HEADS, DH = 8, 64
PAIRS = HEADS // 2
FOX_W = HEADS * DH
MEM = 256
XH, XDH = 4, 128
XW = XH * XDH
DFF = ((8 * D // 3 + 255) // 256) * 256
NB = DFF // (2 * P)
MASKED = -1e30
HIGHEST = 3e38
RAWS, SLOTS = 2, 3

COL_Q = POOL_W
COL_K = COL_Q + FOX_W
COL_V = COL_K + FOX_W
COL_F = COL_V + FOX_W
COL_G = COL_F + HEADS

C_U = 0
C_V = C_U + NG
C_F = C_V + 4
C_PW = C_F + 1
C_PG = C_PW + 1
C_QK = C_PG + 12
C_FG = C_QK + 8
C_WO = C_FG + 12
C_XK = C_WO + 8
C_XV = C_XK + 4
C_XQ = C_XV + 4
C_XO = C_XQ + 4
C_FF = C_XO + 4
N_CHUNKS = C_FF + 6 * NB

N_X, N_MEM, N_CROSS, N_FFN, N_OUT = 0, T, T + 2, 2 * T + 2, 3 * T + 2


def build(nc, x, mem, norm_mix_g, w_in, b_forget, b_gate, pool_w, pool_scale, w_pool_out,
          w_fox_out, w_out, norm_x_g, norm_mem_g, w_xq, w_xkv, w_xo, norm_ffn_g, w_ffn_in,
          w_ffn_out, norm_final_g, out):
    x2, mem2, out2 = x[0], mem[0], out[0]
    w_in, w_out, w_xq, w_xkv, w_xo = w_in[0], w_out[0], w_xq[0], w_xkv[0], w_xo[0]
    w_pool_out, w_fox_out, pool_w = w_pool_out[0], w_fox_out[0], pool_w[0]
    w_ffn_in, w_ffn_out = w_ffn_in[0], w_ffn_out[0]
    za_dram = nc.dram_tensor("za_dram", [KD, P, S], FP32).ap()
    negc_dram = nc.dram_tensor("negc_dram", [HEADS, S], FP32).ap()

    ctx = ExitStack()
    with ctx:
        def keep(name, shape, dt=FP32):
            return ctx.enter_context(nc.sbuf_tensor(name, shape, dt))

        def place(name, kb, shape, dt=FP32):
            with ExitStack() as st:
                if kb:
                    st.enter_context(nc.sbuf_tensor(f"under_{name}", [P, kb * 256], FP32))
                return st.enter_context(nc.sbuf_tensor(name, shape, dt))

        w_raw = [keep(f"w_raw{i}", [P, 1024]) for i in range(RAWS)]
        w_hi = [keep(f"w_hi{i}", [P, 1024], F32R) for i in range(SLOTS)]
        w_lo = [keep(f"w_lo{i}", [P, 1024], F32R) for i in range(SLOTS)]
        ident = keep("ident", [P, P])
        ident_r = keep("ident_r", [P, P], F32R)
        mask = keep("mask", [P, P])
        mask_r = keep("mask_r", [P, P], F32R)
        n_tiles = N_OUT + T
        ss = keep("ss", [P, n_tiles])
        ms = keep("ms", [P, n_tiles])
        rstd = keep("rstd", [P, n_tiles])
        minus_half = keep("minus_half", [P, 1])
        bg = keep("bg", [P, 2 * KD])
        ps_scale = keep("ps_scale", [P, NG])
        count_i = keep("count_i", [P, PAD], mybir.dt.int32)
        count = keep("count", [P, PAD])
        inv_count = keep("inv_count", [P, PAD])
        bf = keep("bf", [HEADS, 1])
        neg_max = keep("neg_max", [P, 2, 2])
        prob_sum = keep("prob_sum", [P, 2, 2])
        prob_inv = keep("prob_inv", [P, 2, 2])
        x_max = keep("x_max", [P, XH, T])
        x_nmax = keep("x_nmax", [P, XH, T])
        x_sum = keep("x_sum", [P, XH, T])
        x_inv = keep("x_inv", [P, XH, T])

        h_hi = place("h_hi", 0, [P, KD, S], F32R)
        h_lo = place("h_lo", 32, [P, KD, S], F32R)
        x_in = [place(f"x_in{i}", 64 + 4 * i, [P, D]) for i in range(4)]
        xn_a = [place(f"xn_a{i}", 80 + 4 * i, [P, D]) for i in range(2)]
        v_sb = place("v_sb", 64, [P, T, FOX_W])
        u_sb = place("u_sb", 88, [P, NG, PAD + S])
        win = [place(f"win{i}", 105 + 5 * i, [P, PAD + S]) for i in range(2)]
        pooled = place("pooled", 115, [P, S])
        d_hi = place("d_hi", 119, [P, NG, S], F32R)
        d_lo = place("d_lo", 135, [P, NG, S], F32R)
        sg = [place(f"sg{i}", 151 + 4 * i, [P, S]) for i in range(2)]
        za = [place(f"za{i}", 80 + 4 * i, [P, S]) for i in range(2)]
        f_h = place("f_h", 90, [HEADS, S])
        f_neg = place("f_neg", 94, [HEADS, S])
        f_min = place("f_min", 98, [HEADS, S])
        f_exp = place("f_exp", 102, [HEADS, S])
        f_u = place("f_u", 106, [HEADS, S])
        f_log = place("f_log", 110, [HEADS, S])
        f_one = place("f_one", 114, [HEADS, S])
        q1 = [[place(f"q1_{i}{a}", (160, 88)[i] + 4 * a, [P, S], F32R) for a in range(2)] for i in range(2)]
        q2 = [place(f"q2_{i}", (168, 96)[i], [P, S], F32R) for i in range(2)]
        k1 = [[place(f"k1_{i}{a}", (80, 100)[i] + 4 * a, [P, S], F32R) for a in range(2)] for i in range(2)]
        negc = [place(f"negc{i}", 108 + 4 * i, [P, S]) for i in range(3)]
        prob = [place(f"prob{i}", 120 + 8 * i, [P, 2, S]) for i in range(2)]
        prob_t = place("prob_t", 136, [P, 2, S])
        o_sb = place("o_sb", 144, [P, PAIRS, S])
        o_hi = place("o_hi", 64, [P, PAIRS, S], F32R)
        o_lo = place("o_lo", 80, [P, PAIRS, S], F32R)
        z_hi = place("z_hi", 96, [P, KD, S], F32R)
        z_lo = place("z_lo", 128, [P, KD, S], F32R)
        sg_e = [place(f"sg_e{i}", 160 + 4 * i, [P, S]) for i in range(2)]
        za_e = place("za_e", 168, [P, S])
        xr = place("xr", 64, [P, T, D])
        gain = place("gain", 168, [P, D])
        mem_in = place("mem_in", 24, [P, 2, D])
        xn_m = place("xn_m", 160, [P, 2, D])
        mt_hi = place("mt_hi", 32, [P, KD, MEM], F32R)
        mt_lo = place("mt_lo", 40, [P, KD, MEM], F32R)
        xk_hi = place("xk_hi", 0, [P, XH, MEM], F32R)
        xk_lo = place("xk_lo", 4, [P, XH, MEM], F32R)
        xv_hi = place("xv_hi", 8, [P, 2, XW], F32R)
        xv_lo = place("xv_lo", 12, [P, 2, XW], F32R)
        hx_hi = place("hx_hi", 96, [P, KD, S], F32R)
        hx_lo = place("hx_lo", 128, [P, KD, S], F32R)
        xn_x = [place(f"xn_x{i}", 160 + 4 * i, [P, D]) for i in range(2)]
        xq_hi = place("xq_hi", 16, [P, S], F32R)
        xq_lo = place("xq_lo", 20, [P, S], F32R)
        xp = place("xp", 24, [P, T, MEM])
        xo_hi = place("xo_hi", 32, [P, XH, S], F32R)
        xo_lo = place("xo_lo", 48, [P, XH, S], F32R)
        xpt_hi = place("xpt_hi", 160, [P, 2, HALF], F32R)
        xpt_lo = place("xpt_lo", 164, [P, 2, HALF], F32R)
        junk_x = place("junk_x", 28, [P, D])
        junk_f = place("junk_f", 156, [P, D])
        hf_hi = place("hf_hi", 0, [P, KD, S], F32R)
        hf_lo = place("hf_lo", 32, [P, KD, S], F32R)
        xn_f = [place(f"xn_f{i}", 160 + 4 * i, [P, D]) for i in range(2)]
        hid_hi = [place(f"hid_hi{i}", 96 + 16 * i, [P, 2, S], F32R) for i in range(2)]
        hid_lo = [place(f"hid_lo{i}", 104 + 16 * i, [P, 2, S], F32R) for i in range(2)]
        silu = [place(f"silu{i}", 128 + 4 * i, [P, S]) for i in range(2)]
        hid = [place(f"hid{i}", 136 + 4 * i, [P, S]) for i in range(2)]
        y_out = [place(f"y_out{i}", 144 + 4 * i, [P, D]) for i in range(3)]

        ps = ctx.enter_context(nc.psum_tensor("ps", [P, 8, HALF], FP32))

        def two(b):
            return ps[:, b:b + 2, :].rearrange("p b n -> p (b n)")

        def sem(name):
            return ctx.enter_context(nc.semaphore(name))

        raw_loaded = [sem(f"raw_loaded{i}") for i in range(RAWS)]
        hi_ready, lo_ready, w_used = sem("hi_ready"), sem("lo_ready"), sem("w_used")
        consts_set, consts_r, small_in, gain_in = sem("consts_set"), sem("consts_r"), sem("small_in"), sem("gain_in")
        x_loaded = [sem(f"x_loaded{i}") for i in range(4)]
        ss_ready, ms_ready, rstd_ready = sem("ss_ready"), sem("ms_ready"), sem("rstd_ready")
        xn_ready, xt_done, xt_hi, xt_lo = sem("xn_ready"), sem("xt_done"), sem("xt_hi"), sem("xt_lo")
        u_done, u_copied, v_done, v_copied = sem("u_done"), sem("u_copied"), sem("v_done"), sem("v_copied")
        pads_zero, win_step, d_ready, d_hi_ready, d_lo_ready = (sem("pads_zero"), sem("win_step"), sem("d_ready"),
                                                                sem("d_hi_ready"), sem("d_lo_ready"))
        mix_done, mix_hi, mix_lo = sem("mix_done"), sem("mix_hi"), sem("mix_lo")
        f_step, f_exp_ready, f_log_ready, negc_ready, negc_stored = (sem("f_step"), sem("f_exp_ready"), sem("f_log_ready"),
                                                                     sem("negc_ready"), sem("negc_stored"))
        gate_done, gate_ready, y_done, za_ready = sem("gate_done"), sem("gate_ready"), sem("y_done"), sem("za_ready")
        za_stored = [sem(f"za_stored{i}") for i in range(2)]
        za_loaded, y_gated, z_sum, z_hi_ready, z_lo_ready = (sem("za_loaded"), sem("y_gated"), sem("z_sum"),
                                                             sem("z_hi_ready"), sem("z_lo_ready"))
        qk_done, qk_hi, qk_lo, negc_loaded = sem("qk_done"), sem("qk_hi"), sem("qk_lo"), [sem(f"negc_loaded{i}") for i in range(3)]
        sc_done, sc_biased, exp_ready, inv_ready, prob_ready = (
            sem("sc_done"), sem("sc_biased"), sem("exp_ready"), sem("inv_ready"), sem("prob_ready"))
        pt_done, pt_act, pt_dve, pv_done, pv_copied, o_hi_ready, o_lo_ready, gate_copied = (
            sem("pt_done"), sem("pt_act"), sem("pt_dve"), sem("pv_done"), sem("pv_copied"), sem("o_hi_ready"),
            sem("o_lo_ready"), sem("gate_copied"))
        mem_loaded, mix_gain_in = sem("mem_loaded"), sem("mix_gain_in")
        xr_loaded, bank_out, xr_added, out_ready, out_stored = (sem("xr_loaded"), sem("bank_out"), sem("xr_added"),
                                                                sem("out_ready"), [sem(f"out_stored{i}") for i in range(3)])
        kv_done, kv_hi, kv_lo = sem("kv_done"), sem("kv_hi"), sem("kv_lo")
        xq_done, xq_hi_ready, xq_lo_ready = sem("xq_done"), sem("xq_hi_ready"), sem("xq_lo_ready")
        xs_done, xs_max, xs_nmax, xs_exp, xs_inv, xp_ready = (sem("xs_done"), sem("xs_max"), sem("xs_nmax"),
                                                              sem("xs_exp"), sem("xs_inv"), sem("xp_ready"))
        xpt_done, xpt_hi_ready, xpt_lo_ready, xpv_done, xo_hi_ready, xo_lo_ready = (
            sem("xpt_done"), sem("xpt_hi_ready"), sem("xpt_lo_ready"), sem("xpv_done"), sem("xo_hi_ready"), sem("xo_lo_ready"))
        fg_done, fu_done, silu_ready, hid_ready, hid_hi_ready, hid_lo_ready = (
            sem("fg_done"), sem("fu_done"), sem("silu_ready"), sem("hid_ready"), sem("hid_hi_ready"), sem("hid_lo_ready"))

        def cols(w, c0, n=P):
            return w[:, c0:c0 + n].rearrange("(k p) n -> p k n", p=P)

        def rows(w, k0, c0, n=HALF):
            return w[k0 * P:(k0 + 2) * P, c0:c0 + n].rearrange("(k p) n -> p k n", p=P)

        def ffn_in_cols(c0):
            return w_ffn_in[:, bass.ds(c0, P)].rearrange("(k p) n -> p k n", p=P)

        def ffn_out_rows(r0, c0):
            return w_ffn_out[bass.ds(r0, 2 * P), c0:c0 + HALF].rearrange("(k p) n -> p k n", p=P)

        def chunk_view(k):
            if k < C_V:
                return cols(w_in, (k - C_U) * P)
            if k < C_F:
                return rows(w_in, 2 * (k - C_V), COL_V)
            if k == C_F:
                return cols(w_in, COL_F)
            if k == C_PW:
                return pool_w.rearrange("g c d -> c g d")
            if k < C_QK:
                j, r = divmod(k - C_PG, 3)
                return cols(w_pool_out, 2 * j * P, 2 * P) if r == 2 else cols(w_in, COL_G + (2 * j + r) * P)
            if k < C_FG:
                p, r = divmod(k - C_QK, 2)
                return cols(w_in, (COL_K if r else COL_Q) + p * P)
            if k < C_WO:
                j, r = divmod(k - C_FG, 3)
                return cols(w_fox_out, 2 * j * P, 2 * P) if r == 2 else cols(w_in, COL_G + D + (2 * j + r) * P)
            if k < C_XK:
                n, r = divmod(k - C_WO, 4)
                return rows(w_out, 2 * r, n * HALF)
            if k < C_XV:
                return cols(w_xkv, (k - C_XK) * P)
            if k < C_XQ:
                return rows(w_xkv, 2 * (k - C_XV), XW)
            if k < C_XO:
                return cols(w_xq, (k - C_XQ) * P)
            if k < C_FF:
                n, r = divmod(k - C_XO, 2)
                return rows(w_xo, 2 * r, n * HALF)
            return ffn_view(0, k - C_FF)

        def ffn_view(b, r):
            if r < 4:
                t, up = divmod(r, 2)
                return ffn_in_cols(b * 2 * P + (t * P + up * DFF))
            return ffn_out_rows((b - 1) * 2 * P, (r - 4) * HALF)

        def width(k):
            return NG * P if k == C_PW else 1024

        block = ctx.enter_context(nc.Block())

        def half_of(h):
            return slice(h * HALF, (h + 1) * HALF)

        def tile_of(t):
            return slice(t * P, (t + 1) * P)

        def base_of(b):
            return b * 6 + (C_FF - 2)

        @block.sync
        def _(sp):
            def load_raw(n, view, uses=None):
                if n >= RAWS:
                    sp.wait_ge(lo_ready, n - RAWS + 1)
                t = w_raw[n % RAWS][:, 0:width(n)]
                if n == C_PW:
                    t = t.rearrange("p (k n) -> p k n", n=P)
                sp.dma_start(t, view).then_inc(raw_loaded[n % RAWS], 16)

            for t in range(T):
                if t == 4:
                    load_raw(0, chunk_view(0))
                    load_raw(1, chunk_view(1))
                if t >= 4:
                    sp.wait_ge(xn_ready, t - 3)
                sp.dma_start(x_in[t % 4][:], x2[tile_of(t), :]).then_inc(x_loaded[t % 4], 16)
            for k in range(2, C_FF + 4):
                load_raw(k, chunk_view(k) if k < C_FF else ffn_view(0, k - C_FF))
            with sp.Fori(0, (NB - 1) // 2) as i:
                for o in range(2):
                    for r in range(6):
                        n = base_of(1 + o) + r
                        sp.wait_ge(lo_ready, i * 12 + (n - RAWS + 1))
                        if r < 4:
                            j, up = divmod(r, 2)
                            view = ffn_in_cols(i * (4 * P) + ((1 + o) * 2 * P + j * P + up * DFF))
                        else:
                            view = ffn_out_rows(i * (4 * P) + o * 2 * P, (r - 4) * HALF)
                        sp.dma_start(w_raw[n % RAWS][:, :], view).then_inc(raw_loaded[n % RAWS], 16)
            for r in range(2):
                load_raw(N_CHUNKS - 2 + r, ffn_view(NB, 4 + r))
            for t in range(T):
                sp.wait_ge(out_ready, t + 1)
                sp.dma_start(out2[tile_of(t), :], y_out[t % 3][:]).then_inc(out_stored[t % 3], 16)
            for i in range(3):
                sp.wait_ge(out_stored[i], 16 * len(range(i, T, 3)))

        @block.gpsimd
        def _(pool):
            nc.gpsimd.memset(ident[:], 0.0).then_inc(consts_set, 1)
            nc.gpsimd.memset(mask[:], 0.0).then_inc(consts_set, 1)
            nc.gpsimd.memset(minus_half[:], -0.5).then_inc(consts_set, 1)
            pool.wait_ge(consts_set, 3)
            nc.gpsimd.affine_select(out=ident[:], in_=ident[:], compare_op=ALU.not_equal, fill=1.0, base=0,
                                    pattern=[[-1, P]], channel_multiplier=1).then_inc(consts_set, 1)
            nc.gpsimd.affine_select(out=mask[:], in_=mask[:], compare_op=ALU.is_ge, fill=MASKED, base=0,
                                    pattern=[[-1, P]], channel_multiplier=1).then_inc(consts_set, 1)
            nc.gpsimd.iota(count_i[:], pattern=[[1, PAD]], base=1, channel_multiplier=0).then_inc(consts_set, 1)

            def rstd_of(n):
                pool.wait_ge(ss_ready, n + 1)
                nc.gpsimd.tensor_scalar(ms[:, n:n + 1], ss[:, n:n + 1], 1.0 / D, EPS,
                                        ALU.mult, ALU.add).then_inc(ms_ready, 1)
                pool.wait_ge(ms_ready, n + 1)
                nc.gpsimd.tensor_tensor(rstd[:, n:n + 1], ms[:, n:n + 1], minus_half[:],
                                        ALU.pow).then_inc(rstd_ready, 1)

            for n in range(N_X, N_MEM):
                rstd_of(n)
            pool.wait_ge(negc_ready, 1)
            pool.dma_start(negc_dram, f_u[:]).then_inc(negc_stored, 16)
            pool.wait_ge(negc_stored, 16)
            pool.wait_ge(y_gated, KD)
            for h in range(HEADS):
                if h >= 3:
                    pool.wait_ge(sc_biased, 2 * (T * ((h - 3) // 2) + T - 1) + (h - 3) % 2 + 1)
                pool.dma_start(negc[h % 3][:], negc_dram[h:h + 1, :].broadcast_to([P, S])).then_inc(negc_loaded[h % 3], 16)
            pool.wait_ge(sc_done, 2 * PAIRS * T)
            for i in range(2):
                pool.wait_ge(za_stored[i], 16 * (KD // 2))
            for m in range(KD):
                if m:
                    pool.wait_ge(z_sum, m)
                pool.dma_start(za_e[:], za_dram[m]).then_inc(za_loaded, 16)
            pool.wait_ge(w_used, C_WO)
            for t in range(2):
                pool.dma_start(mem_in[:, t, :], mem2[tile_of(t), :]).then_inc(mem_loaded, 16)
            for t in range(T):
                pool.dma_start(xr[:, t, :], x2[tile_of(t), :]).then_inc(xr_loaded, 16)

            def load_gain(g):
                pool.dma_start(gain[:], g.broadcast_to([P, D])).then_inc(gain_in, 16)

            pool.wait_ge(z_sum, KD)
            load_gain(norm_mem_g)
            for n in range(N_MEM, N_CROSS):
                rstd_of(n)
            pool.wait_ge(xn_ready, N_CROSS)
            load_gain(norm_x_g)
            for n in range(N_CROSS, N_FFN):
                rstd_of(n)
            pool.wait_ge(xn_ready, N_FFN)
            load_gain(norm_ffn_g)
            for n in range(N_FFN, N_OUT):
                rstd_of(n)
            pool.wait_ge(xn_ready, N_OUT)
            load_gain(norm_final_g.unsqueeze(0))

            def hid_lo_of(f, par, j):
                pool.wait_ge(hid_hi_ready, f + 1)
                nc.gpsimd.tensor_tensor(hid_lo[par][:, j, :], hid[j][:], hid_hi[par][:, j, :].bitcast(FP32),
                                        ALU.subtract).then_inc(hid_lo_ready, 1)

            for j in range(2):
                hid_lo_of(j, 0, j)
            with pool.Fori(0, (NB - 1) // 2) as i:
                for o in range(2):
                    for j in range(2):
                        hid_lo_of(i * 4 + (2 + 2 * o + j), (1 + o) % 2, j)
            for n in range(N_OUT, N_OUT + T):
                rstd_of(n)

        @block.scalar
        def _(act):
            def split_hi(n, turns=0):
                act.wait_ge(raw_loaded[n % RAWS], turns * (16 * 12 // RAWS) + 16 * (n // RAWS + 1))
                if n >= SLOTS:
                    act.wait_ge(w_used, turns * 12 + (n - SLOTS + 1))
                w = width(n)
                nc.scalar.activation(w_hi[n % SLOTS][:, 0:w], w_raw[n % RAWS][:, 0:w], ACT.Copy).then_inc(hi_ready, 1)

            def square(n, src, junk):
                if n:
                    act.wait_ge(ss_ready, n)
                nc.scalar.activation(junk, src, ACT.Square, accum_out=ss[:, n:n + 1]).then_inc(ss_ready, 1)

            def xt_hi_of(n, bank, dst):
                act.wait_ge(xt_done, n + 1)
                nc.scalar.activation(dst, two(bank).rearrange("p (k n) -> p k n", n=P), ACT.Copy).then_inc(xt_hi, 1)

            act.dma_start(gain[:], norm_mix_g.broadcast_to([P, D])).then_inc(mix_gain_in, 16)
            with nc.allow_non_contiguous_dma(reason="small per-feature vectors"):
                act.dma_start(bg[:], b_gate[0].rearrange("(m p) -> p m", p=P)).then_inc(small_in, 16)
                act.dma_start(ps_scale[:], pool_scale[0].rearrange("(m p) -> p m", p=P)).then_inc(small_in, 16)
                act.dma_start(bf[:], b_forget.rearrange("a h -> h a")).then_inc(small_in, 16)
            act.wait_ge(consts_set, 5)
            nc.scalar.activation(ident_r[:], ident[:], ACT.Copy).then_inc(consts_r, 1)
            nc.scalar.activation(mask_r[:], mask[:], ACT.Copy).then_inc(consts_r, 1)

            for t in range(T + 2):
                if t < T:
                    act.wait_ge(x_loaded[t % 4], 16 * (t // 4 + 1))
                    square(t, x_in[t % 4][:], pooled[:])
                if t == 3:
                    split_hi(0)
                    split_hi(1)
                if t >= 2:
                    xt_hi_of(t - 2, 2 * ((t - 2) % 4), h_hi[:, :, tile_of(t - 2)])

            for k in range(C_U, C_V + 4):
                split_hi(k + 2)
                if C_U < k <= C_V:
                    g = k - 1 - C_U
                    act.wait_ge(w_used, k)
                    nc.scalar.activation(u_sb[:, g, PAD:], two(2 * g), ACT.Copy).then_inc(u_copied, 1)
                if k > C_V:
                    g = k - C_V - 1
                    act.wait_ge(d_ready, g + 1)
                    nc.scalar.activation(d_hi[:, g, :], pooled[:], ACT.Copy).then_inc(d_hi_ready, 1)
            split_hi(C_F + 2)
            act.wait_ge(w_used, C_F)
            for t in range(T):
                nc.scalar.activation(v_sb[:, t, :], ps[:, t, :], ACT.Copy).then_inc(v_copied, 1)
            act.wait_ge(d_ready, NG)
            nc.scalar.activation(d_hi[:, NG - 1, :], pooled[:], ACT.Copy).then_inc(d_hi_ready, 1)
            split_hi(C_PW + 2)
            for g in range(NG):
                act.wait_ge(mix_done if g < NG - 1 else w_used, g + 1 if g < NG - 1 else C_PW + 1)
                if g == 0:
                    act.wait_ge(small_in, 48)
                nc.scalar.activation(d_hi[:, g, :], two(2 + 2 * (g % 3)), ACT.Copy,
                                     scale=ps_scale[:, g:g + 1]).then_inc(mix_hi, 1)

            def sigmoid_gate(m, bias, dst):
                nc.scalar.activation(dst, two(2 * (m % 2)), ACT.Sigmoid, bias=bias).then_inc(gate_ready, 1)

            def store_za(m):
                act.wait_ge(y_gated, m + 1)
                act.dma_start(za_dram[m], za[m % 2][:]).then_inc(za_stored[m % 2], 16)

            for k in range(C_PG, C_QK + 1):
                split_hi(k + 2)
                j, r = divmod(k - 1 - C_PG, 3)
                if k == C_PG:
                    continue
                if r < 2:
                    m = 2 * j + r
                    act.wait_ge(w_used, k)
                    if m >= 2:
                        act.wait_ge(y_gated, m - 1)
                    sigmoid_gate(m, bg[:, m:m + 1], sg[m % 2][:])
                else:
                    store_za(2 * j)
                    store_za(2 * j + 1)
                if k == C_PG + 2:
                    act.wait_ge(f_step, 3)
                    nc.scalar.activation(f_exp[:], f_min[:], ACT.Exp).then_inc(f_exp_ready, 1)
                    act.wait_ge(f_step, 4)
                    nc.scalar.activation(f_log[:], f_u[:], ACT.Ln).then_inc(f_log_ready, 1)

            def qk_hi_of(g):
                p, r = divmod(g, 4)
                which, h = divmod(r, 2)
                bank = 4 + r if p == 0 else 7
                if h == 0:
                    act.wait_ge(qk_done, 2 * p + which + 1)
                else:
                    act.wait_ge(w_used, C_QK + 2 * p + which + 1)
                if g in (2, 3):
                    for i in range(2):
                        act.wait_ge(za_stored[i], 16 * (KD // 2))
                for a in range(2):
                    own, other = slice(a * DH, (a + 1) * DH), slice((1 - a) * DH, (2 - a) * DH)
                    if which == 0:
                        nc.scalar.activation(q1[p % 2][a][other, half_of(h)], ps[own, bank, :], ACT.Copy,
                                             scale=DH ** -0.5).then_inc(qk_hi, 1)
                    nc.scalar.activation((k1 if which else q1)[p % 2][a][own, half_of(h)], ps[own, bank, :], ACT.Copy,
                                         scale=1.0 if which else DH ** -0.5).then_inc(qk_hi, 1)

            split_hi(C_QK + 3)
            for g in range(4):
                qk_hi_of(g)

            def pv_copy(v):
                act.wait_ge(pv_done, v + 1)
                nc.scalar.activation(o_sb[:, v // T, tile_of(v % T)], ps[:, 6, 0:P], ACT.Copy).then_inc(pv_copied, 1)

            done = 0
            for u in range(PAIRS * T + 1):
                p, i = divmod(u, T)
                if u % 4 == 0 and u < PAIRS * T:
                    split_hi(C_QK + 2 + u // 4 + 2)
                if u >= 2:
                    pv_copy(u - 2)
                if u >= 1:
                    for g, (a, j0, n) in enumerate(groups_of((u - 1) % T)):
                        done += 1
                        if g < 2:
                            act.wait_ge(pt_done, done)
                            nc.scalar.activation(prob_t[:, a, j0 * P:(j0 + n) * P], ps[:, 4 + g % 2, 0:n * P],
                                                 ACT.Copy).then_inc(pt_act, 1)
                if u < PAIRS * T:
                    n = (i + 1) * P
                    for a in range(2):
                        act.wait_ge(sc_biased, 2 * u + a + 1)
                        nc.scalar.activation(prob[u % 2][:, a, 0:n], prob[u % 2][:, a, 0:n], ACT.Exp,
                                             bias=neg_max[:, u % 2, a:a + 1], scale=-1.0,
                                             accum_out=prob_sum[:, u % 2, a:a + 1]).then_inc(exp_ready, 1)
                if u < 3 * T and u % 2 == 1:
                    qk_hi_of(4 + u // 2)
                if 3 * T <= u < 4 * T and u % 2 == 1:
                    m, h = divmod(u // 2 - 3 * T // 2, 2)
                    if h == 0:
                        act.wait_ge(qk_done, 2 * PAIRS + m + 1)
                    else:
                        act.wait_ge(w_used, C_FG + m + 1)
                    nc.scalar.activation(sg_e[m][:, half_of(h)], ps[:, 7, :], ACT.Copy).then_inc(gate_copied, 1)
            pv_copy(PAIRS * T - 1)

            for k in range(C_FG + 2, C_WO + 1):
                split_hi(k + 2)
                j, r = divmod(k - 1 - C_FG, 3)
                if k == C_FG + 2:
                    act.wait_ge(pv_copied, PAIRS * T)
                    for p in range(PAIRS):
                        nc.scalar.activation(o_hi[:, p, :], o_sb[:, p, :], ACT.Copy).then_inc(o_hi_ready, 1)
                    act.wait_ge(gate_copied, 4)
                    for m in range(2):
                        nc.scalar.activation(sg_e[m][:], sg_e[m][:], ACT.Sigmoid, bias=bg[:, KD + m:KD + m + 1]).then_inc(gate_ready, 1)
                    continue
                if r < 2:
                    m = 2 * j + r
                    act.wait_ge(w_used, k)
                    if m >= 2:
                        act.wait_ge(z_lo_ready, m - 1)
                    sigmoid_gate(m, bg[:, KD + m:KD + m + 1], sg_e[m % 2][:])
                else:
                    for m in (2 * j, 2 * j + 1):
                        act.wait_ge(z_sum, m + 1)
                        nc.scalar.activation(z_hi[:, m, :], sg_e[m % 2][:], ACT.Copy).then_inc(z_hi_ready, 1)

            for k in range(C_WO + 1, C_XK):
                split_hi(k + 2)
                if k == C_WO + 1:
                    act.wait_ge(mem_loaded, 32)
                    act.wait_ge(z_lo_ready, KD)
                    for t in range(2):
                        square(N_MEM + t, mem_in[:, t, :], xn_m[:, t, :])
                if k == C_WO + 4:
                    for t in range(2):
                        xt_hi_of(N_MEM + t, 2 * t, mt_hi[:, :, tile_of(t)])

            def square_residual(t, n0, added, junk):
                act.wait_ge(xr_added, added + t + 1)
                square(n0 + t, xr[:, t, :], junk)

            for s in range(10):
                if s < 8:
                    split_hi(C_XK + s + 2)
                for t in {0: (0, 1, 2)}.get(s, (s + 2,)):
                    if t < T:
                        square_residual(t, N_CROSS, T, junk_x[:])
                if 1 <= s < 5:
                    act.wait_ge(w_used, C_XK + s)
                    nc.scalar.activation(xk_hi[:, s - 1, :], ps[:, s - 1, 0:MEM], ACT.Copy).then_inc(kv_hi, 1)
                if s == 8:
                    act.wait_ge(w_used, C_XQ)
                    for t in range(2):
                        nc.scalar.activation(xv_hi[:, t, :], ps[:, 4 + t, :], ACT.Copy).then_inc(kv_hi, 1)
                if s >= 2:
                    xt_hi_of(N_CROSS + s - 2, 6, hx_hi[:, :, tile_of(s - 2)])

            def xpt_hi_of(h, half):
                act.wait_ge(xpt_done, 2 * h + half + 1)
                nc.scalar.activation(xpt_hi[:], ps[:, 6:8, :], ACT.Copy).then_inc(xpt_hi_ready, 1)

            def xo_hi_of(h, half):
                act.wait_ge(xpv_done, 2 * h + half + 1)
                nc.scalar.activation(xo_hi[:, h, half_of(half)], ps[:, half, :], ACT.Copy).then_inc(xo_hi_ready, 1)

            for h in range(XH):
                split_hi(C_XQ + h + 2)
                act.wait_ge(w_used, C_XQ + h + 1)
                nc.scalar.activation(xq_hi[:], two(0), ACT.Copy).then_inc(xq_hi_ready, 1)
                for half in range(2):
                    if h:
                        xpt_hi_of(h - 1, half)
                    act.wait_ge(xs_nmax, 2 * h + half + 1)
                    for t in range(4 * half, 4 * half + 4):
                        nc.scalar.activation(xp[:, t, :], ps[:, 2 + t // 2, (t % 2) * MEM:(t % 2 + 1) * MEM], ACT.Exp,
                                             bias=x_nmax[:, h, t:t + 1], scale=XDH ** -0.5,
                                             accum_out=x_sum[:, h, t:t + 1]).then_inc(xs_exp, 1)
                    if h:
                        xo_hi_of(h - 1, half)
            for half in range(2):
                xpt_hi_of(XH - 1, half)
                xo_hi_of(XH - 1, half)
            split_hi(C_XO + 2)
            split_hi(C_XO + 3)
            split_hi(C_FF)
            split_hi(C_FF + 1)
            for t in range(T + 2):
                if t < T:
                    square_residual(t, N_FFN, 3 * T, junk_f[:])
                if t >= 2:
                    xt_hi_of(N_FFN + t - 2, 2 * ((t - 2) % 4), hf_hi[:, :, tile_of(t - 2)])

            def silu_of(b, j, used):
                act.wait_ge(w_used, used)
                if not (isinstance(b, int) and b == 0):
                    act.wait_ge(hid_ready, b * 2 + (j - 1))
                nc.scalar.activation(silu[j][:], two(4 * j), ACT.Silu).then_inc(silu_ready, 1)

            def hid_hi_of(b, par, j, used):
                act.wait_ge(hid_ready, b * 2 + (j + 1))
                if used is not None:
                    act.wait_ge(w_used, used)
                nc.scalar.activation(hid_hi[par][:, j, :], hid[j][:], ACT.Copy).then_inc(hid_hi_ready, 1)

            split_hi(C_FF + 2)
            split_hi(C_FF + 3)
            silu_of(0, 0, C_FF + 1)
            split_hi(C_FF + 4)
            hid_hi_of(0, 0, 0, None)
            split_hi(C_FF + 5)
            silu_of(0, 1, C_FF + 3)
            with act.Fori(0, (NB - 1) // 2) as i:
                for o in range(2):
                    n0 = base_of(1 + o)
                    b = i * 2 + (1 + o)
                    for r in range(6):
                        split_hi(n0 + r + 2, i)
                        if r == 0:
                            hid_hi_of(b - 1, o, 1, i * 12 + base_of(o))
                        if r == 1:
                            silu_of(b, 0, i * 12 + (n0 + 1))
                        if r == 2:
                            hid_hi_of(b, (1 + o) % 2, 0, i * 12 + n0)
                        if r == 3:
                            silu_of(b, 1, i * 12 + (n0 + 3))
            hid_hi_of(NB - 1, (NB - 1) % 2, 1, base_of(NB - 1))
            for t in range(T):
                square_residual(t, N_OUT, 4 * T + 16 * (NB - 1) + T, junk_f[:])

        @block.vector
        def _(dve):
            def split_lo(n, turns=0):
                dve.wait_ge(hi_ready, turns * 12 + (n + 1))
                w = width(n)
                nc.vector.tensor_tensor(w_lo[n % SLOTS][:, 0:w], w_raw[n % RAWS][:, 0:w],
                                        w_hi[n % SLOTS][:, 0:w].bitcast(FP32), ALU.subtract).then_inc(lo_ready, 1)

            def normalise(n, dst, src, gains, done):
                dve.wait_ge(rstd_ready, n + 1)
                dve.wait_ge(gain_in if gains else mix_gain_in, 16 * max(gains, 1))
                nc.vector.scalar_tensor_tensor(out=dst, in0=src, scalar=rstd[:, n:n + 1], in1=gain[:],
                                               op0=ALU.mult, op1=ALU.mult).then_inc(done, 1)

            def minus_hi(out, a, hi, done):
                nc.vector.tensor_tensor(out, a, hi.bitcast(FP32), ALU.subtract).then_inc(done, 1)

            def xt_lo_of(n, bank, hi, lo):
                dve.wait_ge(xt_hi, n + 1)
                minus_hi(lo, two(bank).rearrange("p (k n) -> p k n", n=P), hi, xt_lo)

            nc.vector.memset(u_sb[:, :, 0:PAD], 0.0).then_inc(pads_zero, 1)
            for w in win:
                nc.vector.memset(w[:, 0:PAD], 0.0).then_inc(pads_zero, 1)
            dve.wait_ge(consts_set, 6)
            nc.vector.tensor_copy(count[:], count_i[:]).then_inc(pads_zero, 1)
            dve.wait_ge(pads_zero, 4)
            nc.vector.reciprocal(inv_count[:], count[:]).then_inc(pads_zero, 1)

            for t in range(T + 2):
                if t < T:
                    if t >= 2:
                        dve.wait_ge(xt_done, t - 1)
                    normalise(t, xn_a[t % 2][:], x_in[t % 4][:], 0, xn_ready)
                if t == 3:
                    split_lo(0)
                    split_lo(1)
                if t >= 2:
                    xt_lo_of(t - 2, 2 * ((t - 2) % 4), h_hi[:, :, tile_of(t - 2)], h_lo[:, :, tile_of(t - 2)])

            steps = [0]

            def step(ins):
                steps[0] += 1
                ins.then_inc(win_step, 1)
                dve.wait_ge(win_step, steps[0])

            def pool_group(g):
                w = WINDOWS[g]
                u = u_sb[:, g, :]
                src = u
                for e in range(g + 1):
                    dst = win[e % 2]
                    step(nc.vector.tensor_tensor(dst[:, PAD:], src[:, PAD:], src[:, PAD - (1 << e):PAD + S - (1 << e)], ALU.add))
                    src = dst[:, :]
                step(nc.vector.scalar_tensor_tensor(out=pooled[:], in0=src[:, PAD:], scalar=1.0 / w, in1=u[:, PAD:],
                                                    op0=ALU.mult, op1=ALU.subtract))
                step(nc.vector.tensor_tensor(pooled[:, 0:w], src[:, PAD:PAD + w], inv_count[:, 0:w], ALU.mult))
                nc.vector.tensor_tensor(pooled[:, 0:w], pooled[:, 0:w], u[:, PAD:PAD + w], ALU.subtract).then_inc(d_ready, 1)

            def pooled_lo(g):
                dve.wait_ge(d_hi_ready, g + 1)
                minus_hi(d_lo[:, g, :], pooled[:], d_hi[:, g, :], d_lo_ready)
                dve.wait_ge(d_lo_ready, g + 1)

            dve.wait_ge(pads_zero, 5)
            for k in range(C_U, C_V + 4):
                split_lo(k + 2)
                if k >= C_V:
                    g = k - C_V
                    if g:
                        pooled_lo(g - 1)
                    dve.wait_ge(u_copied, g + 1)
                    pool_group(g)
            split_lo(C_F + 2)
            pooled_lo(NG - 1)
            split_lo(C_PW + 2)

            fsteps = [0]

            def fstep(ins):
                fsteps[0] += 1
                ins.then_inc(f_step, 1)
                dve.wait_ge(f_step, fsteps[0])

            dve.wait_ge(w_used, C_F + 1)
            dve.wait_ge(small_in, 48)
            fstep(nc.vector.tensor_scalar(f_neg[:], two(0)[0:HEADS, :], bf[:, 0:1], -1.0, ALU.add, ALU.mult))
            fstep(nc.vector.tensor_scalar(f_h[:], two(0)[0:HEADS, :], bf[:, 0:1], None, ALU.add))

            def mixed_lo(g):
                dve.wait_ge(mix_hi, g + 1)
                nc.vector.scalar_tensor_tensor(out=d_lo[:, g, :], in0=two(2 + 2 * (g % 3)), scalar=ps_scale[:, g:g + 1],
                                               in1=d_hi[:, g, :].bitcast(FP32), op0=ALU.mult, op1=ALU.subtract).then_inc(mix_lo, 1)

            for g in range(NG):
                mixed_lo(g)

            def gated(m, c, dst, gate, chunk, gates):
                if c == 0:
                    dve.wait_ge(y_done, gates // 2 + m // 2 + 1)
                else:
                    dve.wait_ge(w_used, chunk + 1)
                dve.wait_ge(gate_ready, gates + m + 1)
                nc.vector.tensor_tensor(dst, two(4 + 2 * c), gate, ALU.mult).then_inc(y_gated, 1)

            for k in range(C_PG, C_QK + 1):
                split_lo(k + 2)
                j, r = divmod(k - 1 - C_PG, 3)
                if k > C_PG and r == 2:
                    for c in range(2):
                        m = 2 * j + c
                        if m >= 2:
                            dve.wait_ge(za_stored[c], 16 * (m // 2))
                        gated(m, c, za[c][:], sg[c][:], k - 1, 0)
                if k == C_PG + 2:
                    fstep(nc.vector.tensor_tensor(f_min[:], f_h[:], f_neg[:], ALU.min))
                    dve.wait_ge(f_exp_ready, 1)
                    fstep(nc.vector.tensor_scalar(f_u[:], f_exp[:], 1.0, None, ALU.add))
                if k == C_PG + 4:
                    dve.wait_ge(f_log_ready, 1)
                    fstep(nc.vector.tensor_scalar(f_min[:], f_u[:], -1.0, 1e-30, ALU.add, ALU.max))
                    fstep(nc.vector.reciprocal(f_one[:], f_min[:]))
                    fstep(nc.vector.tensor_tensor(f_one[:], f_one[:], f_exp[:], ALU.mult))
                    fstep(nc.vector.tensor_tensor(f_one[:], f_one[:], f_log[:], ALU.mult))
                    fstep(nc.vector.scalar_tensor_tensor(out=f_log[:], in0=f_min[:], scalar=2e-30, in1=f_exp[:],
                                                         op0=ALU.is_lt, op1=ALU.mult))
                    fstep(nc.vector.tensor_tensor(f_one[:], f_one[:], f_log[:], ALU.add))
                if k == C_PG + 5:
                    fstep(nc.vector.scalar_tensor_tensor(out=f_one[:], in0=f_h[:], scalar=0.0, in1=f_one[:],
                                                         op0=ALU.min, op1=ALU.subtract))
                    fstep(nc.vector.memset(f_min[:], 1.0))
                    nc.vector.tensor_tensor_scan(out=f_u[:], data0=f_min[:], data1=f_one[:], initial=0.0,
                                                 op0=ALU.mult, op1=ALU.subtract).then_inc(negc_ready, 1)
            split_lo(C_QK + 3)

            def qk_lo_of(g):
                p, r = divmod(g, 4)
                which, h = divmod(r, 2)
                bank = 4 + r if p == 0 else 7
                dve.wait_ge(qk_hi, 12 * p + (4, 8, 10, 12)[r])
                for a in range(2):
                    own, other = slice(a * DH, (a + 1) * DH), slice((1 - a) * DH, (2 - a) * DH)
                    if which:
                        minus_hi(k1[p % 2][a][other, half_of(h)], ps[own, bank, :], k1[p % 2][a][own, half_of(h)], qk_lo)
                    else:
                        nc.vector.scalar_tensor_tensor(out=q2[p % 2][own, half_of(h)], in0=ps[own, bank, :], scalar=DH ** -0.5,
                                                       in1=q1[p % 2][a][own, half_of(h)].bitcast(FP32),
                                                       op0=ALU.mult, op1=ALU.subtract).then_inc(qk_lo, 1)

            for g in range(4):
                qk_lo_of(g)

            done = 0
            for u in range(PAIRS * T + 1):
                p, i = divmod(u, T)
                b, n = u % 2, (i + 1) * P
                if u % 4 == 0 and u < PAIRS * T:
                    split_lo(C_QK + 2 + u // 4 + 2)
                for a in range(2 if u < PAIRS * T else 0):
                    h = 2 * p + a
                    dve.wait_ge(sc_done, 2 * u + a + 1)
                    dve.wait_ge(negc_loaded[h % 3], 16 * (h // 3 + 1))
                    if u >= 2:
                        dve.wait_ge(pt_done, groups_before(u - 1))
                    nc.vector.tensor_tensor_reduce(out=prob[b][:, a, 0:n], in0=two(2 * a)[:, 0:n], in1=negc[h % 3][:, 0:n],
                                                   scale=-1.0, scalar=HIGHEST, op0=ALU.add, op1=ALU.min,
                                                   accum_out=neg_max[:, b, a:a + 1]).then_inc(sc_biased, 1)
                if u >= 1:
                    for g, (a, j0, m) in enumerate(groups_of((u - 1) % T)):
                        done += 1
                        if g >= 2:
                            dve.wait_ge(pt_done, done)
                            nc.vector.tensor_copy(prob_t[:, a, j0 * P:(j0 + m) * P], ps[:, 4 + g % 2, 0:m * P]).then_inc(pt_dve, 1)
                for a in range(2 if u < PAIRS * T else 0):
                    dve.wait_ge(exp_ready, 2 * u + a + 1)
                    nc.vector.reciprocal(prob_inv[:, b, a:a + 1], prob_sum[:, b, a:a + 1]).then_inc(inv_ready, 1)
                    dve.wait_ge(inv_ready, 2 * u + a + 1)
                    nc.vector.tensor_scalar(prob[b][:, a, 0:n], prob[b][:, a, 0:n], prob_inv[:, b, a:a + 1], None,
                                            ALU.mult).then_inc(prob_ready, 1)
                if u < 3 * T and u % 2 == 1:
                    qk_lo_of(4 + u // 2)

            for k in range(C_FG + 2, C_WO + 1):
                split_lo(k + 2)
                j, r = divmod(k - 1 - C_FG, 3)
                if k == C_FG + 2:
                    for p in range(PAIRS):
                        dve.wait_ge(o_hi_ready, p + 1)
                        minus_hi(o_lo[:, p, :], o_sb[:, p, :], o_hi[:, p, :], o_lo_ready)
                elif r == 2:
                    for c in range(2):
                        gated(2 * j + c, c, sg_e[c][:], sg_e[c][:], k - 1, KD)
                    for c in range(2):
                        m = 2 * j + c
                        dve.wait_ge(y_gated, KD + m + 1)
                        dve.wait_ge(za_loaded, 16 * (m + 1))
                        nc.vector.tensor_tensor(sg_e[c][:], sg_e[c][:], za_e[:], ALU.add).then_inc(z_sum, 1)
                    for c in range(2):
                        m = 2 * j + c
                        dve.wait_ge(z_hi_ready, m + 1)
                        minus_hi(z_lo[:, m, :], sg_e[c][:], z_hi[:, m, :], z_lo_ready)

            def add(t, n, earlier, outs, used, turns=0):
                if t < T - 1:
                    dve.wait_ge(bank_out, turns * 28 + (outs + t + 1))
                else:
                    dve.wait_ge(w_used, turns * 12 + used)
                if earlier >= 2 * T:
                    dve.wait_ge(xr_added, turns * 32 + (earlier + t - 2 * T + 1))
                nc.vector.tensor_tensor(xr[:, t, half_of(n)], ps[:, t, :], xr[:, t, half_of(n)], ALU.add).then_inc(xr_added, 1)

            for k in range(C_WO + 1, C_XK):
                split_lo(k + 2)
                if k == C_WO + 1:
                    for t in range(2):
                        normalise(N_MEM + t, xn_m[:, t, :], mem_in[:, t, :], 1, xn_ready)
                if k == C_WO + 3:
                    dve.wait_ge(xr_loaded, 16 * T)
                    for t in range(T):
                        add(t, 0, 0, 0, C_WO + 4)
                if k == C_WO + 4:
                    for t in range(2):
                        xt_lo_of(N_MEM + t, 2 * t, mt_hi[:, :, tile_of(t)], mt_lo[:, :, tile_of(t)])
                if k == C_WO + 7:
                    for t in range(T):
                        add(t, 1, T, T - 1, C_WO + 8)

            for s in range(10):
                if s < 8:
                    split_lo(C_XK + s + 2)
                    if s < 2:
                        dve.wait_ge(xt_done, N_CROSS)
                    else:
                        dve.wait_ge(xt_done, N_CROSS + s - 1)
                    normalise(N_CROSS + s, xn_x[s % 2][:], xr[:, s, :], 2, xn_ready)
                if 1 <= s < 5:
                    dve.wait_ge(kv_hi, s)
                    minus_hi(xk_lo[:, s - 1, :], ps[:, s - 1, 0:MEM], xk_hi[:, s - 1, :], kv_lo)
                if s == 8:
                    for t in range(2):
                        dve.wait_ge(kv_hi, XH + t + 1)
                        minus_hi(xv_lo[:, t, :], ps[:, 4 + t, :], xv_hi[:, t, :], kv_lo)
                if s >= 2:
                    xt_lo_of(N_CROSS + s - 2, 6, hx_hi[:, :, tile_of(s - 2)], hx_lo[:, :, tile_of(s - 2)])

            def xpt_lo_of(h, half):
                dve.wait_ge(xpt_hi_ready, 2 * h + half + 1)
                minus_hi(xpt_lo[:], ps[:, 6:8, :], xpt_hi[:], xpt_lo_ready)

            def xo_lo_of(h, half):
                dve.wait_ge(xo_hi_ready, 2 * h + half + 1)
                minus_hi(xo_lo[:, h, half_of(half)], ps[:, half, :], xo_hi[:, h, half_of(half)], xo_lo_ready)

            for h in range(XH):
                split_lo(C_XQ + h + 2)
                dve.wait_ge(xq_hi_ready, h + 1)
                minus_hi(xq_lo[:], two(0), xq_hi[:], xq_lo_ready)
                for half in range(2):
                    if h:
                        xpt_lo_of(h - 1, half)
                    g = 2 * h + half
                    dve.wait_ge(xs_done, g + 1)
                    t4 = slice(4 * half, 4 * half + 4)
                    for b in range(2):
                        t0 = 4 * half + 2 * b
                        nc.vector.tensor_reduce(x_max[:, h, t0:t0 + 2], ps[:, 2 + t0 // 2, :].rearrange("p (q m) -> p q m", m=MEM),
                                                AX, ALU.max).then_inc(xs_max, 1)
                    dve.wait_ge(xs_max, 2 * g + 2)
                    nc.vector.tensor_scalar(x_nmax[:, h, t4], x_max[:, h, t4], -XDH ** -0.5, None, ALU.mult).then_inc(xs_nmax, 1)
                    dve.wait_ge(xs_exp, 4 * g + 4)
                    nc.vector.reciprocal(x_inv[:, h, t4], x_sum[:, h, t4]).then_inc(xs_inv, 1)
                    dve.wait_ge(xs_inv, g + 1)
                    for t in range(4 * half, 4 * half + 4):
                        nc.vector.tensor_scalar(xp[:, t, :], xp[:, t, :], x_inv[:, h, t:t + 1], None, ALU.mult).then_inc(xp_ready, 1)
                    if h:
                        xo_lo_of(h - 1, half)
            for half in range(2):
                xpt_lo_of(XH - 1, half)
                xo_lo_of(XH - 1, half)
            split_lo(C_XO + 2)
            split_lo(C_XO + 3)
            for t in range(T):
                add(t, 0, 2 * T, 2 * (T - 1), C_XO + 2)
            split_lo(C_FF)
            split_lo(C_FF + 1)
            for t in range(T + 4):
                if t < T:
                    add(t, 1, 3 * T, 3 * (T - 1), C_XO + 4)
                if 2 <= t < T + 2:
                    n = t - 2
                    dve.wait_ge(xt_done, N_FFN + n - 1)
                    normalise(N_FFN + n, xn_f[n % 2][:], xr[:, n, :], 3, xn_ready)
                if t >= 4:
                    n = t - 4
                    xt_lo_of(N_FFN + n, 2 * (n % 4), hf_hi[:, :, tile_of(n)], hf_lo[:, :, tile_of(n)])

            def hid_of(b, j, used):
                dve.wait_ge(w_used, used)
                dve.wait_ge(silu_ready, b * 2 + (j + 1))
                if not (isinstance(b, int) and b == 0):
                    dve.wait_ge(hid_lo_ready, b * 2 + (j - 1))
                nc.vector.tensor_tensor(hid[j][:], two(4 * j + 2), silu[j][:], ALU.mult).then_inc(hid_ready, 1)

            split_lo(C_FF + 2)
            split_lo(C_FF + 3)
            split_lo(C_FF + 4)
            hid_of(0, 0, C_FF + 2)
            split_lo(C_FF + 5)
            hid_of(0, 1, C_FF + 4)
            with dve.Fori(0, (NB - 1) // 2) as i:
                for o in range(2):
                    n0 = base_of(1 + o)
                    for r in range(6):
                        split_lo(n0 + r + 2, i)
                        if r in (2, 4):
                            hid_of(i * 2 + (1 + o), r // 2 - 1, i * 12 + (n0 + r))
                        if r >= 4:
                            for t in range(T):
                                add(t, r - 4, 4 * T + 2 * T * o + T * (r - 4), 4 * (T - 1) + 2 * (T - 1) * o + (T - 1) * (r - 4),
                                    n0 + r + 1, i)
            blocks = NB - 1
            for n in range(2):
                for t in range(T + 2 * n):
                    if t < T:
                        add(t, n, 4 * T + 2 * T * blocks + T * n, 4 * (T - 1) + 2 * (T - 1) * blocks + (T - 1) * n, N_CHUNKS - 1 + n)
                    if n == 1 and t >= 2:
                        m = t - 2
                        if m >= 3:
                            dve.wait_ge(out_stored[m % 3], 16 * (m // 3))
                        normalise(N_OUT + m, y_out[m % 3][:], xr[:, m, :], 4, out_ready)

        @block.tensor
        def _(pe):
            def mm3(dst, w_h, w_l, x_h, x_l, start, stop):
                nc.tensor.matmul(dst, w_h, x_l, start=start, stop=False)
                nc.tensor.matmul(dst, w_h, x_h, start=False, stop=False)
                return nc.tensor.matmul(dst, w_l, x_h, start=False, stop=stop)

            def transpose_tile(src, bank, done):
                for k in range(KD):
                    last = nc.tensor.transpose(two(bank)[:, tile_of(k)], src[:, tile_of(k)], ident[:])
                last.then_inc(done, 1)

            def project_half(n, h, dst, x_hi, x_lo, tiles=KD, c=0, stride=P, by_tile=False):
                wh, wl = w_hi[n % SLOTS], w_lo[n % SLOTS]
                for k in range(tiles):
                    w = slice(k * stride + c * P, k * stride + (c + 1) * P)
                    if by_tile:
                        pe.wait_ge(o_lo_ready, k + 1)
                    last = mm3(dst, wh[:, w], wl[:, w], x_hi[:, k, half_of(h)], x_lo[:, k, half_of(h)],
                               k == 0, k == tiles - 1)
                return last

            def project(n, bank, x_hi, x_lo, turns=0):
                pe.wait_ge(lo_ready, turns * 12 + (n + 1))
                for h in range(2):
                    last = project_half(n, h, ps[:, bank + h, :], x_hi, x_lo)
                last.then_inc(w_used, 1)

            def project_pair(n, x_hi, x_lo, by_tile=False):
                pe.wait_ge(lo_ready, n + 1)
                for c in range(2):
                    for h in range(2):
                        last = project_half(n, h, ps[:, 4 + 2 * c + h, :], x_hi, x_lo, 4, c, 2 * P, by_tile and c == h == 0)
                    last.then_inc(y_done if c == 0 else w_used, 1)

            def tokens_by(n, k0, x_hi, x_lo, first, last_chunk, bank_free, turns=0, banks=True):
                pe.wait_ge(lo_ready, turns * 12 + (n + 1))
                wh, wl = w_hi[n % SLOTS], w_lo[n % SLOTS]
                for t in range(T):
                    if first:
                        bank_free(t)
                    for r in range(2):
                        last = mm3(ps[:, t, :], x_hi[:, k0 + r, tile_of(t)], x_lo[:, k0 + r, tile_of(t)],
                                   wh[:, half_of(r)], wl[:, half_of(r)], first and r == 0, last_chunk and r == 1)
                    if t == T - 1:
                        last.then_inc(w_used, 1)
                    elif last_chunk and banks:
                        last.then_inc(bank_out, 1)

            pe.wait_ge(consts_set, 5)
            for t in range(T):
                pe.wait_ge(xn_ready, t + 1)
                if t >= 4:
                    pe.wait_ge(xt_lo, t - 3)
                transpose_tile(xn_a[t % 2], 2 * (t % 4), xt_done)
            pe.wait_ge(xt_lo, T)
            for g in range(NG):
                project(C_U + g, 2 * g, h_hi, h_lo)
            for r in range(4):
                tokens_by(C_V + r, 2 * r, h_hi, h_lo, r == 0, r == 3, lambda t: pe.wait_ge(u_copied, t // 2 + 1), banks=False)
            pe.wait_ge(v_copied, 2)
            project(C_F, 0, h_hi, h_lo)
            pe.wait_ge(lo_ready, C_PW + 1)
            pe.wait_ge(v_copied, T)
            for g in range(NG):
                if g == NG - 1:
                    pe.wait_ge(mix_lo, 1)
                pe.wait_ge(d_lo_ready, g + 1)
                for h in range(2):
                    last = mm3(ps[:, 2 + 2 * (g % 3) + h, :], w_hi[C_PW % SLOTS][:, tile_of(g)], w_lo[C_PW % SLOTS][:, tile_of(g)],
                               d_hi[:, g, half_of(h)], d_lo[:, g, half_of(h)], True, True)
                last.then_inc(mix_done if g < NG - 1 else w_used, 1)
            pe.wait_ge(mix_lo, NG)
            pe.wait_ge(f_step, 2)
            for j in range(4):
                for r in range(2):
                    if j:
                        pe.wait_ge(gate_ready, 2 * j + r - 1)
                    project(C_PG + 3 * j + r, 2 * r, h_hi, h_lo)
                if j:
                    pe.wait_ge(y_gated, 2 * j)
                project_pair(C_PG + 3 * j + 2, d_hi, d_lo)

            def bank7_group(n, h, bank, half):
                for k in range(KD) if half is None else range(4 * half, 4 * half + 4):
                    last = mm3(ps[:, bank, :], w_hi[n % SLOTS][:, tile_of(k)], w_lo[n % SLOTS][:, tile_of(k)],
                               h_hi[:, k, half_of(h)], h_lo[:, k, half_of(h)], k == 0, k == KD - 1)
                if half != 0:
                    last.then_inc(w_used if h else qk_done, 1)

            def qk_group(g, half=None):
                p, r = divmod(g, 4)
                which, h = divmod(r, 2)
                n = C_QK + 2 * p + which
                if half != 1:
                    pe.wait_ge(lo_ready, n + 1)
                    if p:
                        pe.wait_ge(qk_lo, 2 * g)
                bank7_group(n, h, 4 + r if p == 0 else 7, half)

            def gate_group(g, half):
                m, h = divmod(g, 2)
                if half == 0:
                    pe.wait_ge(lo_ready, C_FG + m + 1)
                    if g:
                        pe.wait_ge(gate_copied, g)
                    else:
                        pe.wait_ge(qk_lo, 8 * PAIRS)
                bank7_group(C_FG + m, h, 7, half)

            pe.wait_ge(y_gated, KD)
            pe.wait_ge(gate_ready, KD)
            for g in range(4):
                qk_group(g)

            def beside(u, part):
                if u < 3 * T:
                    qk_group(4 + u // 2, u % 2) if part else None
                elif u < 4 * T:
                    gate_group(u // 2 - 3 * T // 2, u % 2) if part else None

            def transposed(v, groups):
                for g, (a, j0, n) in groups:
                    if g >= 2:
                        pe.wait_ge(pt_act, 2 * v + g - 1)
                    for j in range(j0, j0 + n):
                        last = nc.tensor.transpose(ps[:, 4 + g % 2, tile_of(j - j0)], prob[v % 2][:, a, tile_of(j)], ident[:])
                    last.then_inc(pt_done, 1)

            pe.wait_ge(consts_r, 2)
            for u in range(PAIRS * T + 1):
                p, i = divmod(u, T)
                if u < PAIRS * T:
                    pe.wait_ge(qk_lo, 8 * p + 8)
                    for a in range(2):
                        if u:
                            pe.wait_ge(sc_biased, 2 * (u - 1) + a + 1)
                        own = slice(a * DH, (a + 1) * DH)
                        q1a, k1a, q2a = q1[p % 2][a], k1[p % 2][a], q2[p % 2]
                        for c in range(0, i + 1, 4):
                            n = min(4, i + 1 - c)
                            keys = slice(c * P, (c + n) * P)
                            dst = ps[:, 2 * a + c // 4, 0:n * P]
                            diagonal = c + n == i + 1
                            nc.tensor.matmul(dst, q1a[:, tile_of(i)], k1a[:, keys], start=True, stop=False)
                            last = nc.tensor.matmul(dst, q2a[own, tile_of(i)], k1a[own, keys], start=False, stop=not diagonal)
                            if diagonal:
                                last = nc.tensor.matmul(dst[:, (n - 1) * P:], ident_r[:], mask_r[:], start=False, stop=True)
                        last.then_inc(sc_done, 1)
                v = u - 1
                if u:
                    groups = list(enumerate(groups_of(v % T)))
                    pe.wait_ge(prob_ready, 2 * u)
                    transposed(v, groups[:2])
                beside(u, 1)
                if u:
                    transposed(v, groups[2:])
                    pe.wait_ge(pt_act, 2 * u)
                    if v >= 4:
                        pe.wait_ge(pt_dve, groups_before(u) - 2 * u)
                    if v:
                        pe.wait_ge(pv_copied, v)
                    for j in range(v % T + 1):
                        for a in range(2):
                            hc = (2 * (v // T) + a) * DH
                            last = nc.tensor.matmul(ps[a * DH:(a + 1) * DH, 6, 0:P], v_sb[:, j, hc:hc + DH],
                                                    prob_t[:, a, tile_of(j)], start=j == 0, stop=j == v % T)
                    last.then_inc(pv_done, 1)

            for j in range(4):
                for r in range(2):
                    if j == 0:
                        continue
                    if j > 1:
                        pe.wait_ge(gate_ready, KD + 2 * j + r - 1)
                    project(C_FG + 3 * j + r, 2 * r, h_hi, h_lo)
                if j:
                    pe.wait_ge(y_gated, KD + 2 * j)
                else:
                    pe.wait_ge(pv_copied, PAIRS * T)
                    pe.wait_ge(gate_copied, 4)
                project_pair(C_FG + 3 * j + 2, o_hi, o_lo, j == 0)

            pe.wait_ge(gate_ready, 2 * KD)
            for r in range(4):
                pe.wait_ge(z_lo_ready, 2 * r + 2)
                tokens_by(C_WO + r, 2 * r, z_hi, z_lo, r == 0, r == 3,
                          lambda t: pe.wait_ge(y_gated, 2 * KD) if t == 4 else None)
            for t in range(2):
                pe.wait_ge(xn_ready, N_MEM + t + 1)
                pe.wait_ge(xr_added, 2 * t + 2)
                transpose_tile(xn_m[:, t, :], 2 * t, xt_done)

            def w_out_bank(t):
                pe.wait_ge(xr_added, t + 1)
                if t in (0, 2):
                    pe.wait_ge(xt_lo, N_MEM + t // 2 + 1)

            for r in range(4):
                tokens_by(C_WO + 4 + r, 2 * r, z_hi, z_lo, r == 0, r == 3, w_out_bank)

            def cross_tile(t):
                pe.wait_ge(xn_ready, N_CROSS + t + 1)
                pe.wait_ge(xr_added, 2 * T)
                if t:
                    pe.wait_ge(xt_lo, N_CROSS + t)
                transpose_tile(xn_x[t % 2], 6, xt_done)

            for s in range(8):
                n = C_XK + s
                pe.wait_ge(lo_ready, n + 1)
                if s < XH:
                    pe.wait_ge(xr_added, T + s + 1)
                    for k in range(KD):
                        last = mm3(ps[:, s, 0:MEM], w_hi[n % SLOTS][:, tile_of(k)], w_lo[n % SLOTS][:, tile_of(k)],
                                   mt_hi[:, k, :], mt_lo[:, k, :], k == 0, k == KD - 1)
                else:
                    if s == XH:
                        pe.wait_ge(xr_added, 2 * T)
                    for t in range(2):
                        for r in range(2):
                            k = 2 * (s - XH) + r
                            last = mm3(ps[:, 4 + t, :], mt_hi[:, k, tile_of(t)], mt_lo[:, k, tile_of(t)],
                                       w_hi[n % SLOTS][:, half_of(r)], w_lo[n % SLOTS][:, half_of(r)], k == 0, k == KD - 1)
                last.then_inc(w_used, 1)
                if s >= 1:
                    cross_tile(s - 1)
            cross_tile(T - 1)

            def xpt(h, half):
                pe.wait_ge(xp_ready, 8 * h + 4 * half + 4)
                if h or half:
                    pe.wait_ge(xpt_lo_ready, 2 * h + half)
                for m in range(2):
                    for t in range(4):
                        last = nc.tensor.transpose(ps[:, 6 + m, tile_of(t)], xp[:, 4 * half + t, tile_of(m)], ident[:])
                last.then_inc(xpt_done, 1)

            def xpv(h, half):
                pe.wait_ge(xpt_lo_ready, 2 * h + half + 1)
                for m in range(2):
                    last = mm3(ps[:, half, :], xv_hi[:, m, tile_of(h)], xv_lo[:, m, tile_of(h)],
                               xpt_hi[:, m, :], xpt_lo[:, m, :], m == 0, m == 1)
                last.then_inc(xpv_done, 1)

            pe.wait_ge(xt_lo, N_FFN)
            pe.wait_ge(kv_lo, XH + 2)
            for h in range(XH):
                if h >= 2:
                    pe.wait_ge(xo_lo_ready, 2 * (h - 1))
                project(C_XQ + h, 0, hx_hi, hx_lo)
                for half in range(2):
                    if h:
                        xpt(h - 1, half)
                    if half == 0:
                        pe.wait_ge(xq_lo_ready, h + 1)
                    if h:
                        pe.wait_ge(xs_exp, 8 * (h - 1) + 4 * half + 4)
                    for t in range(4 * half, 4 * half + 4):
                        last = mm3(ps[:, 2 + t // 2, (t % 2) * MEM:(t % 2 + 1) * MEM], xq_hi[:, tile_of(t)], xq_lo[:, tile_of(t)],
                                   xk_hi[:, h, :], xk_lo[:, h, :], True, True)
                    last.then_inc(xs_done, 1)
                    if h:
                        xpv(h - 1, half)
            for half in range(2):
                xpt(XH - 1, half)
                xpv(XH - 1, half)

            pe.wait_ge(xo_lo_ready, 2 * XH)
            for n in range(2):
                for r in range(2):
                    tokens_by(C_XO + 2 * n + r, 2 * r, xo_hi, xo_lo, r == 0, r == 1,
                              (lambda t: pe.wait_ge(xr_added, 2 * T + t + 1)) if n else (lambda t: None))
            for t in range(T):
                pe.wait_ge(xn_ready, N_FFN + t + 1)
                pe.wait_ge(xr_added, 3 * T + 2 * (t % 4) + 2)
                if t >= 4:
                    pe.wait_ge(xt_lo, N_FFN + t - 3)
                transpose_tile(xn_f[t % 2], 2 * (t % 4), xt_done)

            pe.wait_ge(xt_lo, N_OUT)
            for r in range(4):
                project(C_FF + r, 2 * r, hf_hi, hf_lo)

            def ffn_out(b, par, n0, turns, last_block=False):
                pe.wait_ge(hid_lo_ready, turns * 4 + 2 * (b + 1))
                for n in range(2):
                    def bank_free(t):
                        if n:
                            pe.wait_ge(xr_added, turns * 32 + (4 * T + 2 * T * b + t + 1))
                        elif not last_block and t % 2 == 0:
                            pe.wait_ge(hid_ready if t % 4 else silu_ready, turns * 4 + (2 * (b + 1) + t // 4 + 1))
                        elif last_block:
                            pe.wait_ge(xr_added, 4 * T + 2 * T * b - T + t + 1)
                    tokens_by(n0 + n, 0, hid_hi[par], hid_lo[par], True, True, bank_free, turns)

            with pe.Fori(0, (NB - 1) // 2) as i:
                for o in range(2):
                    n0 = base_of(1 + o)
                    for r in range(4):
                        pe.wait_ge(xr_added, i * 32 + (4 * T + 2 * T * (o - 1) + T + 2 * r + 2))
                        pe.wait_ge(hid_ready if r % 2 else silu_ready, i * 4 + (2 * o + r // 2 + 1))
                        project(n0 + r, 2 * r, hf_hi, hf_lo, i)
                    ffn_out(o, o, n0 + 4, i)
            ffn_out(NB - 1, (NB - 1) % 2, N_CHUNKS - 2, 0, True)


def groups_of(i):
    return [(a, j0, min(4, i + 1 - j0)) for a in range(2) for j0 in range(0, i + 1, 4)]


def groups_before(u):
    return sum(len(groups_of(v % T)) for v in range(u))


_INS = ["x", "mem", "norm_mix_g", "w_in", "b_forget", "b_gate", "pool_w", "pool_scale", "w_pool_out", "w_fox_out",
        "w_out", "norm_x_g", "norm_mem_g", "w_xq", "w_xkv", "w_xo", "norm_ffn_g", "w_ffn_in", "w_ffn_out", "norm_final_g"]


def kernel(**inputs):
    import numpy as np
    import concourse.bacc as bacc
    from concourse.bass_utils import run_bass_kernel_spmd

    nc = bacc.Bacc("TRN2", target_bir_lowering=False, num_devices=1)
    arrays, args = {}, []
    for name in _INS:
        a = np.ascontiguousarray(inputs[name])
        arrays[f"in_{name}"] = a
        args.append(nc.dram_tensor(f"in_{name}", a.shape, mybir.dt.from_np(a.dtype), kind="ExternalInput").ap())
    args.append(nc.dram_tensor("out_x", (1, S, D), FP32, kind="ExternalOutput").ap())
    build(nc, *args)
    return run_bass_kernel_spmd(nc, [arrays], core_ids=[0]).results[0]["out_x"]
```

```python
from contextlib import ExitStack

import concourse.bass as bass
from concourse import mybir

FP32 = mybir.dt.float32
F32R = mybir.dt.float32r
ALU = mybir.AluOpType
ACT = mybir.ActivationFunctionType
AX = mybir.AxisListType.X

P = 128
S = 1024
D = 1024
T = S // P
KD = D // P
HALF = 512
EPS = 1e-6
WINDOWS = (2, 4, 8, 16)
NG = len(WINDOWS)
PAD = 16
POOL_W = D // 2
HEADS, DH = 8, 64
PAIRS = HEADS // 2
FOX_W = HEADS * DH
MEM = 256
XH, XDH = 4, 128
XW = XH * XDH
DFF = ((8 * D // 3 + 255) // 256) * 256
NB = DFF // (2 * P)
MASKED = -1e30
HIGHEST = 3e38
RAWS, SLOTS = 2, 3
F_LO = 32
POOL_SPLITS = (0,2,4,6,)
XNS = 4

COL_Q = POOL_W
COL_K = COL_Q + FOX_W
COL_V = COL_K + FOX_W
COL_F = COL_V + FOX_W
COL_G = COL_F + HEADS

C_U = 0
C_F = C_U + NG
C_V = C_F + 1
C_G0 = C_V + 4
C_PW = C_G0 + 1
C_PG = C_PW
C_QK = C_PG + 12
C_FG = C_QK + 8
C_WO = C_FG + 12
C_XK = C_WO + 8
C_XV = C_XK + 4
C_XQ = C_XV + 4
C_XO = C_XQ + 4
C_FF = C_XO + 4
N_CHUNKS = C_FF + 6 * NB

N_X, N_MEM, N_CROSS, N_FFN, N_OUT = 0, T, T + 2, 2 * T + 2, 3 * T + 2


def build(nc, x, mem, norm_mix_g, w_in, b_forget, b_gate, pool_w, pool_scale, w_pool_out,
          w_fox_out, w_out, norm_x_g, norm_mem_g, w_xq, w_xkv, w_xo, norm_ffn_g, w_ffn_in,
          w_ffn_out, norm_final_g, out):
    x2, mem2, out2 = x[0], mem[0], out[0]
    w_in, w_out, w_xq, w_xkv, w_xo = w_in[0], w_out[0], w_xq[0], w_xkv[0], w_xo[0]
    w_pool_out, w_fox_out, pool_w = w_pool_out[0], w_fox_out[0], pool_w[0]
    w_ffn_in, w_ffn_out = w_ffn_in[0], w_ffn_out[0]
    za_dram = nc.dram_tensor("za_dram", [KD, P, S], FP32).ap()
    negc_dram = nc.dram_tensor("negc_dram", [HEADS, S], FP32).ap()

    ctx = ExitStack()
    with ctx:
        def keep(name, shape, dt=FP32):
            return ctx.enter_context(nc.sbuf_tensor(name, shape, dt))

        def place(name, kb, shape, dt=FP32):
            with ExitStack() as st:
                if kb:
                    st.enter_context(nc.sbuf_tensor(f"under_{name}", [P, kb * 256], FP32))
                return st.enter_context(nc.sbuf_tensor(name, shape, dt))

        w_raw = [keep(f"w_raw{i}", [P, 1024]) for i in range(RAWS)]
        w_hi = [keep(f"w_hi{i}", [P, 1024], F32R) for i in range(SLOTS)]
        w_lo = [keep(f"w_lo{i}", [P, 1024], F32R) for i in range(SLOTS)]
        ident = keep("ident", [P, P])
        ident_r = keep("ident_r", [P, P], F32R)
        mask = keep("mask", [P, P])
        mask_r = keep("mask_r", [P, P], F32R)
        n_tiles = N_OUT + T
        ss = keep("ss", [P, n_tiles])
        ms = keep("ms", [P, n_tiles])
        rstd = keep("rstd", [P, n_tiles])
        minus_half = keep("minus_half", [P, 1])
        bg = keep("bg", [P, 2 * KD])
        ps_scale = keep("ps_scale", [P, NG])
        count_i = keep("count_i", [P, PAD], mybir.dt.int32)
        count = keep("count", [P, PAD])
        inv_count = keep("inv_count", [P, PAD])
        bf = keep("bf", [HEADS, 1])
        neg_max = keep("neg_max", [P, 2, 2])
        prob_sum = keep("prob_sum", [P, 2, 2])
        prob_inv = keep("prob_inv", [P, 2, 2])
        x_max = keep("x_max", [P, XH, T])
        x_nmax = keep("x_nmax", [P, XH, T])
        x_sum = keep("x_sum", [P, XH, T])
        x_inv = keep("x_inv", [P, XH, T])

        h_hi = place("h_hi", 0, [P, KD, S], F32R)
        h_lo = place("h_lo", 32, [P, KD, S], F32R)
        x_in = [place(f"x_in{i}", 119 + 4 * i, [P, D]) for i in range(T)]
        xn_a = [place(f"xn_a{i}", 64 + 4 * i, [P, D]) for i in range(XNS)]
        v_sb = place("v_sb", 64, [P, T, FOX_W])
        u_sb = place("u_sb", 88, [P, NG, PAD + S])
        win = [place(f"win{i}", 105 + 5 * i, [P, PAD + S]) for i in range(2)]
        pooled = place("pooled", 115, [P, S])
        d_hi = place("d_hi", 119, [P, NG, S], F32R)
        d_lo = place("d_lo", 135, [P, NG, S], F32R)
        sg = [place(f"sg{i}", 151 + 4 * i, [P, S]) for i in range(2)]
        za = [place(f"za{i}", 80 + 4 * i, [P, S]) for i in range(2)]
        f_h = place("f_h", 160, [HEADS, S])
        f_neg = place("f_neg", 164, [HEADS, S])
        f_min = place("f_min", 98, [HEADS, S])
        f_exp = place("f_exp", 102, [HEADS, S])
        f_u = place("f_u", 106, [HEADS, S])
        f_log = place("f_log", 110, [HEADS, S])
        f_one = place("f_one", 114, [HEADS, S])
        q1 = [[place(f"q1_{i}{a}", (160, 88)[i] + 4 * a, [P, S], F32R) for a in range(2)] for i in range(2)]
        q2 = [place(f"q2_{i}", (168, 96)[i], [P, S], F32R) for i in range(2)]
        k1 = [[place(f"k1_{i}{a}", (80, 100)[i] + 4 * a, [P, S], F32R) for a in range(2)] for i in range(2)]
        negc = [place(f"negc{i}", 108 + 4 * i, [P, S]) for i in range(3)]
        prob = [place(f"prob{i}", 120 + 8 * i, [P, 2, S]) for i in range(2)]
        prob_t = place("prob_t", 136, [P, 2, S])
        o_sb = place("o_sb", 144, [P, PAIRS, S])
        o_hi = place("o_hi", 64, [P, PAIRS, S], F32R)
        o_lo = place("o_lo", 80, [P, PAIRS, S], F32R)
        z_hi = place("z_hi", 96, [P, KD, S], F32R)
        z_lo = place("z_lo", 128, [P, KD, S], F32R)
        sg_e = [place(f"sg_e{i}", 160 + 4 * i, [P, S]) for i in range(2)]
        za_e = place("za_e", 168, [P, S])
        xr = place("xr", 64, [P, T, D])
        gain = place("gain", 168, [P, D])
        mem_in = place("mem_in", 24, [P, 2, D])
        xn_m = place("xn_m", 160, [P, 2, D])
        mt_hi = place("mt_hi", 32, [P, KD, MEM], F32R)
        mt_lo = place("mt_lo", 40, [P, KD, MEM], F32R)
        xk_hi = place("xk_hi", 0, [P, XH, MEM], F32R)
        xk_lo = place("xk_lo", 4, [P, XH, MEM], F32R)
        xv_hi = place("xv_hi", 8, [P, 2, XW], F32R)
        xv_lo = place("xv_lo", 12, [P, 2, XW], F32R)
        hx_hi = place("hx_hi", 96, [P, KD, S], F32R)
        hx_lo = place("hx_lo", 128, [P, KD, S], F32R)
        xn_x = [place(f"xn_x{i}", 160 + 4 * i, [P, D]) for i in range(2)]
        xq_hi = place("xq_hi", 16, [P, S], F32R)
        xq_lo = place("xq_lo", 20, [P, S], F32R)
        xp = place("xp", 24, [P, T, MEM])
        xo_hi = place("xo_hi", 32, [P, XH, S], F32R)
        xo_lo = place("xo_lo", 48, [P, XH, S], F32R)
        xpt_hi = place("xpt_hi", 160, [P, 2, HALF], F32R)
        xpt_lo = place("xpt_lo", 164, [P, 2, HALF], F32R)
        junk_x = place("junk_x", 28, [P, D])
        junk_f = place("junk_f", 156, [P, D])
        hf_hi = place("hf_hi", 0, [P, KD, S], F32R)
        hf_lo = place("hf_lo", 32, [P, KD, S], F32R)
        xn_f = [place(f"xn_f{i}", kb, [P, D]) for i, kb in enumerate((160, 164, 144, 148))]
        hid_hi = [place(f"hid_hi{i}", 96 + 16 * i, [P, 2, S], F32R) for i in range(2)]
        hid_lo = [place(f"hid_lo{i}", 104 + 16 * i, [P, 2, S], F32R) for i in range(2)]
        silu = [place(f"silu{i}", 128 + 4 * i, [P, S]) for i in range(2)]
        hid = [place(f"hid{i}", 136 + 4 * i, [P, S]) for i in range(2)]
        y_out = [place(f"y_out{i}", 144 + 4 * i, [P, D]) for i in range(3)]

        ps = ctx.enter_context(nc.psum_tensor("ps", [P, 8, HALF], FP32))

        def two(b):
            return ps[:, b:b + 2, :].rearrange("p b n -> p (b n)")

        def sem(name):
            return ctx.enter_context(nc.semaphore(name))

        raw_loaded = [sem(f"raw_loaded{i}") for i in range(RAWS)]
        hi_ready, lo_ready, w_used = sem("hi_ready"), sem("lo_ready"), sem("w_used")
        consts_set, consts_r, small_in, gain_in = sem("consts_set"), sem("consts_r"), sem("small_in"), sem("gain_in")
        x_loaded = [sem(f"x_loaded{i}") for i in range(T)]
        ss_ready, ms_ready, rstd_ready = sem("ss_ready"), sem("ms_ready"), sem("rstd_ready")
        xn_ready, xt_done, xt_hi, xt_lo = sem("xn_ready"), sem("xt_done"), sem("xt_hi"), sem("xt_lo")
        u_copied, v_done, v_copied = sem("u_copied"), sem("v_done"), sem("v_copied")
        pads_zero, win_step, d_ready, d_hi_ready, d_lo_ready = (sem("pads_zero"), sem("win_step"), sem("d_ready"),
                                                                sem("d_hi_ready"), sem("d_lo_ready"))
        mix_done, mix_hi, mix_lo = sem("mix_done"), sem("mix_hi"), sem("mix_lo")
        f_step, f_exp_ready, f_log_ready, negc_ready, negc_stored = (sem("f_step"), sem("f_exp_ready"), sem("f_log_ready"),
                                                                     sem("negc_ready"), sem("negc_stored"))
        gate_ready, y_done = sem("gate_ready"), sem("y_done")
        za_stored = [sem(f"za_stored{i}") for i in range(2)]
        za_loaded, y_gated, z_sum, z_hi_ready, z_lo_ready = (sem("za_loaded"), sem("y_gated"), sem("z_sum"),
                                                             sem("z_hi_ready"), sem("z_lo_ready"))
        qk_done, qk_hi, qk_lo, negc_loaded = sem("qk_done"), sem("qk_hi"), sem("qk_lo"), [sem(f"negc_loaded{i}") for i in range(3)]
        sc_done, sc_biased, exp_ready, inv_ready, prob_ready = (
            sem("sc_done"), sem("sc_biased"), sem("exp_ready"), sem("inv_ready"), sem("prob_ready"))
        pt_done, pt_act, pt_dve, pv_done, pv_copied, o_hi_ready, o_lo_ready, gate_copied = (
            sem("pt_done"), sem("pt_act"), sem("pt_dve"), sem("pv_done"), sem("pv_copied"), sem("o_hi_ready"),
            sem("o_lo_ready"), sem("gate_copied"))
        mem_loaded, mix_gain_in = sem("mem_loaded"), sem("mix_gain_in")
        xr_loaded, bank_out, xr_added, out_ready, out_stored = (sem("xr_loaded"), sem("bank_out"), sem("xr_added"),
                                                                sem("out_ready"), [sem(f"out_stored{i}") for i in range(3)])
        kv_hi, kv_lo = sem("kv_hi"), sem("kv_lo")
        xq_done, xq_hi_ready, xq_lo_ready = sem("xq_done"), sem("xq_hi_ready"), sem("xq_lo_ready")
        xs_done, xs_max, xs_nmax, xs_exp, xs_inv, xp_ready = (sem("xs_done"), sem("xs_max"), sem("xs_nmax"),
                                                              sem("xs_exp"), sem("xs_inv"), sem("xp_ready"))
        xpt_done, xpt_hi_ready, xpt_lo_ready, xpv_done, xo_hi_ready, xo_lo_ready = (
            sem("xpt_done"), sem("xpt_hi_ready"), sem("xpt_lo_ready"), sem("xpv_done"), sem("xo_hi_ready"), sem("xo_lo_ready"))
        silu_ready, hid_ready, hid_hi_ready, hid_lo_ready = (sem("silu_ready"), sem("hid_ready"), sem("hid_hi_ready"),
                                                             sem("hid_lo_ready"))

        def cols(w, c0, n=P):
            return w[:, c0:c0 + n].rearrange("(k p) n -> p k n", p=P)

        def rows(w, k0, c0, n=HALF):
            return w[k0 * P:(k0 + 2) * P, c0:c0 + n].rearrange("(k p) n -> p k n", p=P)

        def ffn_in_cols(c0):
            return w_ffn_in[:, bass.ds(c0, P)].rearrange("(k p) n -> p k n", p=P)

        def ffn_out_rows(r0, c0):
            return w_ffn_out[bass.ds(r0, 2 * P), c0:c0 + HALF].rearrange("(k p) n -> p k n", p=P)

        def chunk_view(k):
            if k < C_F:
                return cols(w_in, (k - C_U) * P)
            if k == C_F:
                return cols(w_in, COL_F)
            if k < C_G0:
                return rows(w_in, 2 * (k - C_V), COL_V)
            if k == C_G0:
                return cols(w_in, COL_G)
            if k == C_PW:
                return pool_w.rearrange("g c d -> c g d")
            if k < C_QK:
                j, r = divmod(k - C_PG, 3)
                return cols(w_pool_out, 2 * j * P, 2 * P) if r == 2 else cols(w_in, COL_G + (2 * j + r) * P)
            if k < C_FG:
                p, r = divmod(k - C_QK, 2)
                return cols(w_in, (COL_K if r else COL_Q) + p * P)
            if k < C_WO:
                j, r = {C_FG + 2: (1, 0), C_FG + 3: (0, 2)}.get(k, divmod(k - C_FG, 3))
                return cols(w_fox_out, 2 * j * P, 2 * P) if r == 2 else cols(w_in, COL_G + D + (2 * j + r) * P)
            if k < C_XK:
                n, r = divmod(k - C_WO, 4)
                return rows(w_out, 2 * r, n * HALF)
            if k < C_XV:
                return cols(w_xkv, (k - C_XK) * P)
            if k < C_XQ:
                return rows(w_xkv, 2 * (k - C_XV), XW)
            if k < C_XO:
                return cols(w_xq, (k - C_XQ) * P)
            if k < C_FF:
                n, r = divmod(k - C_XO, 2)
                return rows(w_xo, 2 * r, n * HALF)
            return ffn_view(0, k - C_FF)

        def ffn_view(b, r):
            if r < 4:
                t, up = divmod(r, 2)
                return ffn_in_cols(b * 2 * P + (t * P + up * DFF))
            return ffn_out_rows((b - 1) * 2 * P, (r - 4) * HALF)

        def width(k):
            return NG * P if k == C_PW else 1024

        block = ctx.enter_context(nc.Block())

        def half_of(h):
            return slice(h * HALF, (h + 1) * HALF)

        def tile_of(t):
            return slice(t * P, (t + 1) * P)

        def base_of(b):
            return b * 6 + (C_FF - 2)

        @block.sync
        def _(sp):
            def load_raw(n, view, uses=None):
                if n >= RAWS:
                    sp.wait_ge(lo_ready, n - RAWS + 1)
                t = w_raw[n % RAWS][:, 0:width(n)]
                if n == C_PW:
                    t = t.rearrange("p (k n) -> p k n", n=P)
                sp.dma_start(t, view).then_inc(raw_loaded[n % RAWS], 16)

            for t in range(T):
                if t in (4, 6):
                    load_raw(t // 2 - 2, chunk_view(t // 2 - 2))
                sp.dma_start(x_in[t][:], x2[tile_of(t), :]).then_inc(x_loaded[t], 16)
            for k in range(2, C_FF + 4):
                load_raw(k, chunk_view(k) if k < C_FF else ffn_view(0, k - C_FF))
            with sp.Fori(0, (NB - 1) // 2) as i:
                for o in range(2):
                    for r in range(6):
                        n = base_of(1 + o) + r
                        sp.wait_ge(lo_ready, i * 12 + (n - RAWS + 1))
                        if r < 4:
                            j, up = divmod(r, 2)
                            view = ffn_in_cols(i * (4 * P) + ((1 + o) * 2 * P + j * P + up * DFF))
                        else:
                            view = ffn_out_rows(i * (4 * P) + o * 2 * P, (r - 4) * HALF)
                        sp.dma_start(w_raw[n % RAWS][:, :], view).then_inc(raw_loaded[n % RAWS], 16)
            for r in range(2):
                load_raw(N_CHUNKS - 2 + r, ffn_view(NB, 4 + r))
            for t in range(T):
                sp.wait_ge(out_ready, t + 1)
                sp.dma_start(out2[tile_of(t), :], y_out[t % 3][:]).then_inc(out_stored[t % 3], 16)
            for i in range(3):
                sp.wait_ge(out_stored[i], 16 * len(range(i, T, 3)))

        @block.gpsimd
        def _(pool):
            nc.gpsimd.memset(ident[:], 0.0).then_inc(consts_set, 1)
            nc.gpsimd.memset(mask[:], 0.0).then_inc(consts_set, 1)
            nc.gpsimd.memset(minus_half[:], -0.5).then_inc(consts_set, 1)
            pool.wait_ge(consts_set, 3)
            nc.gpsimd.affine_select(out=ident[:], in_=ident[:], compare_op=ALU.not_equal, fill=1.0, base=0,
                                    pattern=[[-1, P]], channel_multiplier=1).then_inc(consts_set, 1)
            nc.gpsimd.affine_select(out=mask[:], in_=mask[:], compare_op=ALU.is_ge, fill=MASKED, base=0,
                                    pattern=[[-1, P]], channel_multiplier=1).then_inc(consts_set, 1)
            nc.gpsimd.iota(count_i[:], pattern=[[1, PAD]], base=1, channel_multiplier=0).then_inc(consts_set, 1)

            def rstd_of(n):
                pool.wait_ge(ss_ready, n + 1)
                nc.gpsimd.tensor_scalar(ms[:, n:n + 1], ss[:, n:n + 1], 1.0 / D, EPS,
                                        ALU.mult, ALU.add).then_inc(ms_ready, 1)
                pool.wait_ge(ms_ready, n + 1)
                nc.gpsimd.tensor_tensor(rstd[:, n:n + 1], ms[:, n:n + 1], minus_half[:],
                                        ALU.pow).then_inc(rstd_ready, 1)

            def split_lo(n):
                pool.wait_ge(hi_ready, n + 1)
                if n:
                    pool.wait_ge(lo_ready, n)
                nc.gpsimd.tensor_tensor(w_lo[n % SLOTS][:], w_raw[n % RAWS][:], w_hi[n % SLOTS][:].bitcast(FP32),
                                        ALU.subtract).then_inc(lo_ready, 1)

            for n in range(N_X, N_MEM):
                rstd_of(n)
                if n == 3:
                    split_lo(0)
                if n == 4:
                    split_lo(1)
                if n == 6:
                    split_lo(2)
            with nc.allow_non_contiguous_dma(reason="small per-feature vectors"):
                pool.dma_start(bg[:], b_gate[0].rearrange("(m p) -> p m", p=P)).then_inc(small_in, 16)
                pool.dma_start(ps_scale[:], pool_scale[0].rearrange("(m p) -> p m", p=P)).then_inc(small_in, 16)
                pool.dma_start(bf[:], b_forget.rearrange("a h -> h a")).then_inc(small_in, 16)
            pool.wait_ge(negc_ready, 1)
            pool.dma_start(negc_dram, f_u[:]).then_inc(negc_stored, 16)
            pool.wait_ge(negc_stored, 16)
            pool.wait_ge(y_gated, KD)
            for h in range(HEADS):
                if h >= 3:
                    pool.wait_ge(sc_biased, 2 * (T * ((h - 3) // 2) + T - 1) + (h - 3) % 2 + 1)
                pool.dma_start(negc[h % 3][:], negc_dram[h:h + 1, :].broadcast_to([P, S])).then_inc(negc_loaded[h % 3], 16)
            pool.wait_ge(sc_done, 2 * PAIRS * T)
            for i in range(2):
                pool.wait_ge(za_stored[i], 16 * (KD // 2))
            for m in range(KD):
                if m:
                    pool.wait_ge(z_sum, m)
                pool.dma_start(za_e[:], za_dram[m]).then_inc(za_loaded, 16)
            pool.wait_ge(w_used, C_WO)
            for t in range(2):
                pool.dma_start(mem_in[:, t, :], mem2[tile_of(t), :]).then_inc(mem_loaded, 16)
            for t in range(T):
                pool.dma_start(xr[:, t, :], x2[tile_of(t), :]).then_inc(xr_loaded, 16)

            def load_gain(g):
                pool.dma_start(gain[:], g.broadcast_to([P, D])).then_inc(gain_in, 16)

            pool.wait_ge(z_sum, KD)
            load_gain(norm_mem_g)
            for n in range(N_MEM, N_CROSS):
                rstd_of(n)
            pool.wait_ge(xn_ready, N_CROSS)
            load_gain(norm_x_g)
            for s in range(8):
                if s in POOL_SPLITS:
                    split_lo(C_XK + s + 2)
                for t in {0: (0, 1, 2)}.get(s, (s + 2,)):
                    if t < T:
                        rstd_of(N_CROSS + t)
            pool.wait_ge(xn_ready, N_FFN)
            load_gain(norm_ffn_g)
            for n in range(N_FFN, N_OUT):
                rstd_of(n)
            pool.wait_ge(xn_ready, N_OUT)
            load_gain(norm_final_g.unsqueeze(0))

            def hid_lo_of(f, par, j):
                pool.wait_ge(hid_hi_ready, f + 1)
                nc.gpsimd.tensor_tensor(hid_lo[par][:, j, :], hid[j][:], hid_hi[par][:, j, :].bitcast(FP32),
                                        ALU.subtract).then_inc(hid_lo_ready, 1)

            for j in range(2):
                hid_lo_of(j, 0, j)
            with pool.Fori(0, (NB - 1) // 2) as i:
                for o in range(2):
                    for j in range(2):
                        hid_lo_of(i * 4 + (2 + 2 * o + j), (1 + o) % 2, j)
            for n in range(N_OUT, N_OUT + T):
                rstd_of(n)

        @block.scalar
        def _(act):
            def split_hi(n, turns=0):
                act.wait_ge(raw_loaded[n % RAWS], turns * (16 * 12 // RAWS) + 16 * (n // RAWS + 1))
                if n >= SLOTS:
                    act.wait_ge(w_used, turns * 12 + (n - SLOTS + 1))
                w = width(n)
                nc.scalar.activation(w_hi[n % SLOTS][:, 0:w], w_raw[n % RAWS][:, 0:w], ACT.Copy).then_inc(hi_ready, 1)

            def square(n, src, junk):
                if n:
                    act.wait_ge(ss_ready, n)
                nc.scalar.activation(junk, src, ACT.Square, accum_out=ss[:, n:n + 1]).then_inc(ss_ready, 1)

            def xt_hi_of(n, bank, dst):
                act.wait_ge(xt_done, n + 1)
                nc.scalar.activation(dst, two(bank).rearrange("p (k n) -> p k n", n=P), ACT.Copy).then_inc(xt_hi, 1)

            act.dma_start(gain[:], norm_mix_g.broadcast_to([P, D])).then_inc(mix_gain_in, 16)

            def x_hi_of(t):
                xt_hi_of(N_X + t, norm_banks(t), h_hi[:, :, tile_of(t)])

            for t in range(T):
                act.wait_ge(x_loaded[t], 16)
                square(t, x_in[t][:], pooled[:])
                if t == 3:
                    split_hi(0)
                if t in (2, 3):
                    x_hi_of(t - 2)
                if t == 3:
                    x_hi_of(2)
                    x_hi_of(3)
                if t == 4:
                    split_hi(1)
                if t > 4:
                    x_hi_of(t - 1)
                if t == 6:
                    split_hi(2)
            x_hi_of(T - 1)

            for k in range(C_U + 1, C_G0):
                split_hi(k + 2)
                if k <= C_F:
                    g = k - 1 - C_U
                    act.wait_ge(w_used, k)
                    nc.scalar.activation(u_sb[:, g, PAD:], two(2 * g), ACT.Copy).then_inc(u_copied, 1)
                if k > C_F:
                    g = k - C_F - 1
                    act.wait_ge(d_ready, g + 1)
                    nc.scalar.activation(d_hi[:, g, :], pooled[:], ACT.Copy).then_inc(d_hi_ready, 1)
            for t in range(T):
                if t < T - 1:
                    act.wait_ge(v_done, t + 1)
                else:
                    act.wait_ge(w_used, C_G0)
                nc.scalar.activation(v_sb[:, t, :], ps[:, t, :], ACT.Copy).then_inc(v_copied, 1)

            def mixed_hi(g):
                if g < NG - 1:
                    act.wait_ge(mix_done, g + 1)
                else:
                    act.wait_ge(w_used, C_PW + 1)
                nc.scalar.activation(d_hi[:, g, :], two(mix_banks(g)), ACT.Copy,
                                     scale=ps_scale[:, g:g + 1]).then_inc(mix_hi, 1)

            def sigmoid_gate(m, bias, dst):
                nc.scalar.activation(dst, two(2 * (m % 2)), ACT.Sigmoid, bias=bias).then_inc(gate_ready, 1)

            def store_za(m):
                act.wait_ge(y_gated, m + 1)
                act.dma_start(za_dram[m], za[m % 2][:]).then_inc(za_stored[m % 2], 16)

            split_hi(C_PG + 1)
            act.wait_ge(small_in, 48)
            mixed_hi(0)
            mixed_hi(1)
            split_hi(C_PG + 2)
            act.wait_ge(w_used, C_G0 + 1)
            sigmoid_gate(0, bg[:, 0:1], sg[0][:])
            mixed_hi(2)
            mixed_hi(3)
            split_hi(C_PG + 3)
            for k in range(C_PG + 2, C_QK + 1):
                split_hi(k + 2)
                j, r = divmod(k - 1 - C_PG, 3)
                if r < 2:
                    m = 2 * j + r
                    act.wait_ge(w_used, k)
                    if m >= 2:
                        act.wait_ge(y_gated, m - 1)
                    sigmoid_gate(m, bg[:, m:m + 1], sg[m % 2][:])
                else:
                    store_za(2 * j)
                    store_za(2 * j + 1)
                if k == C_PG + 2:
                    act.wait_ge(f_step, 4)
                    nc.scalar.activation(f_exp[:], f_min[:], ACT.Exp).then_inc(f_exp_ready, 1)
                    act.wait_ge(f_step, 5)
                    nc.scalar.activation(f_log[:], f_u[:], ACT.Ln).then_inc(f_log_ready, 1)

            def qk_hi_of(g):
                p, r = divmod(g, 4)
                which, h = divmod(r, 2)
                bank = (0, 1, 2, 7)[r] if p == 0 else beside_bank(g)
                if h == 0:
                    act.wait_ge(qk_done, 2 * p + which + 1)
                else:
                    act.wait_ge(w_used, C_QK + 2 * p + which + 1)
                if g in (2, 3):
                    for i in range(2):
                        act.wait_ge(za_stored[i], 16 * (KD // 2))
                for a in range(2):
                    own, other = slice(a * DH, (a + 1) * DH), slice((1 - a) * DH, (2 - a) * DH)
                    if which == 0:
                        nc.scalar.activation(q1[p % 2][a][other, half_of(h)], ps[own, bank, :], ACT.Copy,
                                             scale=DH ** -0.5).then_inc(qk_hi, 1)
                    nc.scalar.activation((k1 if which else q1)[p % 2][a][own, half_of(h)], ps[own, bank, :], ACT.Copy,
                                         scale=1.0 if which else DH ** -0.5).then_inc(qk_hi, 1)

            act.wait_ge(consts_set, 5)
            nc.scalar.activation(ident_r[:], ident[:], ACT.Copy).then_inc(consts_r, 1)
            nc.scalar.activation(mask_r[:], mask[:], ACT.Copy).then_inc(consts_r, 1)

            split_hi(C_QK + 3)
            for g in range(4):
                qk_hi_of(g)

            def pv_copy(v):
                act.wait_ge(pv_done, v + 1)
                nc.scalar.activation(o_sb[:, v // T, tile_of(v % T)], ps[:, 6, 0:P], ACT.Copy).then_inc(pv_copied, 1)

            done = 0
            for u in range(PAIRS * T + 1):
                p, i = divmod(u, T)
                if u % 4 == 0 and u < PAIRS * T:
                    split_hi(C_QK + 2 + u // 4 + 2)
                if u >= 2:
                    pv_copy(u - 2)
                if u >= 1:
                    for g, (a, j0, n) in enumerate(groups_of((u - 1) % T)):
                        done += 1
                        if g < 2:
                            act.wait_ge(pt_done, done)
                            nc.scalar.activation(prob_t[:, a, j0 * P:(j0 + n) * P], ps[:, 4 + g % 2, 0:n * P],
                                                 ACT.Copy).then_inc(pt_act, 1)
                if u < PAIRS * T:
                    n = (i + 1) * P
                    for a in range(2):
                        act.wait_ge(sc_biased, 2 * u + a + 1)
                        nc.scalar.activation(prob[u % 2][:, a, 0:n], prob[u % 2][:, a, 0:n], ACT.Exp,
                                             bias=neg_max[:, u % 2, a:a + 1], scale=-1.0,
                                             accum_out=prob_sum[:, u % 2, a:a + 1]).then_inc(exp_ready, 1)
                if u < 3 * T and u % 2 == 1:
                    qk_hi_of(4 + u // 2)
                if 3 * T <= u < 4 * T and u % 2 == 1:
                    m, h = divmod(u // 2 - 3 * T // 2, 2)
                    if h == 0:
                        act.wait_ge(qk_done, 2 * PAIRS + m + 1)
                    else:
                        act.wait_ge(w_used, C_FG + m + 1)
                    nc.scalar.activation(sg_e[m][:, half_of(h)], ps[:, beside_bank(2 * m + h), :], ACT.Copy).then_inc(gate_copied, 1)
            pv_copy(PAIRS * T - 1)

            for k in range(C_FG + 2, C_WO + 1):
                split_hi(k + 2)
                j, r = {C_FG + 4: (0, 2)}.get(k, divmod(k - 1 - C_FG, 3))
                if k == C_FG + 3:
                    continue
                if k == C_FG + 2:
                    act.wait_ge(pv_copied, PAIRS * T)
                    for p in range(PAIRS):
                        nc.scalar.activation(o_hi[:, p, :], o_sb[:, p, :], ACT.Copy).then_inc(o_hi_ready, 1)
                    act.wait_ge(gate_copied, 4)
                    for m in range(2):
                        nc.scalar.activation(sg_e[m][:], sg_e[m][:], ACT.Sigmoid, bias=bg[:, KD + m:KD + m + 1]).then_inc(gate_ready, 1)
                    continue
                if r < 2:
                    m = 2 * j + r
                    act.wait_ge(w_used, k)
                    if m >= 2:
                        act.wait_ge(z_lo_ready, m - 1)
                    sigmoid_gate(m, bg[:, KD + m:KD + m + 1], sg_e[m % 2][:])
                else:
                    for m in (2 * j, 2 * j + 1):
                        act.wait_ge(z_sum, m + 1)
                        nc.scalar.activation(z_hi[:, m, :], sg_e[m % 2][:], ACT.Copy).then_inc(z_hi_ready, 1)
                if k == C_FG + 4:
                    act.wait_ge(z_lo_ready, 1)
                    sigmoid_gate(2, bg[:, KD + 2:KD + 3], sg_e[0][:])

            for k in range(C_WO + 1, C_XK):
                split_hi(k + 2)
                if k == C_WO + 1:
                    act.wait_ge(mem_loaded, 32)
                    act.wait_ge(z_lo_ready, KD)
                    for t in range(2):
                        square(N_MEM + t, mem_in[:, t, :], xn_m[:, t, :])
                if k == C_WO + 4:
                    for t in range(2):
                        xt_hi_of(N_MEM + t, 2 * t, mt_hi[:, :, tile_of(t)])

            def square_residual(t, n0, added, junk):
                act.wait_ge(xr_added, added + t + 1)
                square(n0 + t, xr[:, t, :], junk)

            for s in range(10):
                if s < 8:
                    split_hi(C_XK + s + 2)
                for t in {0: (0, 1, 2)}.get(s, (s + 2,)):
                    if t < T:
                        square_residual(t, N_CROSS, T, junk_x[:])
                if s in (2, 4):
                    act.wait_ge(w_used, C_XK + s)
                    nc.scalar.activation(xk_hi[:, s - 2:s, :], ps[:, s // 2 - 1, :].rearrange("p (h m) -> p h m", m=MEM),
                                         ACT.Copy).then_inc(kv_hi, 1)
                if s == 8:
                    act.wait_ge(w_used, C_XQ)
                    for t in range(2):
                        nc.scalar.activation(xv_hi[:, t, :], ps[:, 4 + t, :], ACT.Copy).then_inc(kv_hi, 1)
                if s >= 2:
                    xt_hi_of(N_CROSS + s - 2, cross_banks(s - 2), hx_hi[:, :, tile_of(s - 2)])

            def xpt_hi_of(h, half):
                act.wait_ge(xpt_done, 2 * h + half + 1)
                nc.scalar.activation(xpt_hi[:], ps[:, 4:6, :], ACT.Copy).then_inc(xpt_hi_ready, 1)

            def xo_hi_of(h, half):
                act.wait_ge(xpv_done, 2 * h + half + 1)
                nc.scalar.activation(xo_hi[:, h, half_of(half)], ps[:, 6 + half, :], ACT.Copy).then_inc(xo_hi_ready, 1)

            def xq_hi_of(h, half):
                if half:
                    act.wait_ge(w_used, C_XQ + h + 1)
                else:
                    act.wait_ge(xq_done, h + 1)
                nc.scalar.activation(xq_hi[:, half_of(half)], ps[:, half, :], ACT.Copy).then_inc(xq_hi_ready, 1)

            split_hi(C_XQ + 2)
            xq_hi_of(0, 0)
            xq_hi_of(0, 1)
            for h in range(XH + 1):
                if h < XH - 1:
                    split_hi(C_XQ + h + 3)
                for half in range(2):
                    if h:
                        xpt_hi_of(h - 1, half)
                    if h < XH:
                        act.wait_ge(xs_nmax, 2 * h + half + 1)
                        for q in range(4):
                            t = 4 * half + q
                            nc.scalar.activation(xp[:, t, :], ps[:, 2 + q // 2, (q % 2) * MEM:(q % 2 + 1) * MEM], ACT.Exp,
                                                 bias=x_nmax[:, h, t:t + 1], scale=XDH ** -0.5,
                                                 accum_out=x_sum[:, h, t:t + 1]).then_inc(xs_exp, 1)
                    if h:
                        xo_hi_of(h - 1, half)
                    if h < XH - 2:
                        xq_hi_of(h + 1, half)
                    if (h, half) == (XH - 2, 0):
                        xq_hi_of(XH - 1, 0)
                    if (h, half) == (XH - 1, 0):
                        xq_hi_of(XH - 1, 1)
                        split_hi(C_XO + 2)
            split_hi(C_XO + 3)
            split_hi(C_FF)
            split_hi(C_FF + 1)
            def ffn_hi_of(t):
                xt_hi_of(N_FFN + t, norm_banks(t), hf_hi[:, :, tile_of(t)])

            for t in range(T):
                square_residual(t, N_FFN, 3 * T, junk_f[:])
                if t >= 4:
                    ffn_hi_of(t - 4)
            for t in range(4, T):
                ffn_hi_of(t)
                if t == 5:
                    split_hi(C_FF + 2)

            def silu_of(b, j, used):
                act.wait_ge(w_used, used)
                if not (isinstance(b, int) and b == 0):
                    act.wait_ge(hid_ready, b * 2 + (j - 1))
                nc.scalar.activation(silu[j][:], two(4 * j), ACT.Silu).then_inc(silu_ready, 1)

            def hid_hi_of(b, par, j, used):
                act.wait_ge(hid_ready, b * 2 + (j + 1))
                if used is not None:
                    act.wait_ge(w_used, used)
                nc.scalar.activation(hid_hi[par][:, j, :], hid[j][:], ACT.Copy).then_inc(hid_hi_ready, 1)

            split_hi(C_FF + 3)
            silu_of(0, 0, C_FF + 1)
            split_hi(C_FF + 4)
            hid_hi_of(0, 0, 0, None)
            split_hi(C_FF + 5)
            silu_of(0, 1, C_FF + 3)
            with act.Fori(0, (NB - 1) // 2) as i:
                for o in range(2):
                    n0 = base_of(1 + o)
                    b = i * 2 + (1 + o)
                    for r in range(6):
                        split_hi(n0 + r + 2, i)
                        if r == 0:
                            hid_hi_of(b - 1, o, 1, i * 12 + base_of(o))
                        if r == 1:
                            silu_of(b, 0, i * 12 + (n0 + 1))
                        if r == 2:
                            hid_hi_of(b, (1 + o) % 2, 0, i * 12 + n0)
                        if r == 3:
                            silu_of(b, 1, i * 12 + (n0 + 3))
            hid_hi_of(NB - 1, (NB - 1) % 2, 1, base_of(NB - 1))
            for t in range(T):
                square_residual(t, N_OUT, 4 * T + 2 * T * (NB - 1) + t + 1, junk_f[:])

        @block.vector
        def _(dve):
            def split_lo(n, turns=0, lag=0):
                dve.wait_ge(hi_ready, turns * 12 + (n + 1))
                if lag:
                    dve.wait_ge(lo_ready, n)
                if n == C_F and not turns:
                    hi, raw = (w[:, :].rearrange("p (k n) -> p k n", n=P) for w in (w_hi[n % SLOTS], w_raw[n % RAWS]))
                    nc.vector.tensor_tensor(hi[:, :, F_LO:F_LO + HEADS], raw[:, :, 0:HEADS], hi[:, :, 0:HEADS].bitcast(FP32),
                                            ALU.subtract).then_inc(lo_ready, 1)
                    return
                w = width(n)
                nc.vector.tensor_tensor(w_lo[n % SLOTS][:, 0:w], w_raw[n % RAWS][:, 0:w],
                                        w_hi[n % SLOTS][:, 0:w].bitcast(FP32), ALU.subtract).then_inc(lo_ready, 1)

            def normalise(n, dst, src, gains, done):
                dve.wait_ge(rstd_ready, n + 1)
                dve.wait_ge(gain_in if gains else mix_gain_in, 16 * max(gains, 1))
                nc.vector.scalar_tensor_tensor(out=dst, in0=src, scalar=rstd[:, n:n + 1], in1=gain[:],
                                               op0=ALU.mult, op1=ALU.mult).then_inc(done, 1)

            def minus_hi(out, a, hi, done):
                nc.vector.tensor_tensor(out, a, hi.bitcast(FP32), ALU.subtract).then_inc(done, 1)

            def xt_lo_of(n, bank, hi, lo):
                dve.wait_ge(xt_hi, n + 1)
                minus_hi(lo, two(bank).rearrange("p (k n) -> p k n", n=P), hi, xt_lo)

            nc.vector.memset(u_sb[:, :, 0:PAD], 0.0).then_inc(pads_zero, 1)
            for w in win:
                nc.vector.memset(w[:, 0:PAD], 0.0).then_inc(pads_zero, 1)
            dve.wait_ge(consts_set, 6)
            nc.vector.tensor_copy(count[:], count_i[:]).then_inc(pads_zero, 1)
            dve.wait_ge(pads_zero, 4)
            nc.vector.reciprocal(inv_count[:], count[:]).then_inc(pads_zero, 1)

            def x_lo_of(t):
                xt_lo_of(N_X + t, norm_banks(t), h_hi[:, :, tile_of(t)], h_lo[:, :, tile_of(t)])

            for t in range(T):
                if t >= XNS:
                    dve.wait_ge(xt_done, t - XNS + 1)
                normalise(t, xn_a[t % XNS][:], x_in[t][:], 0, xn_ready)
                if t in (2, 3):
                    x_lo_of(t - 2)
                if t == 3:
                    x_lo_of(2)
                    x_lo_of(3)
                if t > 4:
                    x_lo_of(t - 1)
            x_lo_of(T - 1)

            steps = [0]

            def step(ins):
                steps[0] += 1
                ins.then_inc(win_step, 1)
                dve.wait_ge(win_step, steps[0])

            def pool_group(g):
                w = WINDOWS[g]
                u = u_sb[:, g, :]
                src = u
                for e in range(g + 1):
                    dst = win[e % 2]
                    step(nc.vector.tensor_tensor(dst[:, PAD:], src[:, PAD:], src[:, PAD - (1 << e):PAD + S - (1 << e)], ALU.add))
                    src = dst[:, :]
                step(nc.vector.scalar_tensor_tensor(out=pooled[:], in0=src[:, PAD:], scalar=1.0 / w, in1=u[:, PAD:],
                                                    op0=ALU.mult, op1=ALU.subtract))
                step(nc.vector.tensor_tensor(pooled[:, 0:w], src[:, PAD:PAD + w], inv_count[:, 0:w], ALU.mult))
                nc.vector.tensor_tensor(pooled[:, 0:w], pooled[:, 0:w], u[:, PAD:PAD + w], ALU.subtract).then_inc(d_ready, 1)

            def pooled_lo(g):
                dve.wait_ge(d_hi_ready, g + 1)
                minus_hi(d_lo[:, g, :], pooled[:], d_hi[:, g, :], d_lo_ready)
                dve.wait_ge(d_lo_ready, g + 1)

            fsteps = [0]

            def fstep(ins):
                fsteps[0] += 1
                ins.then_inc(f_step, 1)
                dve.wait_ge(f_step, fsteps[0])

            def forget_logits():
                dve.wait_ge(w_used, C_F + 1)
                dve.wait_ge(small_in, 48)
                fstep(nc.vector.tensor_copy(f_neg[:], two(0)[F_LO:F_LO + HEADS, :]))
                fstep(nc.vector.scalar_tensor_tensor(out=f_h[:], in0=two(0)[0:HEADS, :], scalar=bf[:, 0:1], in1=f_neg[:],
                                                     op0=ALU.add, op1=ALU.add))
                fstep(nc.vector.tensor_scalar(f_neg[:], f_h[:], -1.0, None, ALU.mult))

            dve.wait_ge(pads_zero, 5)
            for k in range(C_U + 1, C_G0):
                split_lo(k + 2, lag=1)
                if k == C_V:
                    forget_logits()
                if k >= C_F:
                    g = k - C_F
                    if g:
                        pooled_lo(g - 1)
                    if g < NG:
                        dve.wait_ge(u_copied, g + 1)
                        pool_group(g)

            def mixed_lo(g):
                dve.wait_ge(mix_hi, g + 1)
                nc.vector.scalar_tensor_tensor(out=d_lo[:, g, :], in0=two(mix_banks(g)), scalar=ps_scale[:, g:g + 1],
                                               in1=d_hi[:, g, :].bitcast(FP32), op0=ALU.mult, op1=ALU.subtract).then_inc(mix_lo, 1)

            split_lo(C_PG + 1)
            mixed_lo(0)
            mixed_lo(1)
            split_lo(C_PG + 2)
            mixed_lo(2)
            mixed_lo(3)
            split_lo(C_PG + 3)

            def gated(m, c, dst, gate, chunk, gates):
                if c == 0:
                    dve.wait_ge(y_done, gates // 2 + m // 2 + 1)
                else:
                    dve.wait_ge(w_used, chunk + 1)
                dve.wait_ge(gate_ready, gates + m + 1)
                nc.vector.tensor_tensor(dst, two(4 + 2 * c), gate, ALU.mult).then_inc(y_gated, 1)

            for k in range(C_PG + 2, C_QK + 1):
                split_lo(k + 2)
                j, r = divmod(k - 1 - C_PG, 3)
                if r == 2:
                    for c in range(2):
                        m = 2 * j + c
                        if m >= 2:
                            dve.wait_ge(za_stored[c], 16 * (m // 2))
                        gated(m, c, za[c][:], sg[c][:], k - 1, 0)
                if k == C_PG + 2:
                    fstep(nc.vector.tensor_tensor(f_min[:], f_h[:], f_neg[:], ALU.min))
                    dve.wait_ge(f_exp_ready, 1)
                    fstep(nc.vector.tensor_scalar(f_u[:], f_exp[:], 1.0, None, ALU.add))
                if k == C_PG + 4:
                    dve.wait_ge(f_log_ready, 1)
                    fstep(nc.vector.tensor_scalar(f_min[:], f_u[:], -1.0, 1e-30, ALU.add, ALU.max))
                    fstep(nc.vector.reciprocal(f_one[:], f_min[:]))
                    fstep(nc.vector.tensor_tensor(f_one[:], f_one[:], f_exp[:], ALU.mult))
                    fstep(nc.vector.tensor_tensor(f_one[:], f_one[:], f_log[:], ALU.mult))
                    fstep(nc.vector.scalar_tensor_tensor(out=f_log[:], in0=f_min[:], scalar=2e-30, in1=f_exp[:],
                                                         op0=ALU.is_lt, op1=ALU.mult))
                    fstep(nc.vector.tensor_tensor(f_one[:], f_one[:], f_log[:], ALU.add))
                if k == C_PG + 5:
                    fstep(nc.vector.scalar_tensor_tensor(out=f_one[:], in0=f_h[:], scalar=0.0, in1=f_one[:],
                                                         op0=ALU.min, op1=ALU.subtract))
                    fstep(nc.vector.memset(f_min[:], 1.0))
                    nc.vector.tensor_tensor_scan(out=f_u[:], data0=f_min[:], data1=f_one[:], initial=0.0,
                                                 op0=ALU.mult, op1=ALU.subtract).then_inc(negc_ready, 1)
            split_lo(C_QK + 3)

            def qk_lo_of(g):
                p, r = divmod(g, 4)
                which, h = divmod(r, 2)
                bank = (0, 1, 2, 7)[r] if p == 0 else beside_bank(g)
                dve.wait_ge(qk_hi, 12 * p + (4, 8, 10, 12)[r])
                for a in range(2):
                    own, other = slice(a * DH, (a + 1) * DH), slice((1 - a) * DH, (2 - a) * DH)
                    if which:
                        minus_hi(k1[p % 2][a][other, half_of(h)], ps[own, bank, :], k1[p % 2][a][own, half_of(h)], qk_lo)
                    else:
                        nc.vector.scalar_tensor_tensor(out=q2[p % 2][own, half_of(h)], in0=ps[own, bank, :], scalar=DH ** -0.5,
                                                       in1=q1[p % 2][a][own, half_of(h)].bitcast(FP32),
                                                       op0=ALU.mult, op1=ALU.subtract).then_inc(qk_lo, 1)

            for g in range(4):
                qk_lo_of(g)

            done = 0
            for u in range(PAIRS * T + 1):
                p, i = divmod(u, T)
                b, n = u % 2, (i + 1) * P
                if u % 4 == 0 and u < PAIRS * T:
                    split_lo(C_QK + 2 + u // 4 + 2)
                for a in range(2 if u < PAIRS * T else 0):
                    h = 2 * p + a
                    dve.wait_ge(sc_done, 2 * u + a + 1)
                    dve.wait_ge(negc_loaded[h % 3], 16 * (h // 3 + 1))
                    if u >= 2:
                        dve.wait_ge(pt_done, groups_before(u - 1))
                    nc.vector.tensor_tensor_reduce(out=prob[b][:, a, 0:n], in0=two(2 * a)[:, 0:n], in1=negc[h % 3][:, 0:n],
                                                   scale=-1.0, scalar=HIGHEST, op0=ALU.add, op1=ALU.min,
                                                   accum_out=neg_max[:, b, a:a + 1]).then_inc(sc_biased, 1)
                if u >= 1:
                    for g, (a, j0, m) in enumerate(groups_of((u - 1) % T)):
                        done += 1
                        if g >= 2:
                            dve.wait_ge(pt_done, done)
                            nc.vector.tensor_copy(prob_t[:, a, j0 * P:(j0 + m) * P], ps[:, 4 + g % 2, 0:m * P]).then_inc(pt_dve, 1)
                for a in range(2 if u < PAIRS * T else 0):
                    dve.wait_ge(exp_ready, 2 * u + a + 1)
                    nc.vector.reciprocal(prob_inv[:, b, a:a + 1], prob_sum[:, b, a:a + 1]).then_inc(inv_ready, 1)
                    dve.wait_ge(inv_ready, 2 * u + a + 1)
                    nc.vector.tensor_scalar(prob[b][:, a, 0:n], prob[b][:, a, 0:n], prob_inv[:, b, a:a + 1], None,
                                            ALU.mult).then_inc(prob_ready, 1)
                if u < 3 * T and u % 2 == 1:
                    qk_lo_of(4 + u // 2)

            for k in range(C_FG + 2, C_WO + 1):
                split_lo(k + 2)
                j, r = {C_FG + 3: (0, 0), C_FG + 4: (0, 2)}.get(k, divmod(k - 1 - C_FG, 3))
                if k == C_FG + 2:
                    for p in range(PAIRS):
                        dve.wait_ge(o_hi_ready, p + 1)
                        minus_hi(o_lo[:, p, :], o_sb[:, p, :], o_hi[:, p, :], o_lo_ready)
                elif r == 2:
                    for c in range(2):
                        gated(2 * j + c, c, sg_e[c][:], sg_e[c][:], k - 1, KD)
                    for c in range(2):
                        m = 2 * j + c
                        dve.wait_ge(y_gated, KD + m + 1)
                        dve.wait_ge(za_loaded, 16 * (m + 1))
                        nc.vector.tensor_tensor(sg_e[c][:], sg_e[c][:], za_e[:], ALU.add).then_inc(z_sum, 1)
                    for c in range(2):
                        m = 2 * j + c
                        dve.wait_ge(z_hi_ready, m + 1)
                        minus_hi(z_lo[:, m, :], sg_e[c][:], z_hi[:, m, :], z_lo_ready)

            def add(t, n, earlier, outs, used, turns=0):
                if t < T - 1:
                    dve.wait_ge(bank_out, turns * 28 + (outs + t + 1))
                else:
                    dve.wait_ge(w_used, turns * 12 + used)
                if earlier >= 2 * T:
                    dve.wait_ge(xr_added, turns * 32 + (earlier + t - 2 * T + 1))
                nc.vector.tensor_tensor(xr[:, t, half_of(n)], ps[:, t, :], xr[:, t, half_of(n)], ALU.add).then_inc(xr_added, 1)

            for k in range(C_WO + 1, C_XK):
                split_lo(k + 2)
                if k == C_WO + 1:
                    for t in range(2):
                        normalise(N_MEM + t, xn_m[:, t, :], mem_in[:, t, :], 1, xn_ready)
                if k == C_WO + 3:
                    dve.wait_ge(xr_loaded, 16 * T)
                    for t in range(T):
                        add(t, 0, 0, 0, C_WO + 4)
                if k == C_WO + 4:
                    for t in range(2):
                        xt_lo_of(N_MEM + t, 2 * t, mt_hi[:, :, tile_of(t)], mt_lo[:, :, tile_of(t)])
                if k == C_WO + 7:
                    for t in range(T):
                        add(t, 1, T, T - 1, C_WO + 8)

            for s in range(10):
                if s < 8:
                    if s not in POOL_SPLITS:
                        split_lo(C_XK + s + 2, lag=1)
                    if s < 2:
                        dve.wait_ge(xt_done, N_CROSS)
                    else:
                        dve.wait_ge(xt_done, N_CROSS + s - 1)
                    normalise(N_CROSS + s, xn_x[s % 2][:], xr[:, s, :], 2, xn_ready)
                if s in (2, 4):
                    dve.wait_ge(kv_hi, s // 2)
                    minus_hi(xk_lo[:, s - 2:s, :], ps[:, s // 2 - 1, :].rearrange("p (h m) -> p h m", m=MEM),
                             xk_hi[:, s - 2:s, :], kv_lo)
                if s == 8:
                    for t in range(2):
                        dve.wait_ge(kv_hi, XH // 2 + t + 1)
                        minus_hi(xv_lo[:, t, :], ps[:, 4 + t, :], xv_hi[:, t, :], kv_lo)
                if s >= 2:
                    xt_lo_of(N_CROSS + s - 2, cross_banks(s - 2), hx_hi[:, :, tile_of(s - 2)], hx_lo[:, :, tile_of(s - 2)])

            def xpt_lo_of(h, half):
                dve.wait_ge(xpt_hi_ready, 2 * h + half + 1)
                minus_hi(xpt_lo[:], ps[:, 4:6, :], xpt_hi[:], xpt_lo_ready)

            def xo_lo_of(h, half):
                dve.wait_ge(xo_hi_ready, 2 * h + half + 1)
                minus_hi(xo_lo[:, h, half_of(half)], ps[:, 6 + half, :], xo_hi[:, h, half_of(half)], xo_lo_ready)

            def xq_lo_of(h, half):
                dve.wait_ge(xq_hi_ready, 2 * h + half + 1)
                minus_hi(xq_lo[:, half_of(half)], ps[:, half, :], xq_hi[:, half_of(half)], xq_lo_ready)

            def probabilities(h, half):
                g = 2 * h + half
                dve.wait_ge(xs_done, g + 1)
                t4 = slice(4 * half, 4 * half + 4)
                for b in range(2):
                    t0 = 4 * half + 2 * b
                    nc.vector.tensor_reduce(x_max[:, h, t0:t0 + 2], ps[:, 2 + b, :].rearrange("p (q m) -> p q m", m=MEM),
                                            AX, ALU.max).then_inc(xs_max, 1)
                dve.wait_ge(xs_max, 2 * g + 2)
                nc.vector.tensor_scalar(x_nmax[:, h, t4], x_max[:, h, t4], -XDH ** -0.5, None, ALU.mult).then_inc(xs_nmax, 1)
                dve.wait_ge(xs_exp, 4 * g + 4)
                nc.vector.reciprocal(x_inv[:, h, t4], x_sum[:, h, t4]).then_inc(xs_inv, 1)
                dve.wait_ge(xs_inv, g + 1)
                for t in range(4 * half, 4 * half + 4):
                    nc.vector.tensor_scalar(xp[:, t, :], xp[:, t, :], x_inv[:, h, t:t + 1], None, ALU.mult).then_inc(xp_ready, 1)

            split_lo(C_XQ + 2)
            xq_lo_of(0, 0)
            xq_lo_of(0, 1)
            for h in range(XH + 1):
                if h < XH - 1:
                    split_lo(C_XQ + h + 3)
                for half in range(2):
                    if h:
                        xpt_lo_of(h - 1, half)
                    if h < XH:
                        probabilities(h, half)
                    if h:
                        xo_lo_of(h - 1, half)
                    if h < XH - 2:
                        xq_lo_of(h + 1, half)
                    if (h, half) == (XH - 2, 0):
                        xq_lo_of(XH - 1, 0)
                    if (h, half) == (XH - 1, 0):
                        xq_lo_of(XH - 1, 1)
                        split_lo(C_XO + 2)
            split_lo(C_XO + 3)
            for t in range(T):
                add(t, 0, 2 * T, 2 * (T - 1), C_XO + 2)
            split_lo(C_FF)
            split_lo(C_FF + 1)
            def ffn_lo_of(t):
                xt_lo_of(N_FFN + t, norm_banks(t), hf_hi[:, :, tile_of(t)], hf_lo[:, :, tile_of(t)])

            def ffn_normalise(t):
                if t >= XNS:
                    dve.wait_ge(xt_done, N_FFN + t - XNS + 1)
                normalise(N_FFN + t, xn_f[t % XNS][:], xr[:, t, :], 3, xn_ready)

            for t in range(T):
                add(t, 1, 3 * T, 3 * (T - 1), C_XO + 4)
                if 2 <= t < 6:
                    ffn_normalise(t - 2)
                if t >= 6:
                    ffn_lo_of(t - 6)
            ffn_lo_of(2)
            ffn_lo_of(3)
            for t in range(4, T):
                ffn_normalise(t)
                if t > 4:
                    ffn_lo_of(t - 1)
                if t == 6:
                    split_lo(C_FF + 2)
            ffn_lo_of(T - 1)

            def hid_of(b, j, used):
                dve.wait_ge(w_used, used)
                dve.wait_ge(silu_ready, b * 2 + (j + 1))
                if not (isinstance(b, int) and b == 0):
                    dve.wait_ge(hid_lo_ready, b * 2 + (j - 1))
                nc.vector.tensor_tensor(hid[j][:], two(4 * j + 2), silu[j][:], ALU.mult).then_inc(hid_ready, 1)

            split_lo(C_FF + 3)
            split_lo(C_FF + 4)
            hid_of(0, 0, C_FF + 2)
            split_lo(C_FF + 5)
            hid_of(0, 1, C_FF + 4)
            with dve.Fori(0, (NB - 1) // 2) as i:
                for o in range(2):
                    n0 = base_of(1 + o)
                    for r in range(6):
                        split_lo(n0 + r + 2, i)
                        if r in (2, 4):
                            hid_of(i * 2 + (1 + o), r // 2 - 1, i * 12 + (n0 + r))
                        if r >= 4:
                            for t in range(T):
                                add(t, r - 4, 4 * T + 2 * T * o + T * (r - 4), 4 * (T - 1) + 2 * (T - 1) * o + (T - 1) * (r - 4),
                                    n0 + r + 1, i)
            added = 4 * T + 2 * T * (NB - 1)
            outs = 4 * (T - 1) + 2 * (T - 1) * (NB - 1)
            dve.wait_ge(xr_added, added)
            for t in range(T + 1):
                for n in range(2 if t < T else 0):
                    if t < T - 1:
                        dve.wait_ge(bank_out, outs + 2 * t + n + 1)
                    else:
                        dve.wait_ge(w_used, N_CHUNKS - 1 + n)
                    nc.vector.tensor_tensor(xr[:, t, half_of(n)], ps[:, 2 * (t % 4) + n, :], xr[:, t, half_of(n)],
                                            ALU.add).then_inc(xr_added, 1)
                if t:
                    m = t - 1
                    if m >= 3:
                        dve.wait_ge(out_stored[m % 3], 16 * (m // 3))
                    normalise(N_OUT + m, y_out[m % 3][:], xr[:, m, :], 4, out_ready)

        @block.tensor
        def _(pe):
            def mm3(dst, w_h, w_l, x_h, x_l, start, stop):
                nc.tensor.matmul(dst, w_h, x_l, start=start, stop=False)
                nc.tensor.matmul(dst, w_h, x_h, start=False, stop=False)
                return nc.tensor.matmul(dst, w_l, x_h, start=False, stop=stop)

            def transpose_tile(src, bank, done):
                for k in range(KD):
                    last = nc.tensor.transpose(two(bank)[:, tile_of(k)], src[:, tile_of(k)], ident[:])
                last.then_inc(done, 1)

            def project_half(n, h, dst, x_hi, x_lo, tiles=KD, c=0, stride=P):
                wh, wl = w_hi[n % SLOTS], w_lo[n % SLOTS]
                for k in range(tiles):
                    w = slice(k * stride + c * P, k * stride + (c + 1) * P)
                    last = mm3(dst, wh[:, w], wl[:, w], x_hi[:, k, half_of(h)], x_lo[:, k, half_of(h)],
                               k == 0, k == tiles - 1)
                return last

            def project(n, bank, x_hi, x_lo, turns=0):
                pe.wait_ge(lo_ready, turns * 12 + (n + 1))
                for h in range(2):
                    last = project_half(n, h, ps[:, bank + h, :], x_hi, x_lo)
                last.then_inc(w_used, 1)

            def project_pair(n, x_hi, x_lo):
                pe.wait_ge(lo_ready, n + 1)
                for c in range(2):
                    for h in range(2):
                        last = project_half(n, h, ps[:, 4 + 2 * c + h, :], x_hi, x_lo, 4, c, 2 * P)
                    last.then_inc(y_done if c == 0 else w_used, 1)

            def tokens_by(n, k0, x_hi, x_lo, first, last_chunk, bank_free, turns=0, done=None, after=None,
                          order=range(T)):
                pe.wait_ge(lo_ready, turns * 12 + (n + 1))
                wh, wl = w_hi[n % SLOTS], w_lo[n % SLOTS]
                for t in order:
                    if first:
                        bank_free(t)
                    for r in range(2):
                        last = mm3(ps[:, t, :], x_hi[:, k0 + r, tile_of(t)], x_lo[:, k0 + r, tile_of(t)],
                                   wh[:, half_of(r)], wl[:, half_of(r)], first and r == 0, last_chunk and r == 1)
                    if t == order[-1]:
                        last.then_inc(w_used, 1)
                    elif last_chunk:
                        last.then_inc(done or bank_out, 1)
                    if after:
                        after(t)

            def norm_and_project(n, xn, bank_free, c0, x_hi, x_lo, ahead=0):
                def tiles(r, h, k0, k1):
                    c = c0 + r
                    if h == 0 and k0 == 0:
                        pe.wait_ge(lo_ready, c + 1)
                    for k in range(k0, k1):
                        last = mm3(ps[:, 2 * r + h, :], w_hi[c % SLOTS][:, tile_of(k)], w_lo[c % SLOTS][:, tile_of(k)],
                                   x_hi[:, k, half_of(h)], x_lo[:, k, half_of(h)], k == 0, k == KD - 1)
                    if h and k1 == KD:
                        last.then_inc(w_used, 1)

                def token_pair(e, k0, k1):
                    tok = slice(2 * e * P, 2 * (e + 1) * P)
                    for k in range(k0, k1):
                        mm3(ps[:, 0, tok], w_hi[c0 % SLOTS][:, tile_of(k)], w_lo[c0 % SLOTS][:, tile_of(k)],
                            x_hi[:, k, tok], x_lo[:, k, tok], k == 0, k == KD - 1)

                for t in range(ahead, 4):
                    pe.wait_ge(xn_ready, n + t + 1)
                    bank_free(t)
                    transpose_tile(xn[t % XNS], norm_banks(t), xt_done)
                pe.wait_ge(lo_ready, c0 + 1)
                pe.wait_ge(xt_lo, n + 2)
                token_pair(0, 0, KD)
                pe.wait_ge(xt_lo, n + 4)
                for t in range(4, T):
                    if t < 6:
                        token_pair(1, 4 * (t - 4), 4 * (t - 4) + 4)
                    else:
                        tiles(1, 0, 4 * (t - 6), 4 * (t - 6) + 4)
                    pe.wait_ge(xn_ready, n + t + 1)
                    pe.wait_ge(xt_lo, n + t - 1)
                    transpose_tile(xn[t % XNS], norm_banks(t), xt_done)
                pe.wait_ge(xt_lo, n + T - 1)
                tiles(2, 0, 0, KD)
                pe.wait_ge(xt_lo, n + T)
                for r in range(3):
                    tiles(r, 1, 0, KD)
                project(c0 + 3, 6, x_hi, x_lo)

            pe.wait_ge(consts_set, 5)
            norm_and_project(N_X, xn_a, lambda t: None, C_U, h_hi, h_lo)
            pe.wait_ge(lo_ready, C_F + 1)
            pe.wait_ge(u_copied, 1)
            for h in range(2):
                for k in range(KD):
                    w = w_hi[C_F % SLOTS][:, k * P:k * P + F_LO + HEADS]
                    nc.tensor.matmul(ps[0:F_LO + HEADS, h, :], w, h_lo[:, k, half_of(h)], start=k == 0, stop=False)
                    last = nc.tensor.matmul(ps[0:F_LO + HEADS, h, :], w, h_hi[:, k, half_of(h)], start=False, stop=k == KD - 1)
            last.then_inc(w_used, 1)

            def v_bank(t):
                pe.wait_ge(u_copied, t // 2 + 1)
                if t < 2:
                    pe.wait_ge(f_step, 2)

            for r in range(4):
                tokens_by(C_V + r, 2 * r, h_hi, h_lo, r == 0, r == 3, v_bank, done=v_done,
                          order=(2, 3, 4, 5, 6, 7, 0, 1) if r == 0 else range(T))

            def mix(g):
                pe.wait_ge(d_lo_ready, g + 1)
                for h in range(2):
                    last = mm3(ps[:, mix_banks(g) + h, :], w_hi[C_PW % SLOTS][:, tile_of(g)], w_lo[C_PW % SLOTS][:, tile_of(g)],
                               d_hi[:, g, half_of(h)], d_lo[:, g, half_of(h)], True, True)
                last.then_inc(mix_done if g < NG - 1 else w_used, 1)

            pe.wait_ge(lo_ready, C_PW + 1)
            pe.wait_ge(v_copied, 4)
            mix(0)
            pe.wait_ge(v_copied, 6)
            mix(1)
            project(C_G0, 0, h_hi, h_lo)
            pe.wait_ge(v_copied, T)
            mix(2)
            pe.wait_ge(mix_lo, 2)
            mix(3)
            for j in range(4):
                for r in range(2):
                    if j:
                        pe.wait_ge(gate_ready, 2 * j + r - 1)
                    if j or r:
                        project(C_PG + 3 * j + r, 2 * r, h_hi, h_lo)
                if j:
                    pe.wait_ge(y_gated, 2 * j)
                else:
                    pe.wait_ge(mix_lo, NG)
                project_pair(C_PG + 3 * j + 2, d_hi, d_lo)

            def token_half(n, h, bank, quarter):
                for k in range(KD) if quarter is None else range(2 * quarter, 2 * quarter + 2):
                    last = mm3(ps[:, bank, :], w_hi[n % SLOTS][:, tile_of(k)], w_lo[n % SLOTS][:, tile_of(k)],
                               h_hi[:, k, half_of(h)], h_lo[:, k, half_of(h)], k == 0, k == KD - 1)
                if quarter in (None, 3):
                    last.then_inc(w_used if h else qk_done, 1)

            def qk_group(g, quarter=None):
                p, r = divmod(g, 4)
                which, h = divmod(r, 2)
                n = C_QK + 2 * p + which
                if not quarter:
                    pe.wait_ge(lo_ready, n + 1)
                    if p and r >= 2:
                        pe.wait_ge(qk_lo, 2 * g)
                token_half(n, h, (0, 1, 2, 7)[r] if p == 0 else beside_bank(g), quarter)

            def gate_group(g, quarter):
                m, h = divmod(g, 2)
                if quarter == 0:
                    pe.wait_ge(lo_ready, C_FG + m + 1)
                    if g >= 2:
                        pe.wait_ge(gate_copied, g)
                token_half(C_FG + m, h, beside_bank(g), quarter)

            pe.wait_ge(gate_ready, KD)
            for g in range(4):
                if g == 3:
                    pe.wait_ge(y_gated, KD)
                qk_group(g)

            def beside(u, part):
                if u < 3 * T:
                    qk_group(4 + u // 2, 2 * (u % 2) + part)
                elif u < 4 * T:
                    gate_group(u // 2 - 3 * T // 2, 2 * (u % 2) + part)

            def transposed(v, groups):
                for g, (a, j0, n) in groups:
                    if g >= 2:
                        pe.wait_ge(pt_act, 2 * v + g - 1)
                    for j in range(j0, j0 + n):
                        last = nc.tensor.transpose(ps[:, 4 + g % 2, tile_of(j - j0)], prob[v % 2][:, a, tile_of(j)], ident[:])
                    last.then_inc(pt_done, 1)

            pe.wait_ge(consts_r, 2)
            for u in range(PAIRS * T + 1):
                p, i = divmod(u, T)
                if u == 0:
                    beside(0, 0)
                    beside(0, 1)
                v = u - 1
                groups = list(enumerate(groups_of(v % T))) if u else []
                if u and i == 0:
                    pe.wait_ge(prob_ready, 2 * u)
                    transposed(v, groups[:2])
                if u < PAIRS * T:
                    pe.wait_ge(qk_lo, 8 * p + 8)
                    for a in range(2):
                        if u:
                            pe.wait_ge(sc_biased, 2 * (u - 1) + a + 1)
                        if i == 4 and a == 1:
                            pe.wait_ge(qk_lo if p < PAIRS - 1 else gate_copied, 8 * p + 10 if p < PAIRS - 1 else 1)
                        own = slice(a * DH, (a + 1) * DH)
                        q1a, k1a, q2a = q1[p % 2][a], k1[p % 2][a], q2[p % 2]
                        for c in range(0, i + 1, 4):
                            n = min(4, i + 1 - c)
                            keys = slice(c * P, (c + n) * P)
                            dst = ps[:, 2 * a + c // 4, 0:n * P]
                            diagonal = c + n == i + 1
                            nc.tensor.matmul(dst, q1a[:, tile_of(i)], k1a[:, keys], start=True, stop=False)
                            last = nc.tensor.matmul(dst, q2a[own, tile_of(i)], k1a[own, keys], start=False, stop=not diagonal)
                            if diagonal:
                                last = nc.tensor.matmul(dst[:, (n - 1) * P:], ident_r[:], mask_r[:], start=False, stop=True)
                        last.then_inc(sc_done, 1)
                if i:
                    pe.wait_ge(prob_ready, 2 * u)
                    transposed(v, groups[:2])
                if u:
                    beside(u, 0)
                    transposed(v, groups[2:])
                    beside(u, 1)
                    pe.wait_ge(pt_act, 2 * u)
                    if v >= 4:
                        pe.wait_ge(pt_dve, groups_before(u) - 2 * u)
                    if v:
                        pe.wait_ge(pv_copied, v)
                    for j in range(v % T + 1):
                        for a in range(2):
                            hc = (2 * (v // T) + a) * DH
                            last = nc.tensor.matmul(ps[a * DH:(a + 1) * DH, 6, 0:P], v_sb[:, j, hc:hc + DH],
                                                    prob_t[:, a, tile_of(j)], start=j == 0, stop=j == v % T)
                    last.then_inc(pv_done, 1)

            pe.wait_ge(sc_biased, 2 * PAIRS * T)
            project(C_FG + 2, 0, h_hi, h_lo)
            pe.wait_ge(pv_copied, PAIRS * T)
            pe.wait_ge(gate_copied, 4)
            pe.wait_ge(o_lo_ready, PAIRS)
            project_pair(C_FG + 3, o_hi, o_lo)
            project(C_FG + 4, 2, h_hi, h_lo)
            for j in range(1, 4):
                if j > 1:
                    for r in range(2):
                        pe.wait_ge(gate_ready, KD + 2 * j + r - 1)
                        project(C_FG + 3 * j + r, 2 * r, h_hi, h_lo)
                pe.wait_ge(y_gated, KD + 2 * j)
                project_pair(C_FG + 3 * j + 2, o_hi, o_lo)

            pe.wait_ge(gate_ready, 2 * KD)
            for r in range(4):
                pe.wait_ge(z_lo_ready, 2 * r + 2)
                tokens_by(C_WO + r, 2 * r, z_hi, z_lo, r == 0, r == 3,
                          lambda t: pe.wait_ge(y_gated, 2 * KD) if t == 4 else None)
            for t in range(2):
                pe.wait_ge(xn_ready, N_MEM + t + 1)
                pe.wait_ge(xr_added, 2 * t + 2)
                transpose_tile(xn_m[:, t, :], 2 * t, xt_done)

            def w_out_bank(t):
                pe.wait_ge(xr_added, t + 1)
                if t in (0, 2):
                    pe.wait_ge(xt_lo, N_MEM + t // 2 + 1)

            for r in range(4):
                tokens_by(C_WO + 4 + r, 2 * r, z_hi, z_lo, r == 0, r == 3, w_out_bank,
                          order=(4, 5, 6, 7, 0, 1, 2, 3) if r == 0 else range(T))

            def cross_tile(t):
                pe.wait_ge(xn_ready, N_CROSS + t + 1)
                pe.wait_ge(xr_added, 2 * T)
                if t >= 2:
                    pe.wait_ge(xt_lo, N_CROSS + t - 1)
                transpose_tile(xn_x[t % 2], cross_banks(t), xt_done)

            for s in range(8):
                n = C_XK + s
                pe.wait_ge(lo_ready, n + 1)
                if s < XH:
                    pe.wait_ge(xr_added, T + s // 2 + 1)
                    for k in range(KD):
                        last = mm3(ps[:, s // 2, (s % 2) * MEM:(s % 2 + 1) * MEM], w_hi[n % SLOTS][:, tile_of(k)], w_lo[n % SLOTS][:, tile_of(k)],
                                   mt_hi[:, k, :], mt_lo[:, k, :], k == 0, k == KD - 1)
                else:
                    if s == XH:
                        pe.wait_ge(xr_added, 2 * T)
                    for t in range(2):
                        for r in range(2):
                            k = 2 * (s - XH) + r
                            last = mm3(ps[:, 4 + t, :], mt_hi[:, k, tile_of(t)], mt_lo[:, k, tile_of(t)],
                                       w_hi[n % SLOTS][:, half_of(r)], w_lo[n % SLOTS][:, half_of(r)], k == 0, k == KD - 1)
                last.then_inc(w_used, 1)
                if s >= 1:
                    cross_tile(s - 1)
            cross_tile(T - 1)

            def xq_quarter(h, q):
                half = q // 2
                n = C_XQ + h
                if q == 0:
                    pe.wait_ge(lo_ready, n + 1)
                if h and q % 2 == 0:
                    pe.wait_ge(xq_lo_ready, 2 * (h - 1) + half + 1)
                for k in range(4 * (q % 2), 4 * (q % 2) + 4):
                    last = mm3(ps[:, half, :], w_hi[n % SLOTS][:, tile_of(k)], w_lo[n % SLOTS][:, tile_of(k)],
                               hx_hi[:, k, half_of(half)], hx_lo[:, k, half_of(half)], k == 0, k == KD - 1)
                if q % 2:
                    last.then_inc(w_used if half else xq_done, 1)

            def scores(h, half):
                pe.wait_ge(xq_lo_ready, 2 * h + half + 1)
                if h or half:
                    pe.wait_ge(xs_exp, 4 * (2 * h + half))
                for q in range(4):
                    t = 4 * half + q
                    last = mm3(ps[:, 2 + q // 2, (q % 2) * MEM:(q % 2 + 1) * MEM], xq_hi[:, tile_of(t)], xq_lo[:, tile_of(t)],
                               xk_hi[:, h, :], xk_lo[:, h, :], True, True)
                last.then_inc(xs_done, 1)

            def xpt(h, half):
                pe.wait_ge(xp_ready, 8 * h + 4 * half + 4)
                if h or half:
                    pe.wait_ge(xpt_lo_ready, 2 * h + half)
                for m in range(2):
                    for t in range(4):
                        last = nc.tensor.transpose(ps[:, 4 + m, tile_of(t)], xp[:, 4 * half + t, tile_of(m)], ident[:])
                last.then_inc(xpt_done, 1)

            def xpv(h, half):
                pe.wait_ge(xpt_lo_ready, 2 * h + half + 1)
                if h:
                    pe.wait_ge(xo_lo_ready, 2 * (h - 1) + half + 1)
                for m in range(2):
                    last = mm3(ps[:, 6 + half, :], xv_hi[:, m, tile_of(h)], xv_lo[:, m, tile_of(h)],
                               xpt_hi[:, m, :], xpt_lo[:, m, :], m == 0, m == 1)
                last.then_inc(xpv_done, 1)

            def w_xo_tile(t):
                wh, wl = w_hi[C_XO % SLOTS], w_lo[C_XO % SLOTS]
                for r in range(2):
                    last = mm3(ps[:, t, :], xo_hi[:, r, tile_of(t)], xo_lo[:, r, tile_of(t)],
                               wh[:, half_of(r)], wl[:, half_of(r)], r == 0, False)
                if t == T - 1:
                    last.then_inc(w_used, 1)

            pe.wait_ge(kv_lo, XH // 2)
            pe.wait_ge(xt_lo, N_CROSS + 4)
            for q in range(4):
                if q == 2:
                    pe.wait_ge(xt_lo, N_FFN)
                xq_quarter(0, q)
            pe.wait_ge(kv_lo, XH // 2 + 2)
            last_head = {(XH - 2, 0): 0, (XH - 2, 1): 1, (XH - 1, 0): 2, (XH - 1, 1): 3}

            def between(h, place):
                if h < XH - 2:
                    xq_quarter(h + 1, place)
                elif (h, place) in last_head:
                    xq_quarter(XH - 1, last_head[h, place])
                elif (h, place) == (XH - 1, 2):
                    pe.wait_ge(lo_ready, C_XO + 1)
                    pe.wait_ge(xo_lo_ready, 4)
                    pe.wait_ge(xq_lo_ready, 2 * XH)
                    w_xo_tile(0)
                elif (h, place) == (XH, 0):
                    w_xo_tile(1)
                    pe.wait_ge(xs_exp, 8 * XH)
                    w_xo_tile(2)
                elif (h, place) == (XH, 2):
                    w_xo_tile(3)

            for h in range(XH + 1):
                for half in range(2):
                    if h:
                        xpt(h - 1, half)
                    if h < XH:
                        scores(h, half)
                    between(h, 2 * half)
                    if h:
                        xpv(h - 1, half)
                    between(h, 2 * half + 1)

            for t in range(4, T):
                if t >= 6:
                    pe.wait_ge(xo_lo_ready, 2 * XH - (0 if t == 7 else 1))
                w_xo_tile(t)
            pe.wait_ge(xo_lo_ready, 2 * XH)
            for r in range(1, 3):
                tokens_by(C_XO + r, 2 * (r % 2), xo_hi, xo_lo, r == 2, r % 2 == 1,
                          lambda t: pe.wait_ge(xr_added, 2 * T + t + 1))

            def banks_added(t):
                pe.wait_ge(xr_added, 3 * T + 2 * t + 2)

            def early_tile(t):
                if 4 <= t < 7:
                    e = t - 4
                    pe.wait_ge(xn_ready, N_FFN + e + 1)
                    banks_added(e)
                    transpose_tile(xn_f[e], 2 * e, xt_done)

            tokens_by(C_XO + 3, 2, xo_hi, xo_lo, False, True, None, after=early_tile)

            norm_and_project(N_FFN, xn_f, banks_added, C_FF, hf_hi, hf_lo, 3)

            def ffn_out(b, par, n0, turns):
                pe.wait_ge(hid_lo_ready, turns * 4 + 2 * (b + 1))
                for n in range(2):
                    def bank_free(t):
                        if n:
                            pe.wait_ge(xr_added, turns * 32 + (4 * T + 2 * T * b + t + 1))
                        elif t % 2 == 0:
                            pe.wait_ge(hid_ready if t % 4 else silu_ready, turns * 4 + (2 * (b + 1) + t // 4 + 1))
                    tokens_by(n0 + n, 0, hid_hi[par], hid_lo[par], True, True, bank_free, turns)

            with pe.Fori(0, (NB - 1) // 2) as i:
                for o in range(2):
                    n0 = base_of(1 + o)
                    for r in range(4):
                        pe.wait_ge(xr_added, i * 32 + (4 * T + 2 * T * (o - 1) + T + 2 * r + 2))
                        pe.wait_ge(hid_ready if r % 2 else silu_ready, i * 4 + (2 * o + r // 2 + 1))
                        project(n0 + r, 2 * r, hf_hi, hf_lo, i)
                    ffn_out(o, o, n0 + 4, i)
            par = (NB - 1) % 2
            pe.wait_ge(hid_lo_ready, 2 * NB)
            pe.wait_ge(lo_ready, N_CHUNKS)
            for t in range(T):
                for n in range(2):
                    wh, wl = w_hi[(N_CHUNKS - 2 + n) % SLOTS], w_lo[(N_CHUNKS - 2 + n) % SLOTS]
                    pe.wait_ge(xr_added, 4 * T + 2 * T * (NB - 1) + (2 * (t - 4) + n + 1 if t >= 4 else 2 * t + n + 1 - T))
                    for r in range(2):
                        last = mm3(ps[:, 2 * (t % 4) + n, :], hid_hi[par][:, r, tile_of(t)], hid_lo[par][:, r, tile_of(t)],
                                   wh[:, half_of(r)], wl[:, half_of(r)], r == 0, r == 1)
                    last.then_inc(w_used if t == T - 1 else bank_out, 1)


def mix_banks(g):
    return (2, 4, 6, 4)[g]


def norm_banks(t):
    return 2 * t if t < 4 else 4 + 2 * (t % 2)


def cross_banks(t):
    return 2 if t % 2 else 6


def beside_bank(g):
    return 7 if g % 4 else 3


def groups_of(i):
    return [(a, j0, min(4, i + 1 - j0)) for a in range(2) for j0 in range(0, i + 1, 4)]


def groups_before(u):
    return sum(len(groups_of(v % T)) for v in range(u))


_INS = ["x", "mem", "norm_mix_g", "w_in", "b_forget", "b_gate", "pool_w", "pool_scale", "w_pool_out", "w_fox_out",
        "w_out", "norm_x_g", "norm_mem_g", "w_xq", "w_xkv", "w_xo", "norm_ffn_g", "w_ffn_in", "w_ffn_out", "norm_final_g"]


def kernel(**inputs):
    import numpy as np
    import concourse.bacc as bacc
    from concourse.bass_utils import run_bass_kernel_spmd

    nc = bacc.Bacc("TRN2", target_bir_lowering=False, num_devices=1)
    arrays, args = {}, []
    for name in _INS:
        a = np.ascontiguousarray(inputs[name])
        arrays[f"in_{name}"] = a
        args.append(nc.dram_tensor(f"in_{name}", a.shape, mybir.dt.from_np(a.dtype), kind="ExternalInput").ap())
    args.append(nc.dram_tensor("out_x", (1, S, D), FP32, kind="ExternalOutput").ap())
    build(nc, *args)
    return run_bass_kernel_spmd(nc, [arrays], core_ids=[0]).results[0]["out_x"]
```
